# Optimizing a Trainium2 kernel written in Bass

```python
import math
import jax
import jax.numpy as jnp
from jax import lax
import numpy as np

D_MODEL = 1024
BATCH = 1
SEQ = 1024
DEPTH = 2
DEC_BATCH = 1
DEC_SEQ = 64
PAST_LEN = 256

CHUNK = 64
HEAD_DIM = 64
D_MIX = D_MODEL
RMS_EPS = 1e-6
NEG_INF = -1e30
N_EVEN = (DEPTH + 1) // 2
N_ODD = DEPTH // 2

H_A = (D_MIX // 2) // HEAD_DIM
KVH_A = 2
G_A = H_A // KVH_A
WINDOW = 128
A_LEFT = WINDOW // CHUNK
A_KEEP = min(WINDOW, PAST_LEN)
T5_BUCKETS = 32
T5_MAX_DIST = 128

C_B = D_MIX // 2
H_B = C_B // HEAD_DIM
DECAY_LORA = 64
ICLR_LORA = 64
VRES_LORA = 32
GATE_LORA = 128
LNX_EPS = 64e-5
B_SPLITS = (C_B, DECAY_LORA, C_B, C_B, ICLR_LORA, GATE_LORA)
B_PROJ = sum(B_SPLITS)

H_C = (D_MIX // 2) // HEAD_DIM
C_LEFT = 8
C_KEEP = min(C_LEFT * CHUNK, PAST_LEN)
REL_CLIP = 128

C_D = D_MIX // 2
CONV_W = 31
LN_EPS = 1e-5

D_FF = -(-8 * D_MODEL // (3 * 256)) * 256

E_SPLITS = (H_A * HEAD_DIM, KVH_A * HEAD_DIM, KVH_A * HEAD_DIM, B_PROJ)
O_SPLITS = (H_C * HEAD_DIM, H_C * HEAD_DIM, H_C * HEAD_DIM, 2 * C_D)
E_IN = sum(E_SPLITS)
O_IN = sum(O_SPLITS)

kernel_name = 'hybrid_streaming_encoder_step'

def split_cols(p, sizes):
    return jnp.split(p, np.cumsum(sizes)[:-1].tolist(), axis=-1)

def rmsnorm(x, g):
    xf = x.astype(jnp.float32)
    y = xf * lax.rsqrt(jnp.mean(xf * xf, axis=-1, keepdims=True) + RMS_EPS)
    return (y * g.astype(jnp.float32)).astype(x.dtype)

def t5_bucket(rel):
    nb = T5_BUCKETS // 2
    exact = nb // 2
    n = np.abs(rel)
    nf = np.maximum(n, exact).astype(np.float32)
    large = exact + (np.log(nf / exact) / math.log(T5_MAX_DIST / exact) * (nb - exact)).astype(np.int32)
    return np.where(rel > 0, nb, 0) + np.where(n < exact, n, np.minimum(large, nb - 1))

def t5_bias(table, rel):
    b = table[jnp.asarray(t5_bucket(rel))]
    return jnp.moveaxis(b, -1, 0).reshape((KVH_A, G_A) + rel.shape).astype(jnp.float32)

def clipped_rel_bias(table, dist):
    idx = np.clip(dist, -REL_CLIP, REL_CLIP) + REL_CLIP
    return table[:, jnp.asarray(idx)][:, None].astype(jnp.float32)

def chunk_band(t, n_left):
    b, s = t.shape[:2]
    nc = s // CHUNK
    tp = jnp.pad(t, ((0, 0), (n_left * CHUNK, 0)) + ((0, 0),) * (t.ndim - 2))
    tc = tp.reshape((b, nc + n_left, CHUNK) + t.shape[2:])
    return jnp.concatenate([tc[:, o:o + nc] for o in range(n_left + 1)], axis=2)

def prompt_band_geometry(n_left, seq):
    nk = (n_left + 1) * CHUNK
    rel = np.arange(nk)[None, :] - n_left * CHUNK - np.arange(CHUNK)[:, None]
    kpos = (np.arange(seq // CHUNK)[:, None] - n_left) * CHUNK + np.arange(nk)[None, :]
    return rel, jnp.asarray(kpos >= 0)[:, None, None, None, :]

def sample_rel(keep, t):
    qpos = PAST_LEN + np.arange(t)
    kpos = np.concatenate([PAST_LEN - keep + np.arange(keep), PAST_LEN + np.arange(t)])
    return kpos[None, :] - qpos[:, None]

def attend(q, k, v, bias, mask, sink):
    s = jnp.einsum('...qhgd,...khd->...hgqk', q, k).astype(jnp.float32) * (HEAD_DIM ** -0.5) + bias
    if mask is not None:
        s = jnp.where(mask, s, NEG_INF)
    if sink is None:
        p = jax.nn.softmax(s, axis=-1)
    else:
        sk = sink.astype(jnp.float32)[..., None, None]
        m = jnp.maximum(jnp.max(s, axis=-1, keepdims=True), sk)
        e = jnp.exp(s - m)
        p = e / (jnp.sum(e, axis=-1, keepdims=True) + jnp.exp(sk - m))
    return jnp.einsum('...hgqk,...khd->...qhgd', p.astype(v.dtype), v)

def mixer_a(q, k, v, sink, t5_table, cache):
    b, t = q.shape[:2]
    q = q.reshape(b, t, KVH_A, G_A, HEAD_DIM)
    sk = sink.reshape(KVH_A, G_A)
    if cache is None:
        rel, valid = prompt_band_geometry(A_LEFT, t)
        qc = q.reshape(b, t // CHUNK, CHUNK, KVH_A, G_A, HEAD_DIM)
        o = attend(qc, chunk_band(k, A_LEFT), chunk_band(v, A_LEFT), t5_bias(t5_table, rel), valid, sk)
        new = (k[:, -WINDOW:], v[:, -WINDOW:])
    else:
        ck, cv = cache
        rel = sample_rel(ck.shape[1], t)
        kk = jnp.concatenate([ck.astype(k.dtype), k], axis=1)
        vv = jnp.concatenate([cv.astype(v.dtype), v], axis=1)
        o = attend(q, kk, vv, t5_bias(t5_table, rel), None, sk)
        new = (k, v)
    return o.reshape(b, t, H_A * HEAD_DIM), new

def mixer_c(q, k, v, rel_table, cache):
    b, t = q.shape[:2]
    q = q[:, :, :, None, :]
    if cache is None:
        rel, valid = prompt_band_geometry(C_LEFT, t)
        qc = q.reshape(b, t // CHUNK, CHUNK, H_C, 1, HEAD_DIM)
        o = attend(qc, chunk_band(k, C_LEFT), chunk_band(v, C_LEFT), clipped_rel_bias(rel_table, -rel), valid, None)
        new = (k[:, -C_LEFT * CHUNK:], v[:, -C_LEFT * CHUNK:])
    else:
        ck, cv = cache
        rel = sample_rel(ck.shape[1], t)
        kk = jnp.concatenate([ck.astype(k.dtype), k], axis=1)
        vv = jnp.concatenate([cv.astype(v.dtype), v], axis=1)
        o = attend(q, kk, vv, clipped_rel_bias(rel_table, -rel), None, None)
        new = (k, v)
    return o.reshape(b, t, H_C * HEAD_DIM), new

def rwkv7_scan(r, decay, k, v, a, bb, s0):
    def step(s, inp):
        r_t, w_t, k_t, v_t, a_t, b_t = inp
        sa = jnp.einsum('bhij,bhj->bhi', s, a_t)
        s = s * w_t[:, :, None, :] + sa[..., None] * b_t[:, :, None, :] + v_t[..., None] * k_t[:, :, None, :]
        return s, jnp.einsum('bhij,bhj->bhi', s, r_t)
    xs = tuple(jnp.moveaxis(z, 1, 0) for z in (r, decay, k, v, a, bb))
    s, ys = lax.scan(step, s0, xs)
    return jnp.moveaxis(ys, 0, 1), s

def mixer_b(pb, shift_prev, wkv0, v_first, mu, w0, w2, a0, a2, g2, kk_scale, k_a, r_k, lnx_w, lnx_b, vres):
    b, t, _ = pb.shape
    f32 = jnp.float32
    prev = jnp.concatenate([shift_prev[:, None].astype(pb.dtype), pb[:, :-1]], axis=1)
    xsh = pb + (prev - pb) * mu
    r, wd, k, v, ad, gd = split_cols(xsh, B_SPLITS)
    w = -jax.nn.softplus(-(w0 + jnp.tanh(wd) @ w2)) - 0.5
    a = jax.nn.sigmoid(a0 + ad @ a2)
    g = jax.nn.sigmoid(gd) @ g2
    if vres is None:
        v_first = v
    else:
        v0, v1, v2 = vres
        v = v + (v_first - v) * jax.nn.sigmoid(v0 + (v @ v1) @ v2)
    heads = lambda z: z.reshape(b, t, H_B, HEAD_DIM).astype(f32)
    kk = heads(k * kk_scale)
    kk = kk / jnp.maximum(jnp.sqrt(jnp.sum(kk * kk, axis=-1, keepdims=True)), 1e-12)
    kh = heads(k * (1 + (a - 1) * k_a))
    rh, vh, ah = heads(r), heads(v), heads(a)
    decay = jnp.exp(-jnp.exp(heads(w)))
    y, wkv = rwkv7_scan(rh, decay, kh, vh, -kk, kk * ah, wkv0.astype(f32))
    mean = jnp.mean(y, axis=-1, keepdims=True)
    var = jnp.mean(jnp.square(y - mean), axis=-1, keepdims=True)
    y = (y - mean) * lax.rsqrt(var + LNX_EPS) * lnx_w.reshape(H_B, HEAD_DIM).astype(f32) + lnx_b.reshape(H_B, HEAD_DIM).astype(f32)
    y = y + jnp.sum(rh * kh * r_k.astype(f32), axis=-1, keepdims=True) * vh
    out = y.reshape(b, t, C_B).astype(pb.dtype) * g
    return out, v_first, pb[:, -1], wkv

def mixer_d(pd, conv_prev, dw_w, dw_b, ln_g, ln_b):
    u = pd[..., :C_D] * jax.nn.sigmoid(pd[..., C_D:])
    b = u.shape[0]
    buf = jnp.zeros((b, CONV_W - 1, C_D), u.dtype) if conv_prev is None else conv_prev.astype(u.dtype)
    up = jnp.concatenate([buf, u], axis=1)
    z = lax.conv_general_dilated(up, dw_w[:, None, :].astype(u.dtype), window_strides=(1,), padding='VALID',
                                 dimension_numbers=('NWC', 'WIO', 'NWC'), feature_group_count=C_D) + dw_b
    zf = z.astype(jnp.float32)
    mean = jnp.mean(zf, axis=-1, keepdims=True)
    var = jnp.mean(jnp.square(zf - mean), axis=-1, keepdims=True)
    zn = (zf - mean) * lax.rsqrt(var + LN_EPS) * ln_g.astype(jnp.float32) + ln_b.astype(jnp.float32)
    return jax.nn.silu(zn).astype(u.dtype), up[:, -(CONV_W - 1):]

def swiglu(h, wg, wu, wd):
    return (jax.nn.silu(h @ wg) * (h @ wu)) @ wd

def setup_inputs(seed: int = 0) -> dict:
    key = jax.random.key(seed)
    keys = iter(jax.random.split(key, 48))

    def nrm(shape, scale=1.0, mean=0.0):
        return mean + scale * jax.random.normal(next(keys), shape, jnp.float32)

    def uni(shape, lo, hi):
        return jax.random.uniform(next(keys), shape, jnp.float32, lo, hi)

    NE, NO = N_EVEN, N_ODD
    return {
        'x_prompt': nrm((BATCH, SEQ, D_MODEL)),
        'x_sample': nrm((DEC_BATCH, DEC_SEQ, D_MODEL)),
        'cache_a_k': nrm((NE, DEC_BATCH, A_KEEP, KVH_A, HEAD_DIM)),
        'cache_a_v': nrm((NE, DEC_BATCH, A_KEEP, KVH_A, HEAD_DIM)),
        'state_b_wkv': nrm((NE, DEC_BATCH, H_B, HEAD_DIM, HEAD_DIM), 0.5),
        'state_b_shift': nrm((NE, DEC_BATCH, B_PROJ)),
        'cache_c_k': nrm((NO, DEC_BATCH, C_KEEP, H_C, HEAD_DIM)),
        'cache_c_v': nrm((NO, DEC_BATCH, C_KEEP, H_C, HEAD_DIM)),
        'state_d_conv': nrm((NO, DEC_BATCH, CONV_W - 1, C_D), 0.5),
        'norm_mix_g': nrm((DEPTH, D_MODEL), 0.05, 1.0),
        'norm_ffn_g': nrm((DEPTH, D_MODEL), 0.05, 1.0),
        'norm_final_g': nrm((D_MODEL,), 0.05, 1.0),
        't5_table': nrm((T5_BUCKETS, H_A), 0.5),
        'w_in_e': nrm((NE, D_MODEL, E_IN), D_MODEL ** -0.5),
        'w_out_e': nrm((NE, D_MIX, D_MODEL), D_MIX ** -0.5),
        'a_sink': nrm((NE, H_A), 0.5),
        'b_mu': uni((NE, B_PROJ), 0.0, 1.0),
        'b_w0': uni((NE, C_B), -6.0, -1.0),
        'b_w2': nrm((NE, DECAY_LORA, C_B), 0.1 * DECAY_LORA ** -0.5),
        'b_a0': nrm((NE, C_B), 0.1),
        'b_a2': nrm((NE, ICLR_LORA, C_B), ICLR_LORA ** -0.5),
        'b_g2': nrm((NE, GATE_LORA, C_B), GATE_LORA ** -0.5),
        'b_kk': nrm((NE, C_B), 0.05, 0.85),
        'b_ka': nrm((NE, C_B), 0.05, 1.0),
        'b_rk': nrm((NE, H_B, HEAD_DIM), 0.1),
        'b_lnx_w': nrm((NE, C_B), 0.05, 1.0),
        'b_lnx_b': nrm((NE, C_B), 0.02),
        'b_v0': nrm((NE - 1, C_B), 0.1),
        'b_v1': nrm((NE - 1, C_B, VRES_LORA), C_B ** -0.5),
        'b_v2': nrm((NE - 1, VRES_LORA, C_B), VRES_LORA ** -0.5),
        'w_in_o': nrm((NO, D_MODEL, O_IN), D_MODEL ** -0.5),
        'w_out_o': nrm((NO, D_MIX, D_MODEL), D_MIX ** -0.5),
        'c_rel_table': nrm((NO, H_C, 2 * REL_CLIP + 1), 0.5),
        'd_dw_w': nrm((NO, CONV_W, C_D), CONV_W ** -0.5),
        'd_dw_b': nrm((NO, C_D), 0.02),
        'd_ln_g': nrm((NO, C_D), 0.05, 1.0),
        'd_ln_b': nrm((NO, C_D), 0.02),
        'ffn_w_gate': nrm((DEPTH, D_MODEL, D_FF), D_MODEL ** -0.5),
        'ffn_w_up': nrm((DEPTH, D_MODEL, D_FF), D_MODEL ** -0.5),
        'ffn_w_down': nrm((DEPTH, D_FF, D_MODEL), D_FF ** -0.5),
    }

def reference(x_prompt, x_sample, cache_a_k, cache_a_v, state_b_wkv, state_b_shift,
              cache_c_k, cache_c_v, state_d_conv,
              norm_mix_g, norm_ffn_g, norm_final_g, t5_table,
              w_in_e, w_out_e, a_sink,
              b_mu, b_w0, b_w2, b_a0, b_a2, b_g2, b_kk, b_ka, b_rk, b_lnx_w, b_lnx_b,
              b_v0, b_v1, b_v2,
              w_in_o, w_out_o, c_rel_table, d_dw_w, d_dw_b, d_ln_g, d_ln_b,
              ffn_w_gate, ffn_w_up, ffn_w_down):
    xs = [x_prompt, x_sample]
    v_first = [None, None]
    st = [[[] for _ in range(7)] for _ in range(2)]
    for i in range(DEPTH):
        j = i // 2
        for gi in range(2):
            x = xs[gi]
            b, t = x.shape[:2]
            h = rmsnorm(x, norm_mix_g[i])
            if i % 2 == 0:
                q, k, v, pb = split_cols(h @ w_in_e[j], E_SPLITS)
                cache = None if gi == 0 else (cache_a_k[j], cache_a_v[j])
                oa, (nk, nv) = mixer_a(q.reshape(b, t, H_A, HEAD_DIM), k.reshape(b, t, KVH_A, HEAD_DIM),
                                       v.reshape(b, t, KVH_A, HEAD_DIM), a_sink[j], t5_table, cache)
                if gi == 0:
                    shift0 = jnp.zeros((b, B_PROJ), x.dtype)
                    wkv0 = jnp.zeros((b, H_B, HEAD_DIM, HEAD_DIM), jnp.float32)
                else:
                    shift0, wkv0 = state_b_shift[j], state_b_wkv[j]
                vres = None if j == 0 else (b_v0[j - 1], b_v1[j - 1], b_v2[j - 1])
                ob, v_first[gi], nshift, nwkv = mixer_b(pb, shift0, wkv0, v_first[gi], b_mu[j], b_w0[j], b_w2[j],
                                                        b_a0[j], b_a2[j], b_g2[j], b_kk[j], b_ka[j], b_rk[j],
                                                        b_lnx_w[j], b_lnx_b[j], vres)
                x = x + jnp.concatenate([oa, ob], axis=-1) @ w_out_e[j]
                for s_list, val in zip(st[gi][0:4], (nk, nv, nwkv, nshift)):
                    s_list.append(val)
            else:
                q, k, v, pd = split_cols(h @ w_in_o[j], O_SPLITS)
                cache = None if gi == 0 else (cache_c_k[j], cache_c_v[j])
                oc, (nk, nv) = mixer_c(q.reshape(b, t, H_C, HEAD_DIM), k.reshape(b, t, H_C, HEAD_DIM),
                                       v.reshape(b, t, H_C, HEAD_DIM), c_rel_table[j], cache)
                conv_prev = None if gi == 0 else state_d_conv[j]
                od, nconv = mixer_d(pd, conv_prev, d_dw_w[j], d_dw_b[j], d_ln_g[j], d_ln_b[j])
                x = x + jnp.concatenate([oc, od], axis=-1) @ w_out_o[j]
                for s_list, val in zip(st[gi][4:7], (nk, nv, nconv)):
                    s_list.append(val)
            h = rmsnorm(x, norm_ffn_g[i])
            xs[gi] = x + swiglu(h, ffn_w_gate[i], ffn_w_up[i], ffn_w_down[i])
    y_prompt = rmsnorm(xs[0], norm_final_g)
    y_sample = rmsnorm(xs[1], norm_final_g)
    (pak, pav, pbw, pbs, pck, pcv, pdc), (sak, sav, sbw, sbs, sck, scv, sdc) = [[jnp.stack(s) for s in g] for g in st]
    return (y_prompt, y_sample, pak, pav, pbw, pbs, pck, pcv, pdc, sak, sav, sbw, sbs, sck, scv, sdc)


_drawn_inputs = setup_inputs


def setup_inputs(seed=0):
    import zlib

    import numpy as np

    out = dict(_drawn_inputs(seed))
    spreads = {}
    factors = {'a_sink': 58.725,
     'b_w2': 8.0,
     'b_lnx_b': 6.496,
     'd_dw_b': 3.829,
     'd_ln_g': 2.726,
     'd_ln_b': 7.669,
     'c_rel_table': 3.034}
    for name, (base, spread) in spreads.items():
        noise = np.random.default_rng([zlib.crc32(name.encode()), seed]).standard_normal(out[name].shape)
        drawn = base * np.exp(spread * noise) if base else spread * noise
        out[name] = jnp.asarray(drawn.astype(out[name].dtype))
    for name, factor in factors.items():
        out[name] = (out[name] * factor).astype(out[name].dtype)
    return out
```

```python
from contextlib import ExitStack


import numpy as np

import concourse.bass as bass
from concourse import mybir

F32 = mybir.dt.float32
F32R = mybir.dt.float32r
ACT = mybir.ActivationFunctionType
ALU = mybir.AluOpType
AX = mybir.AxisListType.X
ds = bass.ds

P = 128
D = 1024
KT = D // P
SEQ = 1024
DEC = 64
NT = SEQ + DEC
CHUNK = 64
HD = 64
PAIRS = 4
GROUPS = [(0, 384), (384, 384), (768, 320)]
NG = len(GROUPS)
DFF = 2816
FT = DFF // P
HID = 6
FFN_GROUPS = [(k, min(HID, FT - k)) for k in range(0, FT, HID)]
NPB = 14
PBW = 1 + SEQ + 1 + DEC
W1 = PBW - 1
G3 = W1 // 3
WP = W1 - DEC + P
BLOCKS = 9
WAVE = 3
LEVELS = 6
C_CACHE = 256
NEG = -1e30
RMS_EPS = 1e-6
LNX_EPS = 64e-5
LN_EPS = 1e-5
DECAY = float(np.exp(-0.5))
TAPS = 31
N_CONST = 16 * 16
UW = 2 * (TAPS - 1) + NT
ZW = UW - (TAPS - 1)
VEC_A, VEC_C = 384, 768


def repeat(eng, start, end, body):
    if end - start <= 1:
        for i in range(start, end):
            body(i)
    else:
        with eng.Fori(start, end) as i:
            body(i)


class Chain:

    def __init__(self, eng, sem):
        self.eng, self.sem, self.n, self.extra = eng, sem, 0, 0

    def step(self, ins):
        ins.then_inc(self.sem, 1)
        self.n += 1
        return self.n

    def wait(self, n):
        self.eng.wait_ge(self.sem, self.extra + n)

    def __call__(self, ins):
        self.wait(self.step(ins))

    def loop(self, start, end, per, body):
        if end - start <= 1:
            for i in range(start, end):
                body(i)
            return
        first = self.n
        with self.eng.Fori(start, end) as i:
            self.extra = (i - start) * per
            body(i)
        assert self.n - first == per, (self.n - first, per)
        self.extra = 0
        self.n = first + per * (end - start)


def trunk(nc, d):
    ctx = ExitStack()
    with ctx:
        def at(name, shape, offset, dt=F32):
            return nc.alloc_sbuf_tensor_at(name, shape, dt, offset=offset, align_bytes=4)

        def sem(name):
            return ctx.enter_context(nc.semaphore(name))

        tok = 4 * NT
        H0 = 16512
        TMP0 = H0 + 2 * KT * tok
        tmp_bytes = 2 * tok + 4 * 384 * (3 + 2 + 2)
        BIG0 = TMP0 + tmp_bytes
        big_bytes = 12 * tok + 4 * 4 * UW + 4 * tok
        WR0 = BIG0 + big_bytes
        CO0 = WR0 + 6 * 4 * D
        h_hi = at("h_hi", [P, KT, NT], H0, F32R)
        h_lo = at("h_lo", [P, KT, NT], H0 + KT * tok, F32R)
        sumsq = at("sumsq", [P, NT], TMP0)
        rstd = at("rstd", [P, NT], TMP0 + tok)
        o = TMP0 + 2 * tok
        gate_t = at("gate_t", [P, NG, 384], o)
        up_t = at("up_t", [P, 2, 384], o + 4608)
        hid_t = at("hid_t", [P, 2, 384], o + 7680)
        sq_t = gate_t
        x = at("x", [P, KT, NT], BIG0)
        hid0 = BIG0 + 8 * 4 * PBW
        hid_hi = at("hid_hi", [P, HID, NT], hid0, F32R)
        hid_lo = at("hid_lo", [P, HID, NT], hid0 + HID * tok, F32R)
        pb = at("pb", [P, NPB, PBW], BIG0)
        akvq = at("akvq", [P, 6, NT], BIG0 + NPB * 4 * PBW)
        cproj = at("cproj", [P, 12, NT], BIG0)
        u_buf = at("u_buf", [P, 4, UW], BIG0 + 12 * tok)
        z_buf = at("z_buf", [P, 4, NT], BIG0 + 12 * tok + 16 * UW)
        w_raw = [at(f"w_raw{s}", [P, KT, P], WR0 + s * 4 * D) for s in range(2)]
        w_hi = [at(f"w_hi{s}", [P, KT, P], WR0 + (2 + s) * 4 * D, F32R) for s in range(2)]
        w_lo = [at(f"w_lo{s}", [P, KT, P], WR0 + (4 + s) * 4 * D, F32R) for s in range(2)]
        cursor = [CO0]

        def whole(t):
            return t[tuple(slice(None) for _ in t.shape)]

        def const(name, shape):
            t = at(name, shape, cursor[0])
            cursor[0] += 4 * int(np.prod(shape[1:]))
            return t

        ident = const("ident", [P, P])
        flip = const("flip", [P, P])
        ones = const("ones", [P, P])
        head_ones = const("head_ones", [P, P])
        sa_mask = const("sa_mask", [P, 4, P])
        level_mask = const("level_mask", [P, LEVELS - 1, P])
        gains = const("gains", [P, 5, KT])
        mu = const("mu", [P, NPB])
        shift_in = const("shift_in", [P, NPB])
        shift_out = const("shift_out", [P, 2, NPB])
        rw_par = const("rw_par", [P, PAIRS, 9])
        rc = const("rc", [P, 9])
        conv_par = const("conv_par", [P, 4, TAPS + 3])
        cc = const("cc", [P, TAPS + 3])
        sink = const("sink", [P, 8])
        neg_sink = const("neg_sink", [P, 8])
        assert cursor[0] <= nc.sbuf_usable_end, (cursor[0], nc.sbuf_usable_end)

        cursor[0] = H0
        at_rt = const("at_rt", [P, 2, WP])
        kt_ = const("kt_", [P, WP])
        bt_ = const("bt_", [P, WP])
        bonus = const("bonus", [P, WP])
        v_cur = const("v_cur", [P, WP])
        pair0 = cursor[0]
        pinv = const("pinv", [P, WP])
        kk_ = const("kk_", [P, WP])
        xx = at("xx", [P, 2, 2, WAVE, P], pair0)
        y_sb = at("y_sb", [P, 2, WAVE, P], pair0 + 6144)
        sa = const("sa", [P, 2, WAVE, 4, P])
        bt_level = const("bt_level", [P, 2, WAVE, P])
        tm = const("tm", [P, WAVE, 4, P])
        akv = const("akv", [P, 2, WAVE, HD])
        wz = const("wz", [P, 2, WAVE, 2, HD])
        r_eff = const("r_eff", [P, WAVE, P])
        m_bd = const("m_bd", [P, 2 * WAVE, P])
        h_bd = const("h_bd", [P, 2 * WAVE, P])
        s_bd = const("s_bd", [P, 2 * WAVE + 1, P])
        bk_hat = const("bk_hat", [P, 2, WAVE * P])
        decay_end = const("decay_end", [P, 2 * BLOCKS])
        wa2 = const("wa2", [P, PAIRS * P])
        g2 = const("g2", [P, PAIRS * P])
        wa2_cur = const("wa2_cur", [P, P])
        g2_cur = const("g2_cur", [P, P])
        x0_mask = const("x0_mask", [P, 2, P])
        state_in = const("state_in", [P, PAIRS, HD])
        state_out = const("state_out", [P, 2, PAIRS, HD])
        assert cursor[0] <= BIG0 , (cursor[0], BIG0)

        def attention_memory(tag, nb, cache_blocks, v_width, heads_k, slots):
            cursor[0] = H0
            m = {}
            for name, shape in [("bias", [P, 8, nb * P]), ("hankel", [P, 8, nb * P]), ("qz", [P, 2, BLOCKS * P]),
                                ("vf", [P, BLOCKS * P]), ("vt", [P, BLOCKS, P]), ("vcc", [P, cache_blocks, P]),
                                ("k_cache", [P, heads_k, cache_blocks * P]), ("v_cache", [P, cache_blocks, v_width]),
                                ("s", [P, slots, nb * P]), ("pt", [P, 2, nb, P]), ("stat", [P, slots, 4]),
                                ("zc", [P, ZW])]:
                m[name] = const(f"{tag}_{name}", shape)
            assert cursor[0] <= BIG0, (cursor[0], BIG0)
            return m

        mem_a = attention_memory("a", 2, 1, P, 1, 6)
        mem_c = attention_memory("c", 5, 2, 4 * P, 4, 3)
        ln_t = at("ln_t", [P, 4, NT], H0)
        ln_r = at("ln_r", [P, NT], H0 + 4 * tok)
        cursor[0] = hid0
        pick_a = const("pick_a", [P, VEC_A])
        pick_c = const("pick_c", [P, 3, VEC_C])
        table_a = const("table_a", [P, 8])
        table_c = const("table_c", [P, 3, 8])
        vec_sb = const("vec_sb", [P, 2, VEC_C])

        PS = ctx.enter_context(nc.psum_tensor("PS", [P, 8, 512], F32))
        x_home = nc.dram_tensor("x_home", (P, KT, NT), F32, kind="Internal").ap()
        vec_home = nc.dram_tensor("vec_home", (2, 8, VEC_C), F32, kind="Internal")

        names = """consts_loaded w_loaded0 w_loaded1 w_hi_ready w_lo_ready product_done evac_done
            h_hi_ready h_lo_ready sq_done sum_done stat_done stat_read ms_ready rstd_ready gate_ready
            u_ready hid_ready hid_hi_ready hid_lo_ready dve_chain act_chain pool_chain barrier stored x_saved y_ready
            vec_done vec_copied vec_stored
            rw_loaded diff_ready shifted squashed r_staged low_done sg_ready cum_ready exp_ready ksq_ready
            ss_done root_ready rk_ready bonus_done prep_ready hat_ready tm_done tm_ready ab_done sa_ready
            x_init bt_ready y_done ysb_ready xprod_done xadd akv_done akv_ready wz_done wz_ready reff_done
            r_ready mh_done mdiag_ready hbd_ready mbd_ready s_init s_done s_new yb_done y_stored mean_done
            yc_ready var_done vr_ready vroot_ready zg_done gated state_ready
            hk_loaded hk_done bias_ready q_staged v_staged vtr_done vt_ready sc_done st_done max_ready exp_done
            p_ready pt_done pt_ev pv_done o_ev sk_ready conv_done z_ready
            conv_staged cstate_loaded lnm_done lnc_ready lnv_done lnr_ready lnq_ready lnz_ready silu_ready""".split()
        sm = {n: sem(n) for n in names}
        w_loaded = [sm["w_loaded0"], sm["w_loaded1"]]
        x_loaded = [sem(f"x_loaded{g}") for g in range(NG)]
        stages = [("w_e", 20, KT, 0), ("w_oe", 8, KT, 0)]
        for k0, kn in FFN_GROUPS:
            stages += [("w_gu0", 2 * kn, KT, 2 * k0), ("w_d0", 8, kn, k0)]
        stages += [("w_o", 20, KT, 0), ("w_oo", 8, KT, 0)]
        for k0, kn in FFN_GROUPS:
            stages += [("w_gu1", 2 * kn, KT, 2 * k0), ("w_d1", 8, kn, k0)]
        bases = list(np.cumsum([0] + [s[1] for s in stages]))
        tiles_k = [s[2] for s in stages for _ in range(s[1])]
        n_tiles = int(bases[-1])
        bases = [int(b) for b in bases]
        S_IN = [0, 2 + 2 * len(FFN_GROUPS)]

        def stage_groups(layer):
            first = S_IN[layer] + 2
            return [(first + 2 * i, first + 2 * i + 1, k0, kn) for i, (k0, kn) in enumerate(FFN_GROUPS)]

        bars = {"pe": 0, "act": 0, "dve": 0, "pool": 0}

        def sync_all(who, eng):
            bars[who] += 1
            eng.drain().then_inc(sm["barrier"], 1)
            eng.wait_ge(sm["barrier"], 4 * bars[who])

        def pe_tile(pe, n, slot, kn, hi, lo, before=None):
            pe.wait_ge(sm["w_hi_ready"], n + 1)
            pe.wait_ge(sm["w_lo_ready"], n + 1)
            for g, (c0, cn) in enumerate(GROUPS):
                if not (isinstance(n, int) and n < 2):
                    pe.wait_ge(sm["evac_done"], n * NG + (g + 1 - 2 * NG))
                if before:
                    before(g)
                out = PS[:, NG * slot + g, 0:cn]
                for k in range(kn):
                    w_h, w_l = w_hi[slot][:, k, :], w_lo[slot][:, k, :]
                    a_h, a_l = hi[:, k, c0:c0 + cn], lo[:, k, c0:c0 + cn]
                    pe.matmul(out, w_h, a_h, start=k == 0, stop=False)
                    pe.matmul(out, w_h, a_l, start=False, stop=False)
                    last = pe.matmul(out, w_l, a_h, start=False, stop=k == kn - 1)
                last.then_inc(sm["product_done"], 1)

        def pe_stage(pe, s, hi, lo, before=None, norm=None):
            _, count, kn, _ = stages[s]
            base = bases[s]
            pe_tile(pe, base, 0, kn, hi, lo, before)
            if norm is not None:
                pe_stats(pe, norm)
            pe_tile(pe, base + 1, 1, kn, hi, lo)

            def pair(j):
                for slot in range(2):
                    pe_tile(pe, 2 * j + (base + slot), slot, kn, hi, lo)
            repeat(pe, 1, count // 2, pair)

        def pe_stats(pe, norm):
            for g, (c0, cn) in enumerate(GROUPS):
                n = norm * NG + g
                pe.wait_ge(sm["sum_done"], 3 * (norm + 1) + (norm + 1) * KT * NG)
                if n >= 2:
                    pe.wait_ge(sm["stat_read"], n - 1)
                pe.matmul(PS[:, 6 + n % 2, 0:cn], ones[:, :], sumsq[:, c0:c0 + cn],
                          start=True, stop=True).then_inc(sm["stat_done"], 1)

        def h_tiles_first(pe, h):
            return lambda g: pe.wait_ge(sm["h_lo_ready"], h * KT * NG + (KT - 1) * NG + g + 1)

        def h_groups_first(pe, h):
            return lambda g: pe.wait_ge(sm["h_lo_ready"], h * KT * NG + KT * (g + 1))

        def hidden_ready(pe, layer, k0, kn):
            return lambda g: pe.wait_ge(sm["hid_lo_ready"], NG * (layer * FT + k0 + kn - 1) + g + 1)

        def sp_tile(sp, s, slot, i):
            name, _, kn, first = stages[s]
            n = i + bases[s]
            if not (isinstance(n, int) and n < 2):
                sp.wait_ge(sm["w_lo_ready"], n - 1)
            src = d[name][i + first, :, :, :] if not name.startswith("w_d") else d[name][i, :, first:first + kn, :]
            sp.dma_start(w_raw[slot][:, 0:kn, :], src).then_inc(w_loaded[slot], 16)

        def sp_first(sp, s):
            if s < len(stages):
                sp_tile(sp, s, 0, 0)
                sp_tile(sp, s, 1, 1)

        def sp_rest(sp, s):
            def pair(j):
                for slot in range(2):
                    sp_tile(sp, s, slot, 2 * j + slot)
            repeat(sp, 1, stages[s][1] // 2, pair)

        def act_hi(act, j, slot, base, kn):
            act.wait_ge(w_loaded[slot], j * 16 + (base // 2 + 1) * 16)
            if not (isinstance(j, int) and base + 2 * j < 2):
                act.wait_ge(sm["product_done"], j * (2 * NG) + (base + slot - 1) * NG)
            act.activation(w_hi[slot][:, 0:kn, :], w_raw[slot][:, 0:kn, :], ACT.Copy).then_inc(sm["w_hi_ready"], 1)

        def act_stage(act, s, work=None):
            _, count, kn, _ = stages[s]

            def pair(j):
                for slot in range(2):
                    if work:
                        work(j, slot)
                    act_hi(act, j, slot, bases[s] + 2, kn)
            repeat(act, 0, count // 2 - 1, pair)
            for slot in range(2):
                if work:
                    work(count // 2 - 1, slot)
                n = bases[s + 1] + slot
                if n < n_tiles:
                    act_hi(act, 0, slot, bases[s + 1], tiles_k[n])

        def pool_lo(pool, n, slot, kn):
            pool.wait_ge(sm["w_hi_ready"], n + 1)
            pool.tensor_tensor(w_lo[slot][:, 0:kn, :], w_raw[slot][:, 0:kn, :],
                               w_hi[slot][:, 0:kn, :].bitcast(F32), ALU.subtract).then_inc(sm["w_lo_ready"], 1)

        def pool_stage(pool, s, work=None):
            _, count, kn, _ = stages[s]
            base = bases[s]

            def pair(j):
                for slot in range(2):
                    if work:
                        work(j, slot)
                    pool_lo(pool, 2 * j + (base + 2 + slot), slot, kn)
            repeat(pool, 0, count // 2 - 1, pair)
            for slot in range(2):
                if work:
                    work(count // 2 - 1, slot)
                n = bases[s + 1] + slot
                if n < n_tiles:
                    pool_lo(pool, n, slot, tiles_k[n])

        groups0, groups1 = stage_groups(0), stage_groups(1)
        x_from = [None, bases[1], bases[groups0[-1][1]], bases[S_IN[1] + 1], bases[groups1[-1][1]]]

        def wait_x(eng, norm, i, g):
            if norm == 0:
                eng.wait_ge(x_loaded[g], 16)
            else:
                eng.wait_ge(sm["evac_done"], i * NG + (x_from[norm] * NG + g + 1))

        def act_h(act, norm, h, order):
            for i, g in order:
                c0, cn = GROUPS[g]
                wait_x(act, norm, i, g)
                act.activation(h_hi[:, ds(i, 1), c0:c0 + cn], x[:, ds(i, 1), c0:c0 + cn], ACT.Copy,
                               scale=gains[:, norm, ds(i, 1)]).then_inc(sm["h_hi_ready"], 1)

        def dve_h(dve, norm, h, order, first):
            for n, (i, g) in enumerate(order):
                c0, cn = GROUPS[g]
                dve.wait_ge(sm["h_hi_ready"], first + (n + 1))
                dve.scalar_tensor_tensor(h_lo[:, ds(i, 1), c0:c0 + cn], x[:, ds(i, 1), c0:c0 + cn],
                                         gains[:, norm, ds(i, 1)],
                                         h_hi[:, ds(i, 1), c0:c0 + cn].bitcast(F32),
                                         ALU.mult, ALU.subtract).then_inc(sm["h_lo_ready"], 1)

        by_group = [(i, g) for g in range(NG) for i in range(KT)]

        def pool_sq_start(pool, norm):
            if norm:
                pool.wait_ge(sm["stat_done"], norm * NG)
            pool.memset(sumsq[:, :], 0.0).then_inc(sm["sum_done"], 3)

        def pool_sq(pool, norm, i):
            for g, (c0, cn) in enumerate(GROUPS):
                done = 3 * (norm + 1) + norm * KT * NG + g
                wait_x(pool, norm, i, g)
                pool.wait_ge(sm["sum_done"], i * NG + (done - 2))
                pool.tensor_tensor(sq_t[:, g, 0:cn], x[:, ds(i, 1), c0:c0 + cn], x[:, ds(i, 1), c0:c0 + cn],
                                   ALU.mult).then_inc(sm["sq_done"], 1)
                pool.wait_ge(sm["sq_done"], i * NG + (norm * KT * NG + g + 1))
                pool.tensor_tensor(sumsq[:, c0:c0 + cn], sumsq[:, c0:c0 + cn], sq_t[:, g, 0:cn],
                                   ALU.add).then_inc(sm["sum_done"], 1)

        def dve_rstd(dve, norm):
            for g, (c0, cn) in enumerate(GROUPS):
                n = norm * NG + g
                dve.wait_ge(sm["stat_done"], n + 1)
                dve.tensor_scalar(rstd[:, c0:c0 + cn], PS[:, 6 + n % 2, 0:cn], 1.0 / D, RMS_EPS,
                                  ALU.mult, ALU.add).then_inc(sm["stat_read"], 1)
                dve.wait_ge(sm["stat_read"], n + 1)
                dve.reciprocal(rstd[:, c0:c0 + cn], rstd[:, c0:c0 + cn]).then_inc(sm["ms_ready"], 1)

        def act_rstd(act, norm):
            for g, (c0, cn) in enumerate(GROUPS):
                act.wait_ge(sm["ms_ready"], norm * NG + g + 1)
                act.activation(rstd[:, c0:c0 + cn], rstd[:, c0:c0 + cn], ACT.Sqrt).then_inc(sm["rstd_ready"], 1)

        def dve_scaled(dve, n, slot, g, out, signal=True):
            c0, cn = GROUPS[g]
            dve.wait_ge(sm["product_done"], n * NG + (g + 1))
            ins = dve.tensor_tensor(out, PS[:, NG * slot + g, 0:cn], rstd[:, c0:c0 + cn], ALU.mult)
            if signal:
                ins.then_inc(sm["evac_done"], 1)

        PC = SEQ - GROUPS[-1][0]

        def dve_scaled_split(dve, n, slot, out_prompt, out_sample):
            c0, cn = GROUPS[-1]
            dve.wait_ge(sm["product_done"], n * NG + NG)
            dve.tensor_tensor(out_prompt, PS[:, NG * slot + NG - 1, 0:PC], rstd[:, c0:c0 + PC], ALU.mult)
            dve.tensor_tensor(out_sample, PS[:, NG * slot + NG - 1, PC:cn], rstd[:, c0 + PC:NT], ALU.mult)\
               .then_inc(sm["evac_done"], 1)

        def dve_first_rstd(dve, norm):
            dve.wait_ge(sm["rstd_ready"], (norm + 1) * NG)

        def dve_in_even(dve):
            dve_rstd(dve, 0)
            dve_first_rstd(dve, 0)
            dve.wait_ge(sm["vec_stored"], 16)

            def rwkv_tiles(j):
                for slot in range(2):
                    i = 2 * j + slot
                    for g in range(NG - 1):
                        c0, cn = GROUPS[g]
                        dve_scaled(dve, i + bases[0], slot, g, pb[:, ds(i, 1), 1 + c0:1 + c0 + cn])
                    c0 = GROUPS[-1][0]
                    dve_scaled_split(dve, i + bases[0], slot, pb[:, ds(i, 1), 1 + c0:1 + SEQ],
                                     pb[:, ds(i, 1), 2 + SEQ:PBW])

            def attention_tiles(j):
                for slot in range(2):
                    i = 2 * j + slot
                    for g, (c0, cn) in enumerate(GROUPS):
                        dve_scaled(dve, i + (bases[0] + NPB), slot, g, akvq[:, ds(i, 1), c0:c0 + cn])
            repeat(dve, 0, NPB // 2, rwkv_tiles)
            repeat(dve, 0, 3, attention_tiles)

        def dve_in_odd(dve):
            s = S_IN[1]
            dve_rstd(dve, 2)
            dve_first_rstd(dve, 2)
            dve.wait_ge(sm["x_saved"], 16)

            def attention_tiles(j):
                for slot in range(2):
                    i = 2 * j + slot
                    for g, (c0, cn) in enumerate(GROUPS):
                        dve_scaled(dve, i + bases[s], slot, g, cproj[:, ds(i, 1), c0:c0 + cn])
            repeat(dve, 0, 6, attention_tiles)

            def conv_tiles(j):
                n = 2 * j + (bases[s] + 12)
                if not isinstance(j, int):
                    dve.wait_ge(sm["u_ready"], j * NG)
                for g, (c0, cn) in enumerate(GROUPS):
                    dve_scaled(dve, n, 0, g, gate_t[:, g, 0:cn])
                for g, (c0, cn) in enumerate(GROUPS):
                    if g == 2:
                        dve.wait_ge(sm["u_ready"], j * NG + 1)
                    dve_scaled(dve, n + 1, 1, g, up_t[:, g % 2, 0:cn])
                    dve.wait_ge(sm["evac_done"], n * NG + (NG + g + 1))
                    dve.wait_ge(sm["gate_ready"], j * NG + (FT * NG + g + 1))
                    if g < NG - 1:
                        dve.tensor_tensor(u_buf[:, ds(j, 1), TAPS - 1 + c0:TAPS - 1 + c0 + cn],
                                          up_t[:, g % 2, 0:cn], gate_t[:, g, 0:cn], ALU.mult)\
                           .then_inc(sm["u_ready"], 1)
                    else:
                        dve.tensor_tensor(u_buf[:, ds(j, 1), TAPS - 1 + c0:TAPS - 1 + SEQ],
                                          up_t[:, g % 2, 0:PC], gate_t[:, g, 0:PC], ALU.mult)
                        dve.tensor_tensor(u_buf[:, ds(j, 1), 2 * (TAPS - 1) + SEQ:UW],
                                          up_t[:, g % 2, PC:cn], gate_t[:, g, PC:cn], ALU.mult)\
                           .then_inc(sm["u_ready"], 1)
            conv_tiles(0)
            repeat(dve, 1, 4, conv_tiles)

        def gate_first(layer):
            return layer * (FT * NG + 4 * NG)

        def act_gate(act, func, base):
            def work(j, slot):
                if slot:
                    return
                for g, (c0, cn) in enumerate(GROUPS):
                    act.wait_ge(sm["evac_done"], j * (2 * NG) + (base * NG + g + 1))
                    act.activation(gate_t[:, g, 0:cn], gate_t[:, g, 0:cn], func).then_inc(sm["gate_ready"], 1)
            return work

        def dve_hidden(dve, s, layer, k0, kn):
            def tile(j):
                n = 2 * j + bases[s]
                v0 = NG * (layer * FT + k0)
                if v0 or not isinstance(j, int):
                    dve.wait_ge(sm["hid_ready"], j * NG + v0)
                for g, (c0, cn) in enumerate(GROUPS):
                    dve_scaled(dve, n, 0, g, gate_t[:, g, 0:cn])
                for g, (c0, cn) in enumerate(GROUPS):
                    if g == 2:
                        dve.wait_ge(sm["hid_ready"], j * NG + (v0 + 1))
                    dve_scaled(dve, n + 1, 1, g, up_t[:, g % 2, 0:cn])
                    dve.wait_ge(sm["evac_done"], n * NG + (NG + g + 1))
                    dve.wait_ge(sm["gate_ready"], j * NG + (gate_first(layer) + k0 * NG + g + 1))
                    if not (isinstance(j, int) and v0 + g < 2):
                        dve.wait_ge(sm["hid_lo_ready"], j * NG + (v0 + g - 1))
                    dve.tensor_tensor(hid_t[:, g % 2, 0:cn], up_t[:, g % 2, 0:cn], gate_t[:, g, 0:cn],
                                      ALU.mult).then_inc(sm["hid_ready"], 1)
            tile(0)
            repeat(dve, 1, kn, tile)

        def act_hidden(act, s, layer, k0, kn):
            gate = act_gate(act, ACT.Silu, bases[s])

            def work(j, slot):
                gate(j, slot)
                if not slot:
                    return
                for g, (c0, cn) in enumerate(GROUPS):
                    act.wait_ge(sm["hid_ready"], j * NG + (NG * (layer * FT + k0) + g + 1))
                    act.activation(hid_hi[:, ds(j, 1), c0:c0 + cn], hid_t[:, g % 2, 0:cn], ACT.Copy)\
                       .then_inc(sm["hid_hi_ready"], 1)
            act_stage(act, s, work)

        def pool_hidden(pool, s, layer, k0, kn):
            def work(j, slot):
                if not slot:
                    return
                for g, (c0, cn) in enumerate(GROUPS):
                    pool.wait_ge(sm["hid_hi_ready"], j * NG + (NG * (layer * FT + k0) + g + 1))
                    pool.tensor_tensor(hid_lo[:, ds(j, 1), c0:c0 + cn], hid_t[:, g % 2, 0:cn],
                                       hid_hi[:, ds(j, 1), c0:c0 + cn].bitcast(F32),
                                       ALU.subtract).then_inc(sm["hid_lo_ready"], 1)
            pool_stage(pool, s, work)

        def dve_residual(dve, s, after=None):
            def pair(j):
                for slot in range(2):
                    i = 2 * j + slot
                    for g, (c0, cn) in enumerate(GROUPS):
                        dve.wait_ge(sm["product_done"], i * NG + (bases[s] * NG + g + 1))
                        dve.tensor_tensor(x[:, ds(i, 1), c0:c0 + cn], PS[:, NG * slot + g, 0:cn],
                                          x[:, ds(i, 1), c0:c0 + cn], ALU.add).then_inc(sm["evac_done"], 1)
                    if after:
                        after(i)
            repeat(dve, 0, KT // 2, pair)

        def concat_source(layer, i, g):
            c0, cn = GROUPS[g]
            if i >= 4 and layer == 0:
                t = pb[:, 4 + i, :]
                if g < NG - 1:
                    return [((c0, c0 + cn), t[:, 1 + c0:1 + c0 + cn])]
                return [((c0, SEQ), t[:, 1 + c0:1 + SEQ]), ((SEQ, NT), t[:, 2 + SEQ:PBW])]
            t = z_buf[:, i - 4, :] if i >= 4 else akvq[:, 2 + i, :] if layer == 0 else cproj[:, 8 + i, :]
            return [((c0, c0 + cn), t[:, c0:c0 + cn])]

        def act_concat(act, layer):
            for i, g in by_group:
                for (a, b), src in concat_source(layer, i, g):
                    ins = act.activation(h_hi[:, i, a:b], src, ACT.Copy)
                ins.then_inc(sm["h_hi_ready"], 1)

        def dve_concat(dve, layer, first):
            for n, (i, g) in enumerate(by_group):
                dve.wait_ge(sm["h_hi_ready"], first + n + 1)
                for (a, b), src in concat_source(layer, i, g):
                    ins = dve.tensor_tensor(h_lo[:, i, a:b], src, h_hi[:, i, a:b].bitcast(F32), ALU.subtract)
                ins.then_inc(sm["h_lo_ready"], 1)

        def block_cols(b):
            return b * P if b < BLOCKS - 1 else W1 - DEC

        def thirds(t):
            return t.rearrange("p (g c) -> p g c", g=3)

        def wave_runs(w):
            return [(0, WAVE, WAVE * w * P)] if w < 2 else [(0, WAVE - 1, WAVE * w * P), (WAVE - 1, 1, W1 - DEC)]

        halves = [slice(0, HD), slice(HD, P)]

        def rwkv_shift_pool(pool):
            pool.wait_ge(sm["shifted"], 2)

            def pair(j):
                for slot in range(2):
                    pool.wait_ge(sm["shifted"], 2 * j + (slot + 1))
                    pool.tensor_tensor(at_rt[:, slot, 0:W1], pb[:, ds(2 * j + slot, 1), 0:W1],
                                       pb[:, ds(2 * j + slot, 1), 1:PBW], ALU.subtract).then_inc(sm["diff_ready"], 1)
            repeat(pool, 0, NPB // 2, pair)

        def rwkv_shift_dve(dve, chain):
            chain(dve.memset(pb[:, :, 0:1], 0.0))
            chain(dve.tensor_copy(pb[:, :, 1 + SEQ:2 + SEQ], shift_in[:, :].unsqueeze(2)))
            chain(dve.tensor_copy(shift_out[:, 0, :].unsqueeze(2), pb[:, :, SEQ:SEQ + 1]))
            dve.tensor_copy(shift_out[:, 1, :].unsqueeze(2), pb[:, :, PBW - 1:PBW]).then_inc(sm["shifted"], 2)

            def pair(j):
                for slot in range(2):
                    i = 2 * j + slot
                    dve.wait_ge(sm["diff_ready"], 2 * j + (slot + 1))
                    dve.scalar_tensor_tensor(pb[:, ds(i, 1), 1:PBW], at_rt[:, slot, 0:W1], mu[:, ds(i, 1)],
                                             pb[:, ds(i, 1), 1:PBW], ALU.mult, ALU.add).then_inc(sm["shifted"], 1)
            repeat(dve, 0, NPB // 2, pair)

        def rwkv_act(act):
            act.wait_ge(sm["shifted"], 2 + NPB)
            act.activation(pb[0:HD, 12, 1:PBW], pb[0:HD, 12, 1:PBW], ACT.Tanh).then_inc(sm["squashed"], 1)
            act.activation(pb[:, 13, 1:PBW], pb[:, 13, 1:PBW], ACT.Sigmoid).then_inc(sm["squashed"], 1)

            def pair(m):
                act.wait_ge(sm["low_done"], 2 * m + 1)
                act.activation(thirds(at_rt[:, 0, 0:W1]), PS[:, 0:3, 0:G3], ACT.Sigmoid, bias=rc[:, 0:1])\
                   .then_inc(sm["sg_ready"], 1)
                act.wait_ge(sm["low_done"], 2 * m + 2)
                act.activation(thirds(bonus[:, 0:W1]), PS[:, 3:6, 0:G3], ACT.Sigmoid, bias=rc[:, 1:2])\
                   .then_inc(sm["sg_ready"], 1)
                act.wait_ge(sm["cum_ready"], m + 1)
                act.activation(at_rt[:, 1, 0:W1], kt_[:, 0:W1], ACT.Exp, scale=-DECAY).then_inc(sm["exp_ready"], 1)
                act.activation(pinv[:, 0:W1], kt_[:, 0:W1], ACT.Exp, scale=DECAY).then_inc(sm["exp_ready"], 1)
                act.activation(at_rt[:, 0, 0:W1], at_rt[:, 0, 0:W1], ACT.Exp, scale=-DECAY)\
                   .then_inc(sm["exp_ready"], 1)
                act.wait_ge(sm["ss_done"], m + 1)
                act.activation(thirds(kt_[:, 0:W1]), PS[:, 0:3, 0:G3], ACT.Sqrt).then_inc(sm["root_ready"], 1)
                for w in range(3):
                    q = 3 * m + w
                    for blk in range(WAVE):
                        act.wait_ge(sm["tm_done"], 3 * q + (blk + 1))
                        act.activation(tm[:, blk, :, :], PS[:, blk, :].rearrange("p (a b) -> p a b", a=4),
                                       ACT.Copy).then_inc(sm["tm_ready"], 1)
                    act.wait_ge(sm["akv_done"], q + 1)
                    act.activation(akv[:, :, :, :].rearrange("p h b c -> p (h b c)"), PS[:, 6, 0:6 * HD],
                                   ACT.Copy).then_inc(sm["akv_ready"], 1)
                    for l in range(LEVELS - 1):
                        for h in range(2):
                            act.wait_ge(sm["y_done"], 10 * q + (2 * l + h + 1))
                            act.activation(y_sb[:, h, :, :].rearrange("p b c -> p (b c)"),
                                           PS[:, h, 0:WAVE * P], ACT.Copy).then_inc(sm["ysb_ready"], 1)
                    act.wait_ge(sm["mh_done"], q + 1)
                    for h, r in enumerate(halves):
                        for p in range(2):
                            act.activation(h_bd[r, p:2 * WAVE:2, r],
                                           PS[r, 2 + p, 0:WAVE * P].rearrange("p (b c) -> p b c", b=WAVE)[:, :, HD:P],
                                           ACT.Copy).then_inc(sm["hbd_ready"], 1)
                    act.wait_ge(sm["yb_done"], q + 1)
                    for blk, n, c0 in wave_runs(w):
                        ins = act.activation(at_rt[:, 1, c0:c0 + n * P], PS[:, 7, blk * P:(blk + n) * P], ACT.Copy)
                    ins.then_inc(sm["y_stored"], 1)
                act.wait_ge(sm["vr_ready"], m + 1)
                act.activation(kt_[:, 0:W1], kt_[:, 0:W1], ACT.Sqrt).then_inc(sm["vroot_ready"], 1)
            repeat(act, 0, PAIRS, pair)

        def rwkv_pool(pool, chain):
            pool.wait_ge(sm["rw_loaded"], 64)

            def pair(m):
                pool.wait_ge(sm["gated"], m + 1)
                pool.tensor_copy(v_cur[:, 0:W1], pb[:, ds(m + 4, 1), 1:PBW].rearrange("p a c -> p (a c)"))\
                    .then_inc(sm["r_staged"], 1)
                pool.tensor_copy(wa2_cur[:, :], wa2[:, ds(m * P, P)]).then_inc(sm["r_staged"], 1)
                pool.tensor_copy(g2_cur[:, :], g2[:, ds(m * P, P)]).then_inc(sm["r_staged"], 1)
                pool.tensor_copy(rc[:, :], rw_par[:, ds(m, 1), :].rearrange("p a c -> p (a c)"))\
                    .then_inc(sm["r_staged"], 1)
                for w in range(3):
                    q = 3 * m + w
                    for h in range(2):
                        pool.wait_ge(sm["sa_ready"], 6 * q + (2 + (3 if h == 0 else 6)))
                        pool.tensor_tensor(bt_level[:, h, :, :], sa[:, h, :, 0, :],
                                           level_mask[:, 0:1, :].broadcast_to([P, WAVE, P]), ALU.mult)\
                            .then_inc(sm["bt_ready"], 1)
                        chain(pool.tensor_tensor(xx[:, h, 1, :, :], sa[:, h, :, 0, :],
                                                 x0_mask[:, 1:2, :].broadcast_to([P, WAVE, P]), ALU.mult))
                        pool.tensor_tensor(xx[:, h, :, :, :].rearrange("p a b c -> p (a b) c"),
                                           xx[:, h, :, :, :].rearrange("p a b c -> p (a b) c"),
                                           ident[:, :].unsqueeze(1).broadcast_to([P, 2 * WAVE, P]), ALU.add)\
                            .then_inc(sm["x_init"], 1)
                    pool.wait_ge(sm["y_stored"], q + 1)
                    pool.tensor_tensor(m_bd[:, :, :], ident[:, :].unsqueeze(1).broadcast_to([P, 2 * WAVE, P]),
                                       decay_end[:, 2 * WAVE * w:2 * WAVE * (w + 1)].unsqueeze(2)
                                       .broadcast_to([P, 2 * WAVE, P]), ALU.mult).then_inc(sm["mdiag_ready"], 1)
                    for l in range(1, LEVELS - 1):
                        for h in range(2):
                            pool.wait_ge(sm["y_done"], 10 * q + (2 * (l - 1) + h + 1))
                            pool.tensor_tensor(bt_level[:, h, :, :], sa[:, h, :, 0, :],
                                               level_mask[:, l:l + 1, :].broadcast_to([P, WAVE, P]), ALU.mult)\
                                .then_inc(sm["bt_ready"], 1)
            chain.loop(0, PAIRS, 6, pair)

        def rwkv_pe(pe):
            pe.wait_ge(sm["squashed"], 2)

            def spread(lhs, rows, rhs, bank):
                for g in range(3):
                    last = pe.matmul(PS[:, bank + g, 0:G3], lhs, rhs[rows, g * G3:(g + 1) * G3],
                                     start=True, stop=True)
                return last

            def pair(m):
                pe.wait_ge(sm["r_staged"], 4 * m + 4)
                low = pb[:, 12, 1:PBW]
                spread(wa2_cur[0:HD, :], halves[0], low, 0).then_inc(sm["low_done"], 1)
                spread(wa2_cur[HD:P, :], halves[1], low, 3).then_inc(sm["low_done"], 1)
                pe.wait_ge(sm["sg_ready"], 2 * m + 2)
                pe.wait_ge(sm["ksq_ready"], m + 1)
                spread(head_ones[:, :], slice(0, P), kt_[:, 0:W1], 0).then_inc(sm["ss_done"], 1)
                pe.wait_ge(sm["rk_ready"], m + 1)
                spread(head_ones[:, :], slice(0, P), kk_[:, 0:W1], 3).then_inc(sm["bonus_done"], 1)
                for w in range(3):
                    wave(m, w)
                pe.wait_ge(sm["y_stored"], 3 * m + 4)
                spread(head_ones[:, :], slice(0, P), at_rt[:, 1, 0:W1], 0).then_inc(sm["mean_done"], 1)
                pe.wait_ge(sm["yc_ready"], m + 1)
                spread(head_ones[:, :], slice(0, P), kt_[:, 0:W1], 3).then_inc(sm["var_done"], 1)
                spread(g2_cur[:, :], slice(0, P), pb[:, 13, 1:PBW], 0).then_inc(sm["zg_done"], 1)

            def wave(m, w):
                q = 3 * m + w
                cols = [slice(block_cols(WAVE * w + b), block_cols(WAVE * w + b) + P) for b in range(WAVE)]
                pe.wait_ge(sm["hat_ready"], q + 1)
                pe.wait_ge(sm["y_stored"], q + 1)
                for b in range(WAVE):
                    for i, src in enumerate([at_rt[:, 0, cols[b]], bk_hat[:, 0, b * P:(b + 1) * P],
                                             bk_hat[:, 1, b * P:(b + 1) * P], v_cur[:, cols[b]]]):
                        last = pe.transpose(PS[:, b, i * P:(i + 1) * P], src, ident[:, :])
                    last.then_inc(sm["tm_done"], 1)
                for h, r in enumerate(halves):
                    for b in range(WAVE):
                        u = 3 * h + b
                        pe.wait_ge(sm["sa_ready"], 6 * q + (u + 1))
                        pe.matmul(PS[:, 3 + u % 2, 0:2 * P], bt_[r, cols[b]], at_rt[r, :, cols[b]],
                                  start=True, stop=True)
                        pe.matmul(PS[:, 3 + u % 2, 2 * P:4 * P], kt_[r, cols[b]], at_rt[r, :, cols[b]],
                                  start=True, stop=True)
                        pe.matmul(PS[:, 5 + u % 2, 0:P], at_rt[r, 0, cols[b]], bt_[r, cols[b]],
                                  start=True, stop=True).then_inc(sm["ab_done"], 1)
                pe.wait_ge(sm["tm_ready"], 3 * q + 3)
                pe.wait_ge(sm["sa_ready"], 6 * q + 8)
                for h in range(2):
                    for b in range(WAVE):
                        u = 3 * h + b
                        last = pe.matmul(PS[:, 6, u * HD:(u + 1) * HD], sa[:, h, b, 2, :], tm[:, b, 3, halves[h]],
                                         start=True, stop=True)
                last.then_inc(sm["akv_done"], 1)
                for l in range(LEVELS - 1):
                    for h in range(2):
                        pe.wait_ge(sm["bt_ready"], 10 * q + (2 * l + h + 1))
                        if l == 0:
                            pe.wait_ge(sm["x_init"], 2 * q + (h + 1))
                        else:
                            pe.wait_ge(sm["xadd"], 10 * q + (2 * (l - 1) + h + 1))
                        for b in range(WAVE):
                            last = pe.matmul(PS[:, h, b * P:(b + 1) * P], bt_level[:, h, b, :], xx[:, h, 0, b, :],
                                             start=True, stop=True)
                        last.then_inc(sm["y_done"], 1)
                    for h in range(2):
                        pe.wait_ge(sm["ysb_ready"], 10 * q + (2 * l + h + 1))
                        for b in range(WAVE):
                            if l < LEVELS - 2:
                                pe.matmul(PS[:, 2 + 2 * h, b * P:(b + 1) * P], xx[:, h, 1, b, :], y_sb[:, h, b, :],
                                          start=True, stop=True)
                            last = pe.matmul(PS[:, 3 + 2 * h, b * P:(b + 1) * P], y_sb[:, h, b, :],
                                             xx[:, h, 1, b, :], start=True, stop=True)
                        last.then_inc(sm["xprod_done"], 1)
                pe.wait_ge(sm["akv_ready"], q + 1)
                for h in range(2):
                    pe.wait_ge(sm["xadd"], 10 * q + (8 + h + 1))
                    for b in range(WAVE):
                        pe.matmul(PS[:, h, b * P:b * P + HD], xx[:, h, 1, b, :], tm[:, b, 0, halves[h]],
                                  start=True, stop=True)
                        last = pe.matmul(PS[:, h, b * P + HD:(b + 1) * P], xx[:, h, 1, b, :], akv[:, h, b, :],
                                         start=True, stop=True)
                    last.then_inc(sm["wz_done"], 1)
                pe.wait_ge(sm["wz_ready"], 2 * q + 2)
                for h, r in enumerate(halves):
                    for b in range(WAVE):
                        last = pe.matmul(PS[r, 4, b * P:(b + 1) * P], wz[:, h, b, 0, :], sa[:, h, b, 1, :],
                                         start=True, stop=True)
                last.then_inc(sm["reff_done"], 1)
                for p, rows in enumerate(halves):
                    for h, r in enumerate(halves):
                        for b in range(WAVE):
                            pe.matmul(PS[r, 2 + p, b * P:b * P + HD], wz[rows, h, b, 0, :], tm[rows, b, 1, r],
                                      start=True, stop=True)
                            out = PS[r, 2 + p, b * P + HD:(b + 1) * P]
                            pe.matmul(out, tm[rows, b, 1, r], wz[rows, h, b, 1, :], start=True, stop=False)
                            last = pe.matmul(out, tm[rows, b, 2, r], tm[rows, b, 3, r], start=False, stop=True)
                last.then_inc(sm["mh_done"], 1)
                for b in range(WAVE):
                    for h, r in enumerate(halves):
                        out = PS[r, 7, b * P:(b + 1) * P]
                        pe.matmul(out, tm[:, b, 3, r], sa[:, h, b, 3, :], start=b == 0, stop=False,
                                  skip_group_check=True)
                        pe.matmul(out, wz[:, h, b, 1, :], sa[:, h, b, 1, :], start=False, stop=False,
                                  skip_group_check=True)
                steps = 2 * WAVE if w < 2 else 2 * WAVE - 1
                pe.wait_ge(sm["mbd_ready"], q + 1)
                pe.wait_ge(sm["s_init"], q + 1)
                for c in range(steps):
                    if c:
                        pe.wait_ge(sm["s_new"], 17 * m + (6 * w + c))
                    pe.matmul(PS[:, 5, 0:P], m_bd[:, c, :], s_bd[:, c, :], start=True, stop=True)\
                      .then_inc(sm["s_done"], 1)
                pe.wait_ge(sm["s_new"], 17 * m + (6 * w + 5))
                pe.wait_ge(sm["r_ready"], q + 1)
                for b in range(WAVE):
                    for p in range(2):
                        last = pe.matmul(PS[:, 7, b * P + p * HD:b * P + (p + 1) * HD], s_bd[:, 2 * b + p, :],
                                         r_eff[:, b, halves[p]], start=False, stop=True, skip_group_check=True)
                last.then_inc(sm["yb_done"], 1)
            repeat(pe, 0, PAIRS, pair)

        def rwkv_dve(dve, chain):
            for t in (at_rt[:, :, W1:WP], kt_[:, W1:WP], bt_[:, W1:WP], bonus[:, W1:WP], v_cur[:, W1:WP],
                      decay_end[:, :], h_bd[:, :, :]):
                dve.memset(t, 0.0)
            dve.wait_ge(sm["rw_loaded"], 64)
            chain(dve.tensor_scalar(rw_par[:, :, 7:8], rw_par[:, :, 3:4], -1.0, 1.0, ALU.mult, ALU.add))
            dve.memset(s_bd[:, :, :], 0.0).then_inc(sm["gated"], 1)
            dve.memset(wz[:, :, :, :, :], 0.0).then_inc(sm["sa_ready"], 2)
            dve.memset(r_eff[:, :, :], 0.0).then_inc(sm["y_stored"], 1)

            def prep(m):
                v = v_cur[:, 0:W1]
                k = pb[:, ds(m, 1), 1:PBW].rearrange("p a c -> p (a c)")
                r = pb[:, ds(m + 8, 1), 1:PBW].rearrange("p a c -> p (a c)")
                T0, T2, T1 = at_rt[:, 0, 0:W1], at_rt[:, 1, 0:W1], kt_[:, 0:W1]
                T3, T4, T5, T6 = pinv[:, 0:W1], bonus[:, 0:W1], kk_[:, 0:W1], bt_[:, 0:W1]
                dve.wait_ge(sm["sg_ready"], 2 * m + 1)
                for c in range(SEQ // CHUNK + 1):
                    c0 = c * CHUNK if c < SEQ // CHUNK else W1 - DEC
                    n = chain.step(dve.tensor_tensor_scan(kt_[:, c0:c0 + CHUNK], ones[:, 0:CHUNK],
                                                          at_rt[:, 0, c0:c0 + CHUNK], 0.0, ALU.mult, ALU.add))
                n = chain.step(dve.memset(kt_[:, SEQ:W1 - DEC], 0.0))
                chain.wait(n)
                dve.tensor_tensor(T0, T1, T0, ALU.subtract).then_inc(sm["cum_ready"], 1)
                chain(dve.tensor_scalar(T5, k, rc[:, 2:3], None, ALU.mult))
                dve.wait_ge(sm["exp_ready"], 3 * m + 3)
                dve.tensor_tensor(T1, T5, T5, ALU.mult).then_inc(sm["ksq_ready"], 1)
                dve.wait_ge(sm["root_ready"], m + 1)
                chain(dve.tensor_scalar(T1, T1, 1e-12, None, ALU.max))
                chain(dve.reciprocal(T1, T1))
                chain(dve.tensor_tensor(T5, T5, T1, ALU.mult))
                chain.step(dve.scalar_tensor_tensor(T0, T5, -1.0, T0, ALU.mult, ALU.mult))
                dve.wait_ge(sm["sg_ready"], 2 * m + 2)
                chain(dve.tensor_tensor(T6, T5, T4, ALU.mult))
                chain.step(dve.tensor_tensor(T6, T6, T3, ALU.mult))
                chain(dve.tensor_scalar(T1, T4, rc[:, 3:4], rc[:, 7:8], ALU.mult, ALU.add))
                chain(dve.tensor_tensor(T1, T1, k, ALU.mult))
                chain(dve.scalar_tensor_tensor(T5, r, rc[:, 4:5], T1, ALU.mult, ALU.mult))
                dve.tensor_tensor(T1, T1, T3, ALU.mult).then_inc(sm["rk_ready"], 1)
                nq = SEQ // CHUNK
                dve.tensor_copy(decay_end[:, 0:nq].unsqueeze(2),
                                at_rt[:, 1, 0:SEQ].rearrange("p (n c) -> p n c", c=CHUNK)[:, :, CHUNK - 1:CHUNK])
                chain(dve.tensor_copy(decay_end[:, nq:nq + 1], at_rt[:, 1, W1 - 1:W1]))
                chain(dve.tensor_tensor(T2, T2, r, ALU.mult))
                dve.wait_ge(sm["bonus_done"], m + 1)
                chain(dve.tensor_tensor(thirds(T4), PS[:, 3:6, 0:G3], thirds(v), ALU.mult))

            def wave(m, w):
                q = 3 * m + w
                for blk, n, c0 in wave_runs(w):
                    ends = decay_end[:, 2 * (WAVE * w + blk):2 * (WAVE * w + blk + n)]
                    for i, src in enumerate((bt_, kt_)):
                        ins = dve.tensor_tensor(
                            bk_hat[:, i, blk * P:(blk + n) * P].rearrange("p (a c) -> p a c", c=CHUNK),
                            src[:, c0:c0 + n * P].rearrange("p (a c) -> p a c", c=CHUNK),
                            ends.unsqueeze(2).broadcast_to([P, 2 * n, CHUNK]), ALU.mult)
                ins.then_inc(sm["hat_ready"], 1)
                if w == 0:
                    ins = dve.memset(s_bd[:, 0, :], 0.0)
                else:
                    dve.wait_ge(sm["y_stored"], 3 * m + (w + 1))
                    dve.wait_ge(sm["s_new"], 17 * m + 6 * w)
                    ins = dve.tensor_copy(s_bd[:, 0, :], s_bd[:, 2 * WAVE, :])
                if w == 2:
                    for r in halves:
                        ins = dve.tensor_copy(s_bd[r, 4, r], state_in[r, ds(m, 1), :].rearrange("p a c -> p (a c)"))
                ins.then_inc(sm["s_init"], 1)
                for h in range(2):
                    for b in range(WAVE):
                        u = 3 * h + b
                        dve.wait_ge(sm["ab_done"], 6 * q + (u + 1))
                        dve.tensor_tensor(sa[:, h, b, :, :], PS[:, 3 + u % 2, :].rearrange("p (a c) -> p a c", a=4),
                                          sa_mask[:, :, :], ALU.mult)
                        dve.tensor_tensor(xx[:, h, 0, b, :], PS[:, 5 + u % 2, 0:P], x0_mask[:, 0, :],
                                          ALU.mult).then_inc(sm["sa_ready"], 1)
                for l in range(LEVELS - 1):
                    for h in range(2):
                        dve.wait_ge(sm["xprod_done"], 10 * q + (2 * l + h + 1))
                        k0 = 0 if l < LEVELS - 2 else 1
                        dst = xx[:, h, k0:2, :, :].rearrange("p a b c -> p a (b c)")
                        dve.tensor_tensor(dst, PS[:, 2 + 2 * h + k0:4 + 2 * h, 0:WAVE * P], dst, ALU.add)\
                           .then_inc(sm["xadd"], 1)
                for h in range(2):
                    dve.wait_ge(sm["wz_done"], 2 * q + (h + 1))
                    dve.tensor_copy(wz[:, h, :, :, :].rearrange("p b a c -> p (b a c)"), PS[:, h, 0:WAVE * P])\
                       .then_inc(sm["wz_ready"], 1)
                dve.wait_ge(sm["reff_done"], q + 1)
                for blk, n, c0 in wave_runs(w):
                    ins = dve.tensor_tensor(r_eff[:, blk:blk + n, :].rearrange("p b c -> p (b c)"),
                                            PS[:, 4, blk * P:(blk + n) * P], at_rt[:, 1, c0:c0 + n * P], ALU.add)
                ins.then_inc(sm["r_ready"], 1)
                dve.wait_ge(sm["mh_done"], q + 1)
                dve.wait_ge(sm["mdiag_ready"], q + 1)
                dve.wait_ge(sm["hbd_ready"], 4 * q + 4)
                for r in halves:
                    for p in range(2):
                        ins = dve.tensor_tensor(
                            m_bd[r, p:2 * WAVE:2, r],
                            PS[r, 2 + p, 0:WAVE * P].rearrange("p (b c) -> p b c", b=WAVE)[:, :, 0:HD],
                            m_bd[r, p:2 * WAVE:2, r], ALU.add)
                ins.then_inc(sm["mbd_ready"], 1)
                for c in range(2 * WAVE if w < 2 else 2 * WAVE - 1):
                    dve.wait_ge(sm["s_done"], 17 * m + (6 * w + c + 1))
                    to = 2 * WAVE if w == 2 and c == 3 else c + 1
                    dve.tensor_tensor(s_bd[:, to, :], PS[:, 5, 0:P], h_bd[:, c, :], ALU.add).then_inc(sm["s_new"], 1)
                if w == 2:
                    dve.wait_ge(sm["s_new"], 17 * m + 17)
                    for i, slot in enumerate((2 * WAVE, 2 * WAVE - 1)):
                        for r in halves:
                            dve.tensor_copy(state_out[r, i, ds(m, 1), :].rearrange("p a c -> p (a c)"),
                                            s_bd[r, slot, r]).then_inc(sm["state_ready"], 1)

            def finish(m):
                T0, T1, T4 = at_rt[:, 0, 0:W1], kt_[:, 0:W1], bonus[:, 0:W1]
                dve.wait_ge(sm["mean_done"], m + 1)
                chain(dve.scalar_tensor_tensor(thirds(T0), PS[:, 0:3, 0:G3], -1.0 / HD, thirds(at_rt[:, 1, 0:W1]),
                                               ALU.mult, ALU.add))
                dve.tensor_tensor(T1, T0, T0, ALU.mult).then_inc(sm["yc_ready"], 1)
                dve.wait_ge(sm["var_done"], m + 1)
                chain(dve.tensor_scalar(thirds(T1), PS[:, 3:6, 0:G3], 1.0 / HD, LNX_EPS, ALU.mult, ALU.add))
                dve.reciprocal(T1, T1).then_inc(sm["vr_ready"], 1)
                dve.wait_ge(sm["vroot_ready"], m + 1)
                chain(dve.tensor_tensor(T0, T0, T1, ALU.mult))
                chain(dve.tensor_scalar(T0, T0, rc[:, 5:6], rc[:, 6:7], ALU.mult, ALU.add))
                chain(dve.tensor_tensor(T0, T0, T4, ALU.add))
                dve.wait_ge(sm["zg_done"], m + 1)
                dve.tensor_tensor(pb[:, ds(m + 8, 1), 1:PBW].rearrange("p a (g c) -> p (a g) c", g=3),
                                  PS[:, 0:3, 0:G3], thirds(T0), ALU.mult).then_inc(sm["gated"], 1)

            def pair(m):
                prep(m)
                for w in range(3):
                    wave(m, w)
                finish(m)
            chain.loop(0, PAIRS, 36, pair)

        UNITS = 2 * BLOCKS
        TURN_CREDIT = 6

        def in_turn(*parts):
            for step in range(UNITS + max(lag for _, lag in parts)):
                for part, lag in parts:
                    if 0 <= step - lag < UNITS:
                        part(step - lag)

        def unit_shape(cfg, b):
            if b < BLOCKS - 1:
                n = min(b + 1, cfg["nb"])
                return P, n, 0, n * P
            return DEC, 0, cfg["cache"], cfg["cache"] * P + DEC

        def att_pe(pe, cfg):
            mem, nb = cfg["mem"], cfg["nb"]
            pe.wait_ge(sm["hk_loaded"], cfg["hk"] + 16 * 10)
            for hd in range(8):
                if hd >= 2:
                    pe.wait_ge(sm["bias_ready"], cfg["bias0"] + hd - 1)
                for c0 in range(0, nb * P, 512):
                    cn = min(512, nb * P - c0)
                    last = pe.matmul(PS[:, 2 * (hd % 2) + c0 // 512, 0:cn], flip[:, :],
                                     mem["hankel"][:, hd, c0:c0 + cn], start=True, stop=True)
                last.then_inc(sm["hk_done"], 1)
            pe.wait_ge(sm["bias_ready"], cfg["bias0"] + 10)

            def token_major_v(m):
                pe.wait_ge(sm["v_staged"], 2 * m + (cfg["v0"] + 2))
                for b in range(BLOCKS):
                    if b % 4 == 0 and b >= 8:
                        pe.wait_ge(sm["vt_ready"], 3 * m + (3 * cfg["v0"] // 2 + b // 4 - 1))
                    last = pe.transpose(PS[:, 4 + (b // 4) % 2, (b % 4) * P:(b % 4 + 1) * P],
                                        mem["vf"][:, b * P:(b + 1) * P], ident[:, :])
                    if b % 4 == 3 or b == BLOCKS - 1:
                        last.then_inc(sm["vtr_done"], 1)
                pe.wait_ge(sm["vt_ready"], 3 * m + (3 * cfg["v0"] // 2 + 3))

            def pair(m):
                U0 = cfg["unit0"]
                if not cfg["shared_v"]:
                    token_major_v(m)
                pe.wait_ge(sm["q_staged"], 2 * m + (cfg["q0"] + 2))

                def scores(u):
                    b, h = divmod(u, 2)
                    rows, own, cached, width = unit_shape(cfg, b)
                    base = 2 * (u % 2)
                    pe.wait_ge(sm["st_done"], UNITS * m + (U0 + u + 1))
                    q = mem["qz"][:, h, b * P:(b + 1) * P]
                    if own:
                        parts = [(cfg["keys"](m, (b + 1 - own) * P, width), 0, width)]
                    else:
                        parts = [(mem["k_cache"][:, cfg["kslot"](m), :].rearrange("p a c -> p (a c)"), 0, cached * P),
                                 (cfg["keys"](m, SEQ, DEC), cached * P, DEC)]
                    for src, to, width in parts:
                        for c0 in range(0, width, 512):
                            cn = min(512, width - c0)
                            col = to + c0
                            last = pe.matmul(PS[:, base + col // 512, col % 512:col % 512 + cn], q,
                                             src[:, c0:c0 + cn], start=True, stop=True)
                    last.then_inc(sm["sc_done"], 1)

                def turn(u):
                    b, h = divmod(u, 2)
                    rows, own, cached, width = unit_shape(cfg, b)
                    pe.wait_ge(sm["p_ready"], UNITS * m + (U0 + u + 1))
                    pe.wait_ge(sm["pt_ev"], UNITS * m + (U0 + u + 3 - cfg["turns"]))
                    bank = 4 + (u % 2 if cfg["turns"] == 2 else 0)
                    for i in range((width + P - 1) // P):
                        n = min(P, width - i * P)
                        last = pe.transpose(PS[0:n, bank + i // 4, (i % 4) * P:(i % 4 + 1) * P],
                                            mem["s"][:, u % cfg["slots"], i * P:i * P + n], ident[:, :])
                    last.then_inc(sm["pt_done"], 1)

                def values(u):
                    b, h = divmod(u, 2)
                    rows, own, cached, width = unit_shape(cfg, b)
                    r = halves[h]
                    pe.wait_ge(sm["pt_ev"], UNITS * m + (U0 + u + 3))
                    pe.wait_ge(sm["o_ev"], UNITS * m + (U0 + u + 1))
                    count = (width + P - 1) // P
                    for i in range(count):
                        n = min(P, width - i * P)
                        if own:
                            v = mem["vt"][:, b + 1 - own + i, r]
                        elif i < cached:
                            v = mem["vcc"][:, i, r]
                        else:
                            v = mem["vt"][0:DEC, BLOCKS - 1, r]
                        last = pe.matmul(PS[r, 6 + u % 2, 0:rows], v, mem["pt"][0:n, u % 2, i, 0:rows],
                                         start=i == 0, stop=i == count - 1)
                    last.then_inc(sm["pv_done"], 1)

                scores(0)
                in_turn((scores, -1), (turn, cfg["lag"]), (values, cfg["lag"] + 1))
            if cfg["shared_v"]:
                token_major_v(0)
            repeat(pe, 0, PAIRS, pair)

        def att_act(act, cfg):
            mem = cfg["mem"]

            def token_major_v(m):
                for i in range(3):
                    n = min(4, BLOCKS - 4 * i)
                    act.wait_ge(sm["vtr_done"], 3 * m + (3 * cfg["v0"] // 2 + i + 1))
                    rows = P if n > 1 else DEC
                    act.activation(mem["vt"][0:rows, 4 * i:4 * i + n, :],
                                   PS[0:rows, 4 + i % 2, 0:n * P].rearrange("p (a c) -> p a c", c=P), ACT.Copy)\
                       .then_inc(sm["vt_ready"], 1)

            def pair(m):
                U0 = cfg["unit0"]
                if not cfg["shared_v"]:
                    token_major_v(m)

                def exps(u):
                    i = u % cfg["slots"]
                    rows, _, _, width = unit_shape(cfg, u // 2)
                    st = mem["stat"]
                    if cfg["sink"]:
                        act.wait_ge(sm["max_ready"], UNITS * m + (U0 + u + 1))
                    else:
                        act.wait_ge(sm["st_done"], UNITS * m + (U0 + u + 3))
                    ins = act.activation(mem["s"][0:rows, i, 0:width], mem["s"][0:rows, i, 0:width], ACT.Exp,
                                         bias=st[0:rows, i, 0:1], accum_out=st[0:rows, i, 1:2])
                    if cfg["sink"]:
                        ins = act.activation(st[0:rows, i, 3:4], sink[0:rows, ds(2 * m + u % 2, 1)], ACT.Exp,
                                             bias=st[0:rows, i, 0:1])
                    ins.then_inc(sm["exp_done"], 1)

                def evac(u):
                    rows, _, _, width = unit_shape(cfg, u // 2)
                    act.wait_ge(sm["pt_done"], UNITS * m + (U0 + u + 1 + TURN_CREDIT))
                    act.wait_ge(sm["pv_done"], UNITS * m + (U0 + u + 1))
                    whole = width // P
                    bank = 4 + (u % 2 if cfg["turns"] == 2 else 0)
                    pieces = [(i, min(4, whole - i)) for i in range(0, whole, 4)]
                    for i, n in pieces:
                        ins = act.activation(mem["pt"][:, u % 2, i:i + n, 0:rows],
                                             PS[:, bank + i // 4, 0:n * P].rearrange("p (a c) -> p a c", c=P)[:, :, 0:rows],
                                             ACT.Copy)
                    if width % P:
                        i = whole
                        ins = act.activation(mem["pt"][0:DEC, u % 2, i, 0:rows],
                                             PS[0:DEC, bank + i // 4, (i % 4) * P:(i % 4) * P + rows], ACT.Copy)
                    ins.then_inc(sm["pt_ev"], 1)

                in_turn((exps, 0), (evac, cfg["lag"]))
            if cfg["shared_v"]:
                token_major_v(0)
            repeat(act, 0, PAIRS, pair)

        def att_pool(pool, cfg, chain):
            mem = cfg["mem"]
            for t in (mem["qz"][:, :, NT:BLOCKS * P], mem["vf"][:, NT:BLOCKS * P]):
                chain(pool.memset(t, 0.0))

            def stage_v(m):
                pool.tensor_copy(mem["vf"][:, 0:NT], cfg["v"](m)).then_inc(sm["v_staged"], 1)
                pool.tensor_copy(mem["vcc"][:, :, :], cfg["vc"](m)).then_inc(sm["v_staged"], 1)

            def pair(m):
                pool.wait_ge(sm["st_done"], UNITS * m + (cfg["unit0"] + 2))
                for h in range(2):
                    pool.tensor_tensor(mem["qz"][:, h, 0:NT], cfg["q"](m),
                                       head_ones[:, h * HD:h * HD + 1].broadcast_to([P, NT]), ALU.mult)\
                        .then_inc(sm["q_staged"], 1)
                if not cfg["shared_v"]:
                    pool.wait_ge(sm["pv_done"], UNITS * m + (cfg["unit0"] + 2))
                    stage_v(m)
                if not cfg["sink"]:
                    pool.wait_ge(sm["z_ready"], m + 1)
                    pool.tensor_copy(cc[:, :], conv_par[:, ds(m, 1), :].rearrange("p a c -> p (a c)"))\
                        .then_inc(sm["conv_staged"], 1)
            pool.wait_ge(sm["hk_loaded"], cfg["hk"] + 16 * 10)
            if cfg["shared_v"]:
                stage_v(0)
            repeat(pool, 0, PAIRS, pair)

        def att_dve(dve, cfg, chain, taps=None):
            mem, nb = cfg["mem"], cfg["nb"]
            if cfg["sink"]:
                chain(dve.tensor_scalar(neg_sink[:, :], sink[:, :], -1.0, None, ALU.mult))
            for hd in range(8):
                dve.wait_ge(sm["hk_done"], cfg["bias0"] * 8 // 10 + hd + 1)
                for c0 in range(0, nb * P, 512):
                    cn = min(512, nb * P - c0)
                    ins = dve.tensor_copy(mem["bias"][:, hd, c0:c0 + cn], PS[:, 2 * (hd % 2) + c0 // 512, 0:cn])
                ins.then_inc(sm["bias_ready"], 1)
            dve.wait_ge(sm["bias_ready"], cfg["bias0"] + 8)
            dve.memset(mem["bias"][0:HD, :, nb * P - CHUNK:nb * P], NEG).then_inc(sm["bias_ready"], 1)
            dve.memset(mem["bias"][HD:P, :, 0:CHUNK], NEG).then_inc(sm["bias_ready"], 1)
            dve.wait_ge(sm["bias_ready"], cfg["bias0"] + 10)
            if cfg["unit0"] == 0:
                for i, (credit, count) in enumerate(((sm["st_done"], 2), (sm["pt_done"], TURN_CREDIT),
                                                     (sm["pt_ev"], 2), (sm["pv_done"], 2), (sm["o_ev"], 2))):
                    dve.memset(mem["stat"][:, i // 4, i % 4:i % 4 + 1], 0.0).then_inc(credit, count)
                dve.wait_ge(sm["o_ev"], 2)

            def pair(m):
                U0 = cfg["unit0"]
                st = mem["stat"]
                if taps:
                    dve.wait_ge(sm["conv_staged"], m + 1)

                def scores(u):
                    b, h = divmod(u, 2)
                    i = u % cfg["slots"]
                    rows, own, cached, width = unit_shape(cfg, b)
                    dve.wait_ge(sm["sc_done"], UNITS * m + (U0 + u + 1))
                    dve.wait_ge(sm["pt_done"], UNITS * m + (U0 + u + 1 + TURN_CREDIT - cfg["slots"]))
                    blocks = own if own else cached + 1
                    bias0 = (nb - blocks) * P
                    for c0 in range(0, width, 512):
                        cn = min(512, width - c0)
                        n = chain.step(dve.scalar_tensor_tensor(
                            mem["s"][0:rows, i, c0:c0 + cn], PS[0:rows, 2 * (u % 2) + c0 // 512, 0:cn],
                            HD ** -0.5, mem["bias"][0:rows, ds(2 * m + h, 1), bias0 + c0:bias0 + c0 + cn]
                            .rearrange("p a c -> p (a c)"), ALU.mult, ALU.add))
                    chain.wait(n)
                    ins = dve.tensor_reduce(st[0:rows, i, 0:1], mem["s"][0:rows, i, 0:width], AX, ALU.max,
                                            negate=True)
                    ins.then_inc(sm["st_done"], 1)
                    if cfg["sink"]:
                        dve.wait_ge(sm["st_done"], UNITS * m + (U0 + u + 3))
                        dve.tensor_tensor(st[0:rows, i, 0:1], st[0:rows, i, 0:1],
                                          neg_sink[0:rows, ds(2 * m + h, 1)], ALU.min).then_inc(sm["max_ready"], 1)

                def norm(u):
                    i = u % cfg["slots"]
                    rows, _, _, width = unit_shape(cfg, u // 2)
                    dve.wait_ge(sm["exp_done"], UNITS * m + (U0 + u + 1))
                    if cfg["sink"]:
                        chain(dve.tensor_tensor(st[0:rows, i, 1:2], st[0:rows, i, 1:2],
                                                st[0:rows, i, 3:4], ALU.add))
                    chain(dve.reciprocal(st[0:rows, i, 2:3], st[0:rows, i, 1:2]))
                    dve.tensor_scalar(mem["s"][0:rows, i, 0:width], mem["s"][0:rows, i, 0:width],
                                      st[0:rows, i, 2:3], None, ALU.mult).then_inc(sm["p_ready"], 1)

                def out(u):
                    b, h = divmod(u, 2)
                    rows = unit_shape(cfg, b)[0]
                    dve.wait_ge(sm["pv_done"], UNITS * m + (U0 + u + 1 + 2))
                    dve.tensor_copy(cfg["q"](m)[halves[h], b * P:b * P + rows], PS[halves[h], 6 + u % 2, 0:rows])\
                       .then_inc(sm["o_ev"], 1)

                parts = [(scores, 0), (lambda u: taps(m, u), 0), (norm, cfg["lag"]), (out, cfg["lag"] + 2)]
                in_turn(*[part for part in parts if taps or part is not parts[1]])
                if taps:
                    taps(m, None)
            chain.loop(0, PAIRS, cfg["chain"], pair)

        def conv_taps(chain, dve):
            zc = mem_c["zc"]

            def taps(m, u):
                if u is None:
                    dve.tensor_copy(z_buf[:, ds(m, 1), 0:SEQ].rearrange("p a c -> p (a c)"), zc[:, 0:SEQ])
                    dve.tensor_copy(z_buf[:, ds(m, 1), SEQ:NT].rearrange("p a c -> p (a c)"), zc[:, ZW - DEC:ZW])\
                       .then_inc(sm["z_ready"], 1)
                    return
                for t in range(TAPS * u // UNITS, TAPS * (u + 1) // UNITS):
                    src = u_buf[:, ds(m, 1), t:t + ZW].rearrange("p a c -> p (a c)")
                    if t == 0:
                        chain(dve.tensor_scalar(zc[:, :], src, cc[:, 0:1], cc[:, TAPS:TAPS + 1], ALU.mult, ALU.add))
                    else:
                        chain(dve.scalar_tensor_tensor(zc[:, :], src, cc[:, t:t + 1], zc[:, :], ALU.mult, ALU.add))
            return taps

        QN = NT // 4

        def quarters(t):
            return t.rearrange("p (g c) -> p g c", g=4)

        def ln_pe(pe):
            for src, bank, done in ((z_buf, 0, sm["lnm_done"]), (ln_t, 4, sm["lnv_done"])):
                for i in range(4):
                    if bank:
                        pe.wait_ge(sm["lnq_ready"], i + 1)
                    for g in range(4):
                        last = pe.matmul(PS[:, bank + g, 0:QN], ones[:, :], src[:, i, g * QN:(g + 1) * QN],
                                         start=i == 0, stop=i == 3)
                last.then_inc(done, 1)

        def ln_dve(dve, chain):
            dve.wait_ge(sm["lnm_done"], 1)
            for i in range(4):
                dve.scalar_tensor_tensor(quarters(z_buf[:, i, :]), PS[:, 0:4, 0:QN], -1.0 / 512,
                                         quarters(z_buf[:, i, :]), ALU.mult, ALU.add).then_inc(sm["lnc_ready"], 1)
            dve.wait_ge(sm["lnv_done"], 1)
            chain(dve.tensor_scalar(quarters(ln_r[:, :]), PS[:, 4:8, 0:QN], 1.0 / 512, LN_EPS, ALU.mult, ALU.add))
            dve.reciprocal(ln_r[:, :], ln_r[:, :]).then_inc(sm["lnr_ready"], 1)
            dve.wait_ge(sm["lnz_ready"], 1)
            for i in range(4):
                dve.tensor_tensor(z_buf[:, i, :], z_buf[:, i, :], ln_r[:, :], ALU.mult).then_inc(sm["lnc_ready"], 1)

        def ln_pool(pool):
            for i in range(4):
                pool.wait_ge(sm["lnc_ready"], i + 1)
                pool.tensor_tensor(ln_t[:, i, :], z_buf[:, i, :], z_buf[:, i, :], ALU.mult).then_inc(sm["lnq_ready"], 1)

        def ln_act(act):
            act.wait_ge(sm["lnr_ready"], 1)
            act.activation(ln_r[:, :], ln_r[:, :], ACT.Sqrt).then_inc(sm["lnz_ready"], 1)
            for i in range(4):
                act.wait_ge(sm["lnc_ready"], 4 + i + 1)
                act.activation(z_buf[:, i, :], z_buf[:, i, :], ACT.Silu, scale=conv_par[:, i, TAPS + 1:TAPS + 2],
                               bias=conv_par[:, i, TAPS + 2:TAPS + 3]).then_inc(sm["silu_ready"], 1)

        flat = "p a c -> p (a c)"
        cfg_a = dict(nb=2, cache=1, mem=mem_a, sink=True, unit0=0, hk=0, bias0=0, q0=0, v0=0, chain=54,
                     slots=6, lag=2, turns=2, shared_v=True,
                     keys=lambda m, c0, cn: akvq[:, 0, c0:c0 + cn], kslot=lambda m: slice(0, 1),
                     q=lambda m: akvq[:, ds(m + 2, 1), :].rearrange(flat), v=lambda m: akvq[:, 1, :],
                     vc=lambda m: mem_a["v_cache"][:, :, :])
        cfg_c = dict(nb=5, cache=2, mem=mem_c, sink=False, unit0=PAIRS * UNITS, hk=160, bias0=10, q0=8, v0=2,
                     chain=26 + 18 + 31, slots=3, lag=1, turns=1, shared_v=False,
                     keys=lambda m, c0, cn: cproj[:, ds(m, 1), c0:c0 + cn].rearrange(flat),
                     kslot=lambda m: ds(m, 1),
                     q=lambda m: cproj[:, ds(m + 8, 1), :].rearrange(flat),
                     v=lambda m: cproj[:, ds(m + 4, 1), :].rearrange(flat),
                     vc=lambda m: mem_c["v_cache"][:, :, ds(m * P, P)])

        block = ctx.enter_context(nc.Block())

        @block.sync
        def _(sp):
            n_const = 0
            for name, t in (("ident", ident), ("flip", flip), ("ones", ones), ("head_ones", head_ones),
                            ("sa_mask", sa_mask), ("level_mask", level_mask), ("gains", gains), ("mu", mu),
                            ("shift_in", shift_in), ("rw_par", rw_par), ("conv_par", conv_par), ("sink", sink),
                            ("pick_a", pick_a), ("pick_c", pick_c), ("table_a", table_a), ("table_c", table_c)):
                sp.dma_start(whole(t), d[name]).then_inc(sm["consts_loaded"], 16)
                n_const += 16
                if name == "gains":
                    for g, (c0, cn) in enumerate(GROUPS):
                        sp.dma_start(x[:, :, c0:c0 + cn], d["x"][:, :, c0:c0 + cn]).then_inc(x_loaded[g], 16)
                    sp_first(sp, 0)
            assert n_const == N_CONST
            sp.wait_ge(sm["vec_copied"], 3)
            sp.dma_start(vec_home.ap().rearrange("a h c -> h a c"), vec_sb[0:8, :, :]).then_inc(sm["vec_stored"], 16)
            sp_rest(sp, 0)
            sp_first(sp, 1)
            sp.wait_ge(sm["vec_stored"], 16)
            sp.wait_ge(sm["barrier"], 4)
            for t, name in ((wa2, "wa2"), (g2, "g2"), (x0_mask, "x0_mask"), (state_in, "state_in")):
                sp.dma_start(whole(t), d[name]).then_inc(sm["rw_loaded"], 16)
            sp.dma_start(d["out_akv"], akvq[:, 0:2, NT - 192:NT]).then_inc(sm["stored"], 16)
            sp.wait_ge(sm["barrier"], 8)
            sp.dma_start(d["out_state"], state_out[:, :, :, :]).then_inc(sm["stored"], 16)
            sp.dma_start(d["out_shift"], shift_out[:, :, :]).then_inc(sm["stored"], 16)
            sp.wait_ge(sm["stored"], 48)

            def attention_loads(mem, which, nb, length, kc, vc):
                for hd in range(8):
                    src = bass.AP(tensor=vec_home, offset=(which * 8 + hd) * VEC_C, ap=[[1, P], [1, nb * P]])
                    sp.dma_start(mem["hankel"][:, hd, :], src).then_inc(sm["hk_loaded"], 16)
                sp.dma_start(mem["k_cache"][:, :, :], d[kc]).then_inc(sm["hk_loaded"], 16)
                sp.dma_start(mem["v_cache"][:, :, :], d[vc]).then_inc(sm["hk_loaded"], 16)

            attention_loads(mem_a, 0, 2, VEC_A, "a_kc", "a_vc")
            sp.wait_ge(sm["barrier"], 12)
            for g, (c0, cn) in enumerate(GROUPS):
                sp.dma_start(x[:, :, c0:c0 + cn], d["x"][:, :, c0:c0 + cn]).then_inc(x_loaded[g], 16)
            sp_rest(sp, 1)
            for s in range(2, S_IN[1]):
                sp_first(sp, s)
                sp_rest(sp, s)
            sp_first(sp, S_IN[1])
            sp.wait_ge(sm["evac_done"], (x_from[2] + KT) * NG)
            sp.dma_start(x_home, x[:, :, :]).then_inc(sm["x_saved"], 16)
            sp_rest(sp, S_IN[1])
            sp_first(sp, S_IN[1] + 1)
            sp.wait_ge(sm["barrier"], 16)
            sp.dma_start(u_buf[:, :, TAPS - 1 + SEQ:2 * (TAPS - 1) + SEQ], d["conv_in"]).then_inc(sm["cstate_loaded"], 16)
            attention_loads(mem_c, 1, 5, VEC_C, "c_kc", "c_vc")
            sp.dma_start(d["out_ckv"], cproj[:, 0:8, 512:NT]).then_inc(sm["stored"], 16)
            sp.dma_start(d["out_conv"][:, :, 0, :], u_buf[:, :, SEQ:SEQ + TAPS - 1]).then_inc(sm["stored"], 16)
            sp.dma_start(d["out_conv"][:, :, 1, :], u_buf[:, :, UW - TAPS + 1:UW]).then_inc(sm["stored"], 16)
            sp.wait_ge(sm["barrier"], 20)
            sp.wait_ge(sm["stored"], 96)
            for g, (c0, cn) in enumerate(GROUPS):
                sp.dma_start(x[:, :, c0:c0 + cn], x_home[:, :, c0:c0 + cn]).then_inc(x_loaded[g], 16)
            sp_rest(sp, S_IN[1] + 1)
            for s in range(S_IN[1] + 2, len(stages)):
                sp_first(sp, s)
                sp_rest(sp, s)
            for g, (c0, cn) in enumerate(GROUPS):
                sp.wait_ge(sm["y_ready"], KT * (g + 1))
                sp.dma_start(d["out_y"][:, :, c0:c0 + cn], x[:, :, c0:c0 + cn]).then_inc(sm["stored"], 16)
            sp.wait_ge(sm["stored"], 96 + 48)

        @block.tensor
        def _(pe):
            pe.wait_ge(sm["consts_loaded"], N_CONST)
            pe.matmul(PS[0:8, 7, 0:VEC_A], table_a[:, :], pick_a[:, :], start=True, stop=True).then_inc(sm["vec_done"], 1)
            for n, c0 in enumerate(range(0, VEC_C, 512)):
                pe.wait_ge(sm["vec_copied"], n + 1)
                cn = min(512, VEC_C - c0)
                for k in range(3):
                    last = pe.matmul(PS[0:8, 7, 0:cn], table_c[:, k, :], pick_c[:, k, c0:c0 + cn],
                                     start=k == 0, stop=k == 2)
                last.then_inc(sm["vec_done"], 1)
            pe.wait_ge(sm["vec_copied"], 3)
            pe_stage(pe, 0, h_hi, h_lo, h_groups_first(pe, 0), norm=0)
            pe.wait_ge(sm["evac_done"], bases[1] * NG)
            sync_all("pe", pe)
            rwkv_pe(pe)
            sync_all("pe", pe)
            att_pe(pe, cfg_a)
            sync_all("pe", pe)
            pe_stage(pe, 1, h_hi, h_lo, h_groups_first(pe, 1))
            for n, (sg, sd, k0, kn) in enumerate(groups0):
                pe_stage(pe, sg, h_hi, h_lo, None if n else h_groups_first(pe, 2), norm=None if n else 1)
                pe_stage(pe, sd, hid_hi, hid_lo, hidden_ready(pe, 0, k0, kn))
            pe_stage(pe, S_IN[1], h_hi, h_lo, h_tiles_first(pe, 3), norm=2)
            pe.wait_ge(sm["evac_done"], bases[S_IN[1] + 1] * NG)
            sync_all("pe", pe)
            att_pe(pe, cfg_c)
            sync_all("pe", pe)
            ln_pe(pe)
            sync_all("pe", pe)
            pe_stage(pe, S_IN[1] + 1, h_hi, h_lo, h_groups_first(pe, 4))
            for n, (sg, sd, k0, kn) in enumerate(groups1):
                pe_stage(pe, sg, h_hi, h_lo, None if n else h_groups_first(pe, 5), norm=None if n else 3)
                pe_stage(pe, sd, hid_hi, hid_lo, hidden_ready(pe, 1, k0, kn))
            pe_stats(pe, 4)

        @block.scalar
        def _(act):
            act.wait_ge(sm["consts_loaded"], N_CONST)
            act_h(act, 0, 0, by_group)
            act_hi(act, 0, 0, 0, KT)
            act_hi(act, 0, 1, 0, KT)
            act_rstd(act, 0)
            act_stage(act, 0)
            sync_all("act", act)
            rwkv_act(act)
            sync_all("act", act)
            att_act(act, cfg_a)
            sync_all("act", act)
            act_concat(act, 0)
            act_stage(act, 1)

            def ffn(layer, groups, norm, h):
                act.wait_ge(sm["product_done"], bases[groups[0][0]] * NG)
                act_h(act, norm, h, by_group)
                act_rstd(act, norm)
                for n, (sg, sd, k0, kn) in enumerate(groups):
                    act_hidden(act, sg, layer, k0, kn)
                    last = n == len(groups) - 1 and layer == 0
                    act_stage(act, sd, (lambda j, slot: act_h(act, 2, 3, [(2 * j + slot, g) for g in range(NG)]))
                              if last else None)

            ffn(0, groups0, 1, 2)
            act_rstd(act, 2)

            def conv_gate(j, slot):
                if slot:
                    return
                for g, (c0, cn) in enumerate(GROUPS):
                    act.wait_ge(sm["evac_done"], j * (2 * NG) + ((bases[S_IN[1]] + 12) * NG + g + 1))
                    act.activation(gate_t[:, g, 0:cn], gate_t[:, g, 0:cn], ACT.Sigmoid).then_inc(sm["gate_ready"], 1)
            base = bases[S_IN[1]]

            def splits(j):
                for slot in range(2):
                    act_hi(act, j, slot, base + 2, KT)

            def conv_pair(j):
                for slot in range(2):
                    conv_gate(j, slot)
                    act_hi(act, j, slot, base + 14, KT)
            repeat(act, 0, 6, splits)
            repeat(act, 0, 3, conv_pair)
            conv_pair_last = 3
            for slot in range(2):
                conv_gate(conv_pair_last, slot)
                act_hi(act, 0, slot, bases[S_IN[1] + 1], KT)
            sync_all("act", act)
            att_act(act, cfg_c)
            sync_all("act", act)
            ln_act(act)
            sync_all("act", act)
            act_concat(act, 1)
            act_stage(act, S_IN[1] + 1)
            ffn(1, groups1, 3, 5)
            act_rstd(act, 4)

        @block.gpsimd
        def _(pool):
            chain = Chain(pool, sm["pool_chain"])

            def squares(norm):
                return lambda j, slot: pool_sq(pool, norm, 2 * j + slot)

            pool.wait_ge(sm["consts_loaded"], N_CONST)
            pool_sq_start(pool, 0)
            pool_lo(pool, 0, 0, KT)
            pool_lo(pool, 1, 1, KT)
            for i in range(KT):
                pool_sq(pool, 0, i)
            pool_stage(pool, 0)
            sync_all("pool", pool)
            rwkv_shift_pool(pool)
            rwkv_pool(pool, chain)
            sync_all("pool", pool)
            att_pool(pool, cfg_a, chain)
            sync_all("pool", pool)
            pool_sq_start(pool, 1)
            pool_stage(pool, 1, squares(1))
            for n, (sg, sd, k0, kn) in enumerate(groups0):
                pool_hidden(pool, sg, 0, k0, kn)
                last = n == len(groups0) - 1
                if last:
                    pool_sq_start(pool, 2)
                pool_stage(pool, sd, squares(2) if last else None)
            pool_stage(pool, S_IN[1])
            sync_all("pool", pool)
            att_pool(pool, cfg_c, chain)
            sync_all("pool", pool)
            ln_pool(pool)
            sync_all("pool", pool)
            pool_sq_start(pool, 3)
            pool_stage(pool, S_IN[1] + 1, squares(3))
            for n, (sg, sd, k0, kn) in enumerate(groups1):
                pool_hidden(pool, sg, 1, k0, kn)
                last = n == len(groups1) - 1
                if last:
                    pool_sq_start(pool, 4)
                pool_stage(pool, sd, squares(4) if last else None)

        @block.vector
        def _(dve):
            chain = Chain(dve, sm["dve_chain"])
            for n, (which, c0, cn) in enumerate(((0, 0, VEC_A), (1, 0, 512), (1, 512, VEC_C - 512))):
                dve.wait_ge(sm["vec_done"], n + 1)
                if n == 0:
                    chain(dve.memset(vec_sb[0:8, 0, :], 0.0))
                dve.tensor_copy(vec_sb[0:8, which, c0:c0 + cn], PS[0:8, 7, 0:cn]).then_inc(sm["vec_copied"], 1)
            dve_h(dve, 0, 0, by_group, 0)
            dve_in_even(dve)
            dve.wait_ge(sm["evac_done"], bases[1] * NG)
            sync_all("dve", dve)
            rwkv_shift_dve(dve, chain)
            dve.wait_ge(sm["shifted"], 2 + NPB)
            rwkv_dve(dve, chain)
            sync_all("dve", dve)
            att_dve(dve, cfg_a, chain)
            sync_all("dve", dve)
            dve_concat(dve, 0, KT * NG)
            for g in range(NG):
                dve.wait_ge(x_loaded[g], 32)
            dve_residual(dve, 1)

            def ffn(layer, groups, norm, h):
                dve_h(dve, norm, h, by_group, h * KT * NG)
                dve_rstd(dve, norm)
                dve_first_rstd(dve, norm)
                for n, (sg, sd, k0, kn) in enumerate(groups):
                    dve_hidden(dve, sg, layer, k0, kn)
                    last = n == len(groups) - 1 and layer == 0
                    dve_residual(dve, sd, (lambda i: dve_h(dve, 2, 3, [(i, g) for g in range(NG)],
                                                           i * NG + 3 * KT * NG)) if last else None)

            ffn(0, groups0, 1, 2)
            dve_in_odd(dve)
            dve.wait_ge(sm["evac_done"], bases[S_IN[1] + 1] * NG)
            sync_all("dve", dve)
            dve.memset(u_buf[:, :, 0:TAPS - 1], 0.0).then_inc(sm["z_ready"], 1)
            dve.wait_ge(sm["z_ready"], 1)
            dve.wait_ge(sm["cstate_loaded"], 16)
            att_dve(dve, cfg_c, chain, conv_taps(chain, dve))
            sync_all("dve", dve)
            ln_dve(dve, chain)
            sync_all("dve", dve)
            dve_concat(dve, 1, 4 * KT * NG)
            for g in range(NG):
                dve.wait_ge(x_loaded[g], 48)
            dve_residual(dve, S_IN[1] + 1)
            ffn(1, groups1, 3, 5)
            dve_rstd(dve, 4)
            for g, (c0, cn) in enumerate(GROUPS):
                dve.wait_ge(sm["rstd_ready"], 4 * NG + g + 1)
                for i in range(KT):
                    dve.scalar_tensor_tensor(x[:, i, c0:c0 + cn], x[:, i, c0:c0 + cn], gains[:, 4, i:i + 1],
                                             rstd[:, c0:c0 + cn], ALU.mult, ALU.mult).then_inc(sm["y_ready"], 1)


def weight_tiles(w):
    k, m = w.shape
    return w.reshape(k // P, P, m // P, P).transpose(2, 1, 0, 3)


def feature_major(t):
    return t.T.reshape(t.shape[1] // P, P, t.shape[0]).transpose(1, 0, 2)


def shape_constants():
    i = np.arange(P)
    s, t = i[:, None], i[None, :]
    same = s // CHUNK == t // CHUNK
    before, upto = same & (s < t), same & (s <= t)
    c = {"ident": np.eye(P), "flip": np.eye(P)[::-1], "ones": np.ones((P, P)), "head_ones": s // HD == t // HD,
         "sa_mask": np.stack([before, upto, before, upto], 1)}

    def off_diagonal(b):
        return (s // (2 * b) == t // (2 * b)) & (s // b % 2 == 0) & (t // b % 2 == 1)
    c["level_mask"] = np.stack([off_diagonal(2 ** l) for l in range(1, LEVELS)], 1)
    c["x0_mask"] = np.stack([off_diagonal(1).T, off_diagonal(1)], 1)
    rel = np.arange(VEC_A) - 255
    nb = 16
    exact = nb // 2
    n = np.abs(rel)
    nf = np.maximum(n, exact).astype(np.float32)
    large = exact + (np.log(nf / exact) / np.log(128 / exact) * (nb - exact)).astype(np.int32)
    bucket = np.where(rel > 0, nb, 0) + np.where(n < exact, n, np.minimum(large, nb - 1))
    c["pick_a"] = i[:, None] == bucket[None, :]
    dist = np.clip(639 - np.arange(VEC_C), -128, 128) + 128
    c["pick_c"] = (np.arange(3 * P)[:, None] == dist[None, :]).reshape(3, P, VEC_C).transpose(1, 0, 2)
    return {k: np.ascontiguousarray(v, dtype=np.float32) for k, v in c.items()}


def rwkv_columns():
    r, wd, k, v, ad, gd = np.split(np.arange(1792), np.cumsum([512, 64, 512, 512, 64]))
    return np.concatenate([k, v, r, wd, ad, gd])


HEAD_ORDER = [0, 4, 1, 5, 2, 6, 3, 7]


def lay_out(a):
    f = {}
    cols = rwkv_columns()
    heads = np.concatenate([np.arange(h * HD, (h + 1) * HD) for h in HEAD_ORDER])
    f["x"] = feature_major(np.concatenate([a["x_prompt"][0], a["x_sample"][0]], 0))
    f["w_e"] = weight_tiles(a["w_in_e"][0][:, np.concatenate([768 + cols, np.arange(512, 768), heads])])
    f["w_oe"] = weight_tiles(a["w_out_e"][0][np.concatenate([heads, np.arange(512, 1024)])])
    i = np.arange(P)
    pairs = np.concatenate([np.concatenate([2048 + j * P + i, 1536 + j * P + i]) for j in range(4)])
    f["w_o"] = weight_tiles(a["w_in_o"][0][:, np.concatenate([np.arange(512, 1536), np.arange(512), pairs])])
    f["w_oo"] = weight_tiles(a["w_out_o"][0])
    for n in range(2):
        gu = np.stack([weight_tiles(a["ffn_w_gate"][n]), weight_tiles(a["ffn_w_up"][n])], 1)
        f[f"w_gu{n}"] = gu.reshape((2 * FT,) + gu.shape[2:])
        f[f"w_d{n}"] = weight_tiles(a["ffn_w_down"][n])
    g = [a["norm_mix_g"][0], a["norm_ffn_g"][0], a["norm_mix_g"][1], a["norm_ffn_g"][1], a["norm_final_g"]]
    f["gains"] = np.stack([v.reshape(KT, P).T for v in g], 1)
    f["mu"] = a["b_mu"][0][cols].reshape(NPB, P).T
    f["shift_in"] = a["state_b_shift"][0, 0][cols].reshape(NPB, P).T
    par = [a["b_w0"][0], a["b_a0"][0], a["b_kk"][0], a["b_ka"][0], a["b_rk"][0].reshape(-1), a["b_lnx_w"][0],
           a["b_lnx_b"][0]]
    par += [np.zeros_like(par[0])] * 2
    f["rw_par"] = np.stack([v.reshape(PAIRS, P).T for v in par], 2)
    par = list(a["d_dw_w"][0]) + [a["d_dw_b"][0], a["d_ln_g"][0], a["d_ln_b"][0]]
    f["conv_par"] = np.stack([v.reshape(4, P).T for v in par], 2)
    f["sink"] = np.broadcast_to(a["a_sink"][0][HEAD_ORDER], (P, 8))
    table = np.zeros((P, 8), np.float32)
    table[:32] = a["t5_table"][:, HEAD_ORDER]
    f["table_a"] = table
    table = np.zeros((3 * P, 8), np.float32)
    table[:257] = a["c_rel_table"][0].T
    f["table_c"] = table.reshape(3, P, 8).transpose(1, 0, 2)
    f["wa2"] = np.concatenate([a["b_w2"][0], a["b_a2"][0]], 0)
    f["g2"] = a["b_g2"][0]
    f["state_in"] = a["state_b_wkv"][0, 0].reshape(PAIRS, 2, HD, HD).transpose(1, 3, 0, 2).reshape(P, PAIRS, HD)
    f["a_kc"] = feature_major(a["cache_a_k"][0, 0].reshape(P, P))
    f["a_vc"] = a["cache_a_v"][0, 0].reshape(P, 1, P)
    f["c_kc"] = feature_major(a["cache_c_k"][0, 0].reshape(C_CACHE, 512))
    f["c_vc"] = a["cache_c_v"][0, 0].reshape(2, P, 512).transpose(1, 0, 2)
    f["conv_in"] = feature_major(a["state_d_conv"][0, 0])
    f.update(shape_constants())
    return f


OUTPUTS = {"out_y": (P, KT, NT), "out_akv": (P, 2, 192), "out_state": (P, 2, PAIRS, HD), "out_shift": (P, 2, NPB),
           "out_ckv": (P, 8, 576), "out_conv": (P, 4, 2, TAPS - 1)}


def kernel(**inputs):
    import concourse.bacc as bacc
    from concourse.bass_utils import run_bass_kernel_spmd

    nc = bacc.Bacc("TRN2", target_bir_lowering=False, num_devices=1)
    arrays, d = {}, {}
    for name, v in lay_out({k: np.asarray(v) for k, v in inputs.items()}).items():
        arrays[f"in_{name}"] = np.ascontiguousarray(v)
        d[name] = nc.dram_tensor(f"in_{name}", v.shape, F32, kind="ExternalInput").ap()
    for name, shape in OUTPUTS.items():
        d[name] = nc.dram_tensor(name, shape, F32, kind="ExternalOutput").ap()
    trunk(nc, d)
    r = run_bass_kernel_spmd(nc, [arrays], core_ids=[0]).results[0]

    def token_major(t):
        return t.transpose(2, 1, 0).reshape(t.shape[2], -1)

    y = token_major(r["out_y"])
    akv = [r["out_akv"][:, i].T.reshape(192, 2, HD) for i in range(2)]
    ckv = [token_major(r["out_ckv"][:, 4 * i:4 * i + 4]).reshape(576, 8, HD) for i in range(2)]
    wkv = r["out_state"].reshape(2, HD, 2, PAIRS, HD).transpose(2, 3, 0, 4, 1).reshape(2, 8, HD, HD)
    back = np.argsort(rwkv_columns())
    shift = [r["out_shift"][:, i].T.reshape(-1)[back] for i in range(2)]
    conv = [token_major(r["out_conv"][:, :, i]) for i in range(2)]
    return (y[None, :SEQ], y[None, SEQ:],
            akv[0][None, None, :P], akv[1][None, None, :P], wkv[0][None, None], shift[0][None, None],
            ckv[0][None, None, :512], ckv[1][None, None, :512], conv[0][None, None],
            akv[0][None, None, P:], akv[1][None, None, P:], wkv[1][None, None], shift[1][None, None],
            ckv[0][None, None, 512:], ckv[1][None, None, 512:], conv[1][None, None])
```

```python
from contextlib import ExitStack

import numpy as np

import concourse.bass as bass
from concourse import mybir

F32 = mybir.dt.float32
F32R = mybir.dt.float32r
ACT = mybir.ActivationFunctionType
ALU = mybir.AluOpType
AX = mybir.AxisListType.X
ds = bass.ds

P = 128
D = 1024
KT = D // P
SEQ = 1024
DEC = 64
NT = SEQ + DEC
CHUNK = 64
HD = 64
PAIRS = 4
GROUPS = [(0, 384), (384, 384), (768, 320)]
NG = len(GROUPS)
DFF = 2816
FT = DFF // P
HID = 6
FFN_GROUPS = [(0, FT % HID)] + [(k, HID) for k in range(FT % HID, FT, HID)]
NPB = 14
PBW = 1 + SEQ + 1 + DEC
W1 = PBW - 1
G3 = W1 // 3
WP = W1 - DEC + P
BLOCKS = 9
WAVE = 3
LEVELS = 6
C_CACHE = 256
NEG = -1e30
RMS_EPS = 1e-6
LNX_EPS = 64e-5
LN_EPS = 1e-5
DECAY = float(np.exp(-0.5))
TAPS = 31
POOL_TAPS = 8
N_CONST = 15 * 16
UW = 2 * (TAPS - 1) + NT
ZW = UW - (TAPS - 1)
VEC_A, VEC_C = 384, 768


def repeat(eng, start, end, body):
    if end - start <= 1:
        for i in range(start, end):
            body(i)
    else:
        with eng.Fori(start, end) as i:
            body(i)


class Chain:

    def __init__(self, eng, sem):
        self.eng, self.sem, self.n, self.extra = eng, sem, 0, 0

    def step(self, ins):
        ins.then_inc(self.sem, 1)
        self.n += 1
        return self.n

    def wait(self, n):
        self.eng.wait_ge(self.sem, self.extra + n)

    def __call__(self, ins):
        self.wait(self.step(ins))

    def loop(self, start, end, per, body):
        if end - start <= 1:
            for i in range(start, end):
                body(i)
            return
        first = self.n
        with self.eng.Fori(start, end) as i:
            self.extra = (i - start) * per
            body(i)
        assert self.n - first == per, (self.n - first, per)
        self.extra = 0
        self.n = first + per * (end - start)


def trunk(nc, d):
    ctx = ExitStack()
    with ctx:
        def at(name, shape, offset, dt=F32):
            return nc.alloc_sbuf_tensor_at(name, shape, dt, offset=offset, align_bytes=4)

        def sem(name):
            return ctx.enter_context(nc.semaphore(name))

        tok = 4 * NT
        H0 = 16512
        TMP0 = H0 + 2 * KT * tok
        tmp_bytes = 2 * tok + 4 * 384 * (3 + 2 + 2)
        BIG0 = TMP0 + tmp_bytes
        big_bytes = 12 * tok + 4 * 4 * UW + 4 * tok
        WR0 = BIG0 + big_bytes
        CO0 = WR0 + 6 * 4 * D
        h_hi = at("h_hi", [P, KT, NT], H0, F32R)
        h_lo = at("h_lo", [P, KT, NT], H0 + KT * tok, F32R)
        sumsq = at("sumsq", [P, NT], TMP0)
        rstd = at("rstd", [P, NT], TMP0 + tok)
        o = TMP0 + 2 * tok
        gate_t = at("gate_t", [P, NG, 384], o)
        up_t = at("up_t", [P, 2, 384], o + 4608)
        hid_t = at("hid_t", [P, 2, 384], o + 7680)
        shift_t = at("shift_t", [P, 2, W1], o)
        sq_t = gate_t
        x = at("x", [P, KT, NT], BIG0)
        hid0 = BIG0 + 8 * 4 * PBW
        hid_hi = at("hid_hi", [P, HID, NT], hid0, F32R)
        hid_lo = at("hid_lo", [P, HID, NT], hid0 + HID * tok, F32R)
        pb = at("pb", [P, NPB, PBW], BIG0)
        akvq = at("akvq", [P, 6, NT], BIG0 + NPB * 4 * PBW)
        cproj = at("cproj", [P, 12, NT], BIG0)
        u_buf = at("u_buf", [P, 4, UW], BIG0 + 12 * tok)
        z_buf = at("z_buf", [P, 4, NT], BIG0 + 12 * tok + 16 * UW)
        w_raw = [at(f"w_raw{s}", [P, KT, P], WR0 + s * 4 * D) for s in range(2)]
        w_hi = [at(f"w_hi{s}", [P, KT, P], WR0 + (2 + s) * 4 * D, F32R) for s in range(2)]
        w_lo = [at(f"w_lo{s}", [P, KT, P], WR0 + (4 + s) * 4 * D, F32R) for s in range(2)]
        cursor = [CO0]

        def whole(t):
            return t[tuple(slice(None) for _ in t.shape)]

        def const(name, shape):
            t = at(name, shape, cursor[0])
            cursor[0] += 4 * int(np.prod(shape[1:]))
            return t

        ident = const("ident", [P, P])
        flip = const("flip", [P, P])
        ones = const("ones", [P, P])
        head_ones = const("head_ones", [P, P])
        sa_mask = const("sa_mask", [P, 4, P])
        level_mask = const("level_mask", [P, LEVELS - 1, P])
        gains = const("gains", [P, 5, KT])
        mu = const("mu", [P, NPB])
        shift_in = const("shift_in", [P, NPB])
        shift_out = const("shift_out", [P, 2, NPB])
        rw_par = const("rw_par", [P, PAIRS, 9])
        rc = const("rc", [P, 9])
        rc_end = const("rc_end", [P, 9])
        conv_par = const("conv_par", [P, 4, TAPS + 3])
        cc = const("cc", [P, TAPS + 3])
        sink = const("sink", [P, 8])
        neg_sink = const("neg_sink", [P, 8])
        assert cursor[0] <= nc.sbuf_usable_end, (cursor[0], nc.sbuf_usable_end)

        cursor[0] = H0
        at_rt = const("at_rt", [P, 2, WP])
        kt_ = const("kt_", [P, WP])
        bt_ = const("bt_", [P, WP])
        bonus = const("bonus", [P, WP])
        v_cur = const("v_cur", [P, WP])
        pair0 = cursor[0]
        pinv = const("pinv", [P, WP])
        kk_ = const("kk_", [P, WP])
        xx = at("xx", [P, 2, 2, WAVE, P], pair0)
        y_sb = at("y_sb", [P, 2, WAVE, P], pair0 + 6144)
        sa = const("sa", [P, 2, WAVE, 4, P])
        y_mid = at("y_mid", [P, W1], cursor[0] - 4 * 2 * WAVE * 4 * P)
        y_var = at("y_var", [P, W1], cursor[0] - 4 * 2 * WAVE * 4 * P + 4 * W1)
        bt_level = const("bt_level", [P, 2, WAVE, P])
        tm = const("tm", [P, WAVE, 4, P])
        akv = const("akv", [P, 2, WAVE, HD])
        wz = const("wz", [P, 2, WAVE, 2, HD])
        r_eff = const("r_eff", [P, WAVE, P])
        m_bd = const("m_bd", [P, 2 * WAVE, P])
        h_bd = const("h_bd", [P, 2 * WAVE, P])
        s_bd = const("s_bd", [P, 2 * WAVE + 1, P])
        bk_hat = const("bk_hat", [P, 2, WAVE * P])
        decay_end = const("decay_end", [P, 2 * BLOCKS])
        wa2 = const("wa2", [P, PAIRS * P])
        g2 = const("g2", [P, PAIRS * P])
        wa2_cur = const("wa2_cur", [P, P])
        g2_cur = const("g2_cur", [P, P])
        x0_mask = const("x0_mask", [P, 2, P])
        state_in = const("state_in", [P, PAIRS, HD])
        state_out = const("state_out", [P, 2, PAIRS, HD])
        assert cursor[0] <= BIG0 , (cursor[0], BIG0)

        def attention_memory(tag, nb, cache_blocks, v_width, heads_k, slots):
            cursor[0] = H0
            m = {}
            for name, shape in [("bias", [P, 8, nb * P]), ("hankel", [P, 8, nb * P]), ("qz", [P, 2, BLOCKS * P]),
                                ("vf", [P, BLOCKS * P]), ("vt", [P, BLOCKS, P]), ("vcc", [P, cache_blocks, P]),
                                ("k_cache", [P, heads_k, cache_blocks * P]), ("v_cache", [P, cache_blocks, v_width]),
                                ("s", [P, slots, nb * P]), ("pt", [P, 2, nb, P]), ("stat", [P, slots, 4]),
                                ("zc", [P, ZW])]:
                m[name] = const(f"{tag}_{name}", shape)
            assert cursor[0] <= BIG0, (cursor[0], BIG0)
            return m

        mem_a = attention_memory("a", 2, 1, P, 1, 6)
        mem_c = attention_memory("c", 5, 2, 4 * P, 4, 3)
        zc_pool = at("zc_pool", [P, ZW], H0 + 4 * 8 * 5 * P)
        tap_pool = at("tap_pool", [P, ZW], H0 + 4 * 8 * 5 * P + 4 * ZW)
        ln_t = at("ln_t", [P, 4, NT], H0)
        ln_r = at("ln_r", [P, NT], H0 + 4 * tok)
        cursor[0] = hid0
        pick_a = const("pick_a", [P, VEC_A])
        pick_c = const("pick_c", [P, 3, VEC_C])
        table_a = const("table_a", [P, 8])
        table_c = const("table_c", [P, 3, 8])
        vec_sb = const("vec_sb", [P, 2, VEC_C])

        PS = ctx.enter_context(nc.psum_tensor("PS", [P, 8, 512], F32))
        x_home = nc.dram_tensor("x_home", (P, KT, NT), F32, kind="Internal").ap()
        vec_home = nc.dram_tensor("vec_home", (2, 8, VEC_C), F32, kind="Internal")

        names = """first_sums gains_loaded consts_loaded w_loaded0 w_loaded1 w_hi_ready w_lo_ready product_done evac_done
            h_hi_ready h_lo_ready sq_done sum_done stat_done stat_read ms_ready rstd_ready gate_ready
            u_ready hid_ready hid_hi_ready hid_lo_ready dve_chain pool_chain barrier stored x_saved y_ready
            vec_done vec_copied vec_stored
            rw_loaded squashed r_staged low_done sg_ready cum_ready exp_ready ksq_ready
            ss_done ss_read log_ready root_ready end_staged var_read rk_ready bonus_done hat_ready tm_done tm_ready ab_done sa_ready
            x_init x_init1 bt1_ready bt_ready y_done ysb_ready xprod_done xadd akv_done akv_ready wz_done wz_ready reff_done
            r_ready mh_done mdiag_ready hbd_ready mbd_ready s_init s_done s_new yb_done y_stored mean_done
            yc_ready var_done vroot_ready zg_done gated state_ready
            hk_loaded hk_done bias_ready q_staged v_staged vtr_done vt_ready sc_done st_done max_ready exp_done
            p_ready pt_done pt_ev pv_done o_ev z_ready zc_pool_ready
            conv_staged cstate_loaded lnm_done lnc_ready lnv_done lnr_ready lnq_ready lnz_ready silu_ready""".split()
        sm = {n: sem(n) for n in names}
        w_loaded = [sm["w_loaded0"], sm["w_loaded1"]]
        x_loaded = [sem(f"x_loaded{g}") for g in range(NG)]
        stages = [("w_e", 20, KT, 0), ("w_oe", 8, KT, 0)]
        for k0, kn in FFN_GROUPS:
            stages += [("w_gu0", 2 * kn, KT, 2 * k0), ("w_d0", 8, kn, k0)]
        stages += [("w_o", 20, KT, 0), ("w_oo", 8, KT, 0)]
        for k0, kn in FFN_GROUPS:
            stages += [("w_gu1", 2 * kn, KT, 2 * k0), ("w_d1", 8, kn, k0)]
        bases = list(np.cumsum([0] + [s[1] for s in stages]))
        tiles_k = [s[2] for s in stages for _ in range(s[1])]
        n_tiles = int(bases[-1])
        bases = [int(b) for b in bases]
        S_IN = [0, 2 + 2 * len(FFN_GROUPS)]

        def stage_groups(layer):
            first = S_IN[layer] + 2
            return [(first + 2 * i, first + 2 * i + 1, k0, kn) for i, (k0, kn) in enumerate(FFN_GROUPS)]

        bars = {"pe": 0, "act": 0, "dve": 0, "pool": 0}

        def sync_all(who, eng):
            bars[who] += 1
            eng.drain().then_inc(sm["barrier"], 1)
            eng.wait_ge(sm["barrier"], 4 * bars[who])

        def pe_tile(pe, n, slot, kn, hi, lo, before=None):
            pe.wait_ge(sm["w_hi_ready"], n + 1)
            pe.wait_ge(sm["w_lo_ready"], n + 1)
            for g, (c0, cn) in enumerate(GROUPS):
                if not (isinstance(n, int) and n < 2):
                    pe.wait_ge(sm["evac_done"], n * NG + (g + 1 - 2 * NG))
                if before:
                    before(g)
                out = PS[:, NG * slot + g, 0:cn]
                for k in range(kn):
                    w_h, w_l = w_hi[slot][:, k, :], w_lo[slot][:, k, :]
                    a_h, a_l = hi[:, k, c0:c0 + cn], lo[:, k, c0:c0 + cn]
                    pe.matmul(out, w_h, a_h, start=k == 0, stop=False)
                    pe.matmul(out, w_h, a_l, start=False, stop=False)
                    last = pe.matmul(out, w_l, a_h, start=False, stop=k == kn - 1)
                last.then_inc(sm["product_done"], 1)

        def pe_stage(pe, s, hi, lo, before=None, norm=None, between=None):
            _, count, kn, _ = stages[s]
            base = bases[s]
            pe_tile(pe, base, 0, kn, hi, lo, before)
            if between:
                between()
            if norm is not None:
                pe_stats(pe, norm)
            pe_tile(pe, base + 1, 1, kn, hi, lo)

            def pair(j):
                for slot in range(2):
                    pe_tile(pe, 2 * j + (base + slot), slot, kn, hi, lo)
            repeat(pe, 1, count // 2, pair)

        def pe_stats(pe, norm):
            for g, (c0, cn) in enumerate(GROUPS):
                n = norm * NG + g
                pe.wait_ge(sm["sum_done"], 3 * (norm + 1) + (norm + 1) * KT * NG)
                if n >= 2:
                    pe.wait_ge(sm["stat_read"], n - 1)
                if norm == 0:
                    pe.wait_ge(sm["first_sums"], 1)
                    pe.matmul(PS[:, 6 + n % 2, 0:cn], ones[:, :], rstd[:, c0:c0 + cn], start=True, stop=False)
                pe.matmul(PS[:, 6 + n % 2, 0:cn], ones[:, :], sumsq[:, c0:c0 + cn],
                          start=norm > 0, stop=True).then_inc(sm["stat_done"], 1)

        def h_tiles_first(pe, h):
            return lambda g: pe.wait_ge(sm["h_lo_ready"], h * KT * NG + (KT - 1) * NG + g + 1)

        def h_groups_first(pe, h):
            return lambda g: pe.wait_ge(sm["h_lo_ready"], h * KT * NG + KT * (g + 1))

        def hidden_ready(pe, layer, k0, kn):
            return lambda g: pe.wait_ge(sm["hid_lo_ready"], NG * (layer * FT + k0 + kn - 1) + g + 1)

        def sp_tile(sp, s, slot, i):
            name, _, kn, first = stages[s]
            n = i + bases[s]
            if not (isinstance(n, int) and n < 2):
                sp.wait_ge(sm["w_lo_ready"], n - 1)
            src = d[name][i + first, :, :, :] if not name.startswith("w_d") else d[name][i, :, first:first + kn, :]
            sp.dma_start(w_raw[slot][:, 0:kn, :], src).then_inc(w_loaded[slot], 16)

        def sp_first(sp, s):
            if s < len(stages):
                sp_tile(sp, s, 0, 0)
                sp_tile(sp, s, 1, 1)

        def sp_rest(sp, s):
            def pair(j):
                for slot in range(2):
                    sp_tile(sp, s, slot, 2 * j + slot)
            repeat(sp, 1, stages[s][1] // 2, pair)

        def act_hi(act, j, slot, base, kn):
            act.wait_ge(w_loaded[slot], j * 16 + (base // 2 + 1) * 16)
            if not (isinstance(j, int) and base + 2 * j < 2):
                act.wait_ge(sm["product_done"], j * (2 * NG) + (base + slot - 1) * NG)
            act.activation(w_hi[slot][:, 0:kn, :], w_raw[slot][:, 0:kn, :], ACT.Copy).then_inc(sm["w_hi_ready"], 1)

        def act_stage(act, s, work=None):
            _, count, kn, _ = stages[s]

            def pair(j):
                for slot in range(2):
                    if work:
                        work(j, slot)
                    act_hi(act, j, slot, bases[s] + 2, kn)
            repeat(act, 0, count // 2 - 1, pair)
            for slot in range(2):
                if work:
                    work(count // 2 - 1, slot)
                n = bases[s + 1] + slot
                if n < n_tiles:
                    act_hi(act, 0, slot, bases[s + 1], tiles_k[n])

        def pool_lo(pool, n, slot, kn):
            pool.wait_ge(sm["w_hi_ready"], n + 1)
            pool.tensor_tensor(w_lo[slot][:, 0:kn, :], w_raw[slot][:, 0:kn, :],
                               w_hi[slot][:, 0:kn, :].bitcast(F32), ALU.subtract).then_inc(sm["w_lo_ready"], 1)

        def pool_stage(pool, s, work=None):
            _, count, kn, _ = stages[s]
            base = bases[s]

            def pair(j):
                for slot in range(2):
                    if work:
                        work(j, slot)
                    pool_lo(pool, 2 * j + (base + 2 + slot), slot, kn)
            repeat(pool, 0, count // 2 - 1, pair)
            for slot in range(2):
                if work:
                    work(count // 2 - 1, slot)
                n = bases[s + 1] + slot
                if n < n_tiles:
                    pool_lo(pool, n, slot, tiles_k[n])

        groups0, groups1 = stage_groups(0), stage_groups(1)
        x_from = [None, bases[1], bases[groups0[-1][1]], bases[S_IN[1] + 1], bases[groups1[-1][1]]]

        def wait_x(eng, norm, i, g):
            if norm == 0:
                eng.wait_ge(x_loaded[g], 16)
            else:
                eng.wait_ge(sm["evac_done"], i * NG + (x_from[norm] * NG + g + 1))

        def act_h(act, norm, h, order):
            for i, g in order:
                c0, cn = GROUPS[g]
                wait_x(act, norm, i, g)
                act.activation(h_hi[:, ds(i, 1), c0:c0 + cn], x[:, ds(i, 1), c0:c0 + cn], ACT.Copy,
                               scale=gains[:, norm, ds(i, 1)]).then_inc(sm["h_hi_ready"], 1)

        def dve_h(dve, norm, h, order, first):
            for n, (i, g) in enumerate(order):
                c0, cn = GROUPS[g]
                dve.wait_ge(sm["h_hi_ready"], first + (n + 1))
                dve.scalar_tensor_tensor(h_lo[:, ds(i, 1), c0:c0 + cn], x[:, ds(i, 1), c0:c0 + cn],
                                         gains[:, norm, ds(i, 1)],
                                         h_hi[:, ds(i, 1), c0:c0 + cn].bitcast(F32),
                                         ALU.mult, ALU.subtract).then_inc(sm["h_lo_ready"], 1)

        by_group = [(i, g) for g in range(NG) for i in range(KT)]

        def pool_sq_start(pool, norm):
            if norm:
                pool.wait_ge(sm["stat_done"], norm * NG)
            pool.memset(sumsq[:, :], 0.0).then_inc(sm["sum_done"], 3)

        def pool_sq(pool, norm, i, count=1):
            for g, (c0, cn) in enumerate(GROUPS):
                done = 3 * (norm + 1) + norm * KT * NG + g
                wait_x(pool, norm, i, g)
                pool.wait_ge(sm["sum_done"], i * NG + (done - 2))
                pool.tensor_tensor(sq_t[:, g, 0:cn], x[:, ds(i, 1), c0:c0 + cn], x[:, ds(i, 1), c0:c0 + cn],
                                   ALU.mult).then_inc(sm["sq_done"], count)
                pool.wait_ge(sm["sq_done"], i * NG + (norm * KT * NG + (g + 1) * count))
                pool.tensor_tensor(sumsq[:, c0:c0 + cn], sumsq[:, c0:c0 + cn], sq_t[:, g, 0:cn],
                                   ALU.add).then_inc(sm["sum_done"], count)

        POOL_SQ = 3

        def dve_first_squares(dve, chain):
            for g, (c0, cn) in enumerate(GROUPS):
                dve.tensor_tensor(rstd[:, c0:c0 + cn], x[:, POOL_SQ, c0:c0 + cn], x[:, POOL_SQ, c0:c0 + cn], ALU.mult)
                n = []
                for i in range(POOL_SQ + 1, KT):
                    t = hid_t[:, i % 2, 0:cn]
                    if len(n) >= 2:
                        chain.wait(n[-2])
                    k = chain.step(dve.tensor_tensor(t, x[:, i, c0:c0 + cn], x[:, i, c0:c0 + cn], ALU.mult))
                    chain.wait(k)
                    n.append(chain.step(dve.tensor_tensor(rstd[:, c0:c0 + cn], rstd[:, c0:c0 + cn], t, ALU.add)))
                chain.wait(n[-1])
            dve.tensor_copy(up_t[:, 0, 0:1], rstd[:, 0:1]).then_inc(sm["first_sums"], 1)

        def dve_rstd(dve, norm):
            for g, (c0, cn) in enumerate(GROUPS):
                n = norm * NG + g
                dve.wait_ge(sm["stat_done"], n + 1)
                dve.tensor_scalar(rstd[:, c0:c0 + cn], PS[:, 6 + n % 2, 0:cn], 1.0 / D, RMS_EPS,
                                  ALU.mult, ALU.add).then_inc(sm["stat_read"], 1)

        def act_rstd(act, norm):
            for g, (c0, cn) in enumerate(GROUPS):
                act.wait_ge(sm["stat_read"], norm * NG + g + 1)
                act.activation(rstd[:, c0:c0 + cn], rstd[:, c0:c0 + cn], ACT.Ln).then_inc(sm["ms_ready"], 1)
            for g, (c0, cn) in enumerate(GROUPS):
                act.wait_ge(sm["ms_ready"], norm * NG + g + 1)
                act.activation(rstd[:, c0:c0 + cn], rstd[:, c0:c0 + cn], ACT.Exp, scale=-0.5)\
                   .then_inc(sm["rstd_ready"], 1)

        def dve_scaled(dve, n, slot, g, out, signal=True):
            c0, cn = GROUPS[g]
            dve.wait_ge(sm["product_done"], n * NG + (g + 1))
            ins = dve.tensor_tensor(out, PS[:, NG * slot + g, 0:cn], rstd[:, c0:c0 + cn], ALU.mult)
            if signal:
                ins.then_inc(sm["evac_done"], 1)

        PC = SEQ - GROUPS[-1][0]

        def dve_scaled_split(dve, n, slot, out_prompt, out_sample):
            c0, cn = GROUPS[-1]
            dve.wait_ge(sm["product_done"], n * NG + NG)
            dve.tensor_tensor(out_prompt, PS[:, NG * slot + NG - 1, 0:PC], rstd[:, c0:c0 + PC], ALU.mult)
            dve.tensor_tensor(out_sample, PS[:, NG * slot + NG - 1, PC:cn], rstd[:, c0 + PC:NT], ALU.mult)\
               .then_inc(sm["evac_done"], 1)

        def dve_first_rstd(dve, norm):
            dve.wait_ge(sm["rstd_ready"], (norm + 1) * NG)

        def dve_in_even(dve, chain):
            dve_rstd(dve, 0)
            dve_first_rstd(dve, 0)
            dve.wait_ge(sm["vec_stored"], 16)

            def rwkv_tiles(j):
                for slot in range(2):
                    i = 2 * j + slot
                    for g in range(NG - 1):
                        c0, cn = GROUPS[g]
                        dve_scaled(dve, i + bases[0], slot, g, pb[:, ds(i, 1), 1 + c0:1 + c0 + cn])
                    c0 = GROUPS[-1][0]
                    dve_scaled_split(dve, i + bases[0], slot, pb[:, ds(i, 1), 1 + c0:1 + SEQ],
                                     pb[:, ds(i, 1), 2 + SEQ:PBW])

            repeat(dve, 0, NPB // 2, rwkv_tiles)
            dve.wait_ge(sm["evac_done"], NPB * NG)
            dve.memset(pb[:, :, 0:1], 0.0)
            chain(dve.tensor_copy(pb[:, :, 1 + SEQ:2 + SEQ], shift_in[:, :].unsqueeze(2)))
            dve.tensor_copy(shift_out[:, 0, :].unsqueeze(2), pb[:, :, SEQ:SEQ + 1])
            chain(dve.tensor_copy(shift_out[:, 1, :].unsqueeze(2), pb[:, :, PBW - 1:PBW]))
            shifted = []
            for i in range(6):
                for g, (c0, cn) in enumerate(GROUPS):
                    dve_scaled(dve, i + (bases[0] + NPB), i % 2, g, akvq[:, i, c0:c0 + cn])
                for t in range(NPB * i // 6, NPB * (i + 1) // 6):
                    if t >= 2:
                        chain.wait(shifted[t - 2])
                    chain(dve.tensor_tensor(shift_t[:, t % 2, :], pb[:, t, 0:W1], pb[:, t, 1:PBW], ALU.subtract))
                    ins = dve.scalar_tensor_tensor(pb[:, t, 1:PBW], shift_t[:, t % 2, :], mu[:, t:t + 1],
                                                   pb[:, t, 1:PBW], ALU.mult, ALU.add)
                    shifted.append(chain.step(ins))
            chain.wait(shifted[-1])

        def dve_in_odd(dve):
            s = S_IN[1]
            dve_rstd(dve, 2)
            dve_first_rstd(dve, 2)
            dve.wait_ge(sm["x_saved"], 16)

            def attention_tiles(j):
                for slot in range(2):
                    i = 2 * j + slot
                    for g, (c0, cn) in enumerate(GROUPS):
                        dve_scaled(dve, i + bases[s], slot, g, cproj[:, ds(i, 1), c0:c0 + cn])
            repeat(dve, 0, 6, attention_tiles)

            def conv_tiles(j):
                n = 2 * j + (bases[s] + 12)
                if not isinstance(j, int):
                    dve.wait_ge(sm["u_ready"], j * NG)
                for g, (c0, cn) in enumerate(GROUPS):
                    dve_scaled(dve, n, 0, g, gate_t[:, g, 0:cn])
                for g, (c0, cn) in enumerate(GROUPS):
                    if g == 2:
                        dve.wait_ge(sm["u_ready"], j * NG + 1)
                    dve_scaled(dve, n + 1, 1, g, up_t[:, g % 2, 0:cn])
                    dve.wait_ge(sm["evac_done"], n * NG + (NG + g + 1))
                    dve.wait_ge(sm["gate_ready"], j * NG + (FT * NG + g + 1))
                    if g < NG - 1:
                        dve.tensor_tensor(u_buf[:, ds(j, 1), TAPS - 1 + c0:TAPS - 1 + c0 + cn],
                                          up_t[:, g % 2, 0:cn], gate_t[:, g, 0:cn], ALU.mult)\
                           .then_inc(sm["u_ready"], 1)
                    else:
                        dve.tensor_tensor(u_buf[:, ds(j, 1), TAPS - 1 + c0:TAPS - 1 + SEQ],
                                          up_t[:, g % 2, 0:PC], gate_t[:, g, 0:PC], ALU.mult)
                        dve.tensor_tensor(u_buf[:, ds(j, 1), 2 * (TAPS - 1) + SEQ:UW],
                                          up_t[:, g % 2, PC:cn], gate_t[:, g, PC:cn], ALU.mult)\
                           .then_inc(sm["u_ready"], 1)
            conv_tiles(0)
            repeat(dve, 1, 4, conv_tiles)

        def gate_first(layer):
            return layer * (FT * NG + 4 * NG)

        def act_gate(act, func, base):
            def work(j, slot):
                if slot:
                    return
                for g, (c0, cn) in enumerate(GROUPS):
                    act.wait_ge(sm["evac_done"], j * (2 * NG) + (base * NG + g + 1))
                    act.activation(gate_t[:, g, 0:cn], gate_t[:, g, 0:cn], func).then_inc(sm["gate_ready"], 1)
            return work

        def dve_hidden(dve, s, layer, k0, kn):
            def tile(j):
                n = 2 * j + bases[s]
                v0 = NG * (layer * FT + k0)
                if v0 or not isinstance(j, int):
                    dve.wait_ge(sm["hid_ready"], j * NG + v0)
                for g, (c0, cn) in enumerate(GROUPS):
                    dve_scaled(dve, n, 0, g, gate_t[:, g, 0:cn])
                for g, (c0, cn) in enumerate(GROUPS):
                    if g == 2:
                        dve.wait_ge(sm["hid_ready"], j * NG + (v0 + 1))
                    dve_scaled(dve, n + 1, 1, g, up_t[:, g % 2, 0:cn])
                    dve.wait_ge(sm["evac_done"], n * NG + (NG + g + 1))
                    dve.wait_ge(sm["gate_ready"], j * NG + (gate_first(layer) + k0 * NG + g + 1))
                    if not (isinstance(j, int) and v0 + g < 2):
                        dve.wait_ge(sm["hid_lo_ready"], j * NG + (v0 + g - 1))
                    dve.tensor_tensor(hid_t[:, g % 2, 0:cn], up_t[:, g % 2, 0:cn], gate_t[:, g, 0:cn],
                                      ALU.mult).then_inc(sm["hid_ready"], 1)
            tile(0)
            repeat(dve, 1, kn, tile)

        def act_hidden(act, s, layer, k0, kn):
            gate = act_gate(act, ACT.Silu, bases[s])

            def work(j, slot):
                gate(j, slot)
                if not slot:
                    return
                for g, (c0, cn) in enumerate(GROUPS):
                    act.wait_ge(sm["hid_ready"], j * NG + (NG * (layer * FT + k0) + g + 1))
                    act.activation(hid_hi[:, ds(j, 1), c0:c0 + cn], hid_t[:, g % 2, 0:cn], ACT.Copy)\
                       .then_inc(sm["hid_hi_ready"], 1)
            act_stage(act, s, work)

        def pool_hidden(pool, s, layer, k0, kn):
            def work(j, slot):
                if not slot:
                    return
                for g, (c0, cn) in enumerate(GROUPS):
                    pool.wait_ge(sm["hid_hi_ready"], j * NG + (NG * (layer * FT + k0) + g + 1))
                    pool.tensor_tensor(hid_lo[:, ds(j, 1), c0:c0 + cn], hid_t[:, g % 2, 0:cn],
                                       hid_hi[:, ds(j, 1), c0:c0 + cn].bitcast(F32),
                                       ALU.subtract).then_inc(sm["hid_lo_ready"], 1)
            pool_stage(pool, s, work)

        def dve_residual(dve, s, after=None):
            def pair(j):
                for slot in range(2):
                    i = 2 * j + slot
                    for g, (c0, cn) in enumerate(GROUPS):
                        dve.wait_ge(sm["product_done"], i * NG + (bases[s] * NG + g + 1))
                        dve.tensor_tensor(x[:, ds(i, 1), c0:c0 + cn], PS[:, NG * slot + g, 0:cn],
                                          x[:, ds(i, 1), c0:c0 + cn], ALU.add).then_inc(sm["evac_done"], 1)
                    if after:
                        after(i)
            repeat(dve, 0, KT // 2, pair)

        def concat_source(layer, i, g):
            c0, cn = GROUPS[g]
            if i >= 4 and layer == 0:
                t = pb[:, 4 + i, :]
                if g < NG - 1:
                    return [((c0, c0 + cn), t[:, 1 + c0:1 + c0 + cn])]
                return [((c0, SEQ), t[:, 1 + c0:1 + SEQ]), ((SEQ, NT), t[:, 2 + SEQ:PBW])]
            t = z_buf[:, i - 4, :] if i >= 4 else akvq[:, 2 + i, :] if layer == 0 else cproj[:, 8 + i, :]
            return [((c0, c0 + cn), t[:, c0:c0 + cn])]

        def act_concat(act, layer):
            for i, g in by_group:
                for (a, b), src in concat_source(layer, i, g):
                    ins = act.activation(h_hi[:, i, a:b], src, ACT.Copy)
                ins.then_inc(sm["h_hi_ready"], 1)

        def dve_concat(dve, layer, first):
            for n, (i, g) in enumerate(by_group):
                dve.wait_ge(sm["h_hi_ready"], first + n + 1)
                for (a, b), src in concat_source(layer, i, g):
                    ins = dve.tensor_tensor(h_lo[:, i, a:b], src, h_hi[:, i, a:b].bitcast(F32), ALU.subtract)
                ins.then_inc(sm["h_lo_ready"], 1)

        def block_cols(b):
            return b * P if b < BLOCKS - 1 else W1 - DEC

        def thirds(t):
            return t.rearrange("p (g c) -> p g c", g=3)

        def wave_runs(w):
            return [(0, WAVE, WAVE * w * P)] if w < 2 else [(0, WAVE - 1, WAVE * w * P), (WAVE - 1, 1, W1 - DEC)]

        halves = [slice(0, HD), slice(HD, P)]

        def over_pairs(loop, between, waves):
            between(0, None)

            def pair(m):
                waves(m)
                between(m + 1, m)
            loop(0, PAIRS - 1, pair)
            waves(PAIRS - 1)
            between(None, PAIRS - 1)

        def rwkv_act(act):
            act.activation(pb[0:HD, 12, 1:PBW], pb[0:HD, 12, 1:PBW], ACT.Tanh).then_inc(sm["squashed"], 1)
            act.activation(pb[:, 13, 1:PBW], pb[:, 13, 1:PBW], ACT.Sigmoid).then_inc(sm["squashed"], 1)

            def between(p, f):
                if p is not None:
                    act.wait_ge(sm["low_done"], 2 * p + 1)
                    act.activation(thirds(bonus[:, 0:W1]), PS[:, 3:6, 0:G3], ACT.Sigmoid, bias=rc[:, 1:2])\
                       .then_inc(sm["sg_ready"], 1)
                    act.wait_ge(sm["low_done"], 2 * p + 2)
                    act.activation(thirds(at_rt[:, 0, 0:W1]), PS[:, 0:3, 0:G3], ACT.Sigmoid, bias=rc[:, 0:1])\
                       .then_inc(sm["sg_ready"], 1)
                    act.wait_ge(sm["cum_ready"], p + 1)
                    act.activation(at_rt[:, 1, 0:W1], kt_[:, 0:W1], ACT.Exp, scale=-DECAY).then_inc(sm["exp_ready"], 1)
                    act.activation(pinv[:, 0:W1], kt_[:, 0:W1], ACT.Exp, scale=DECAY).then_inc(sm["exp_ready"], 1)
                    act.activation(at_rt[:, 0, 0:W1], at_rt[:, 0, 0:W1], ACT.Exp, scale=-DECAY)\
                       .then_inc(sm["exp_ready"], 1)
                if f is not None:
                    act.wait_ge(sm["var_read"], f + 1)
                    act.activation(y_var[:, :], y_var[:, :], ACT.Ln).then_inc(sm["log_ready"], 1)
                    act.wait_ge(sm["log_ready"], (p if p is not None else PAIRS) + f + 1)
                    act.activation(y_var[:, :], y_var[:, :], ACT.Exp, scale=-0.5).then_inc(sm["vroot_ready"], 1)
                if p is not None:
                    act.wait_ge(sm["ss_read"], p + 1)
                    act.activation(kt_[:, 0:W1], kt_[:, 0:W1], ACT.Ln).then_inc(sm["log_ready"], 1)
                    act.wait_ge(sm["log_ready"], 1 if f is None else p + f + 2)
                    act.activation(kt_[:, 0:W1], kt_[:, 0:W1], ACT.Exp, scale=-0.5).then_inc(sm["root_ready"], 1)

            def token_major(q):
                for blk in range(WAVE):
                    act.wait_ge(sm["tm_done"], 3 * q + (blk + 1))
                    act.activation(tm[:, blk, :, :], PS[:, blk, :].rearrange("p (a b) -> p a b", a=4),
                                   ACT.Copy).then_inc(sm["tm_ready"], 1)

            def waves(m):
                for w in range(3):
                    q = 3 * m + w
                    if w == 0:
                        token_major(q)
                    act.wait_ge(sm["akv_done"], q + 1)
                    act.activation(akv[:, :, :, :].rearrange("p h b c -> p (h b c)"), PS[:, 6, 0:6 * HD],
                                   ACT.Copy).then_inc(sm["akv_ready"], 1)
                    for l in range(LEVELS - 1):
                        for h in range(2):
                            act.wait_ge(sm["y_done"], 10 * q + (2 * l + h + 1))
                            act.activation(y_sb[:, h, :, :].rearrange("p b c -> p (b c)"),
                                           PS[:, h, 0:WAVE * P], ACT.Copy).then_inc(sm["ysb_ready"], 1)
                    act.wait_ge(sm["mh_done"], q + 1)
                    for h, r in enumerate(halves):
                        for p in range(2):
                            act.activation(h_bd[r, p:2 * WAVE:2, r],
                                           PS[r, 2 + p, 0:WAVE * P].rearrange("p (b c) -> p b c", b=WAVE)[:, :, HD:P],
                                           ACT.Copy).then_inc(sm["hbd_ready"], 1)
                    if w < 2:
                        token_major(q + 1)
                    act.wait_ge(sm["yb_done"], q + 1)
                    for blk, n, c0 in wave_runs(w):
                        ins = act.activation(at_rt[:, 1, c0:c0 + n * P], PS[:, 7, blk * P:(blk + n) * P], ACT.Copy)
                    ins.then_inc(sm["y_stored"], 1)
            over_pairs(lambda start, end, body: repeat(act, start, end, body), between, waves)

        def rwkv_pool(pool, chain):
            pool.wait_ge(sm["rw_loaded"], 64)
            pool.wait_ge(sm["gated"], 1)

            def between(p, f):
                if p is None:
                    return
                if f is not None:
                    pool.wait_ge(sm["tm_done"], 9 * p)
                pool.tensor_copy(v_cur[:, 0:W1], pb[:, ds(p + 4, 1), 1:PBW].rearrange("p a c -> p (a c)"))\
                    .then_inc(sm["r_staged"], 1)
                pool.tensor_copy(wa2_cur[:, :], wa2[:, ds(p * P, P)]).then_inc(sm["r_staged"], 1)
                pool.tensor_copy(rc[:, :], rw_par[:, ds(p, 1), :].rearrange("p a c -> p (a c)"))\
                    .then_inc(sm["r_staged"], 1)
                pool.wait_ge(sm["r_staged"], 3 * p + 3)
                pool.wait_ge(sm["gated"], p + 1)
                pool.tensor_tensor(rc_end[:, :], rc[:, :], ones[:, 0:9], ALU.mult).then_inc(sm["end_staged"], 1)
                pool.tensor_copy(g2_cur[:, :], g2[:, ds(p * P, P)]).then_inc(sm["end_staged"], 1)

            def waves(m):
                for w in range(3):
                    q = 3 * m + w
                    pool.wait_ge(sm["sa_ready"], 6 * q + 5)
                    pool.tensor_tensor(bt_level[:, 0, :, :], sa[:, 0, :, 0, :],
                                       level_mask[:, 0:1, :].broadcast_to([P, WAVE, P]), ALU.mult)\
                        .then_inc(sm["bt_ready"], 1)
                    chain(pool.tensor_tensor(xx[:, 0, 1, :, :], sa[:, 0, :, 0, :],
                                             x0_mask[:, 1:2, :].broadcast_to([P, WAVE, P]), ALU.mult))
                    pool.tensor_tensor(xx[:, 0, :, :, :].rearrange("p a b c -> p (a b) c"),
                                       xx[:, 0, :, :, :].rearrange("p a b c -> p (a b) c"),
                                       ident[:, :].unsqueeze(1).broadcast_to([P, 2 * WAVE, P]), ALU.add)\
                        .then_inc(sm["x_init"], 1)
                    pool.wait_ge(sm["y_stored"], q + 1)
                    pool.tensor_tensor(m_bd[:, :, :], ident[:, :].unsqueeze(1).broadcast_to([P, 2 * WAVE, P]),
                                       decay_end[:, 2 * WAVE * w:2 * WAVE * (w + 1)].unsqueeze(2)
                                       .broadcast_to([P, 2 * WAVE, P]), ALU.mult).then_inc(sm["mdiag_ready"], 1)
                    for l in range(1, LEVELS - 1):
                        for h in range(2):
                            pool.wait_ge(sm["y_done"], 10 * q + (2 * (l - 1) + h + 1))
                            pool.tensor_tensor(bt_level[:, h, :, :], sa[:, h, :, 0, :],
                                               level_mask[:, l:l + 1, :].broadcast_to([P, WAVE, P]), ALU.mult)\
                                .then_inc(sm["bt_ready"], 1)
            over_pairs(lambda start, end, body: chain.loop(start, end, 3, body), between, waves)

        def rwkv_pe(pe):
            pe.wait_ge(sm["squashed"], 2)

            def spread(lhs, rows, rhs, bank):
                for g in range(3):
                    last = pe.matmul(PS[:, bank + g, 0:G3], lhs, rhs[rows, g * G3:(g + 1) * G3],
                                     start=True, stop=True)
                return last

            def between(p, f):
                low = pb[:, 12, 1:PBW]
                if f is not None:
                    pe.wait_ge(sm["y_stored"], 3 * f + 4)
                    spread(head_ones[:, :], slice(0, P), at_rt[:, 1, 0:W1], 0).then_inc(sm["mean_done"], 1)
                    pe.wait_ge(sm["s_new"], 17 * f + 17)
                if p is not None:
                    pe.wait_ge(sm["r_staged"], 3 * p + 3)
                    spread(wa2_cur[HD:P, :], halves[1], low, 3).then_inc(sm["low_done"], 1)
                if f is not None:
                    pe.wait_ge(sm["yc_ready"], f + 1)
                if p is not None:
                    spread(wa2_cur[0:HD, :], halves[0], low, 0).then_inc(sm["low_done"], 1)
                    pe.wait_ge(sm["sg_ready"], 2 * p + 1)
                if f is not None:
                    spread(head_ones[:, :], slice(0, P), y_var, 3).then_inc(sm["var_done"], 1)
                if p is not None:
                    pe.wait_ge(sm["sg_ready"], 2 * p + 2)
                    pe.wait_ge(sm["ksq_ready"], p + 1)
                    spread(head_ones[:, :], slice(0, P), kt_, 0).then_inc(sm["ss_done"], 1)
                if f is not None:
                    pe.wait_ge(sm["end_staged"], 2 * f + 2)
                    pe.wait_ge(sm["var_read"], f + 1)
                    spread(g2_cur[:, :], slice(0, P), pb[:, 13, 1:PBW], 3).then_inc(sm["zg_done"], 1)
                if p is not None:
                    pe.wait_ge(sm["rk_ready"], p + 1)
                    pe.wait_ge(sm["ss_read"], p + 1)
                    spread(head_ones[:, :], slice(0, P), kk_, 0).then_inc(sm["bonus_done"], 1)

            def waves(m):
                pe.wait_ge(sm["gated"], m + 1)
                for w in range(3):
                    wave(m, w)

            def token_major(w, b, half):
                cols = slice(block_cols(WAVE * w + b), block_cols(WAVE * w + b) + P)
                sources = [at_rt[:, 0, cols], bk_hat[:, 0, b * P:(b + 1) * P],
                           bk_hat[:, 1, b * P:(b + 1) * P], v_cur[:, cols]]
                for i in (2 * half, 2 * half + 1):
                    last = pe.transpose(PS[:, b, i * P:(i + 1) * P], sources[i], ident[:, :])
                if half:
                    last.then_inc(sm["tm_done"], 1)

            def wave(m, w):
                q = 3 * m + w
                cols = [slice(block_cols(WAVE * w + b), block_cols(WAVE * w + b) + P) for b in range(WAVE)]
                if w == 0:
                    pe.wait_ge(sm["hat_ready"], q + 1)
                    for b in range(WAVE):
                        token_major(0, b, 0)
                        token_major(0, b, 1)
                else:
                    pe.wait_ge(sm["s_new"], 17 * m + 6 * w)
                for h, r in enumerate(halves):
                    for b in range(WAVE):
                        u = 3 * h + b
                        pe.wait_ge(sm["sa_ready"], 6 * q + (u + 1))
                        pe.matmul(PS[:, 3 + u % 2, 0:2 * P], bt_[r, cols[b]], at_rt[r, :, cols[b]],
                                  start=True, stop=True)
                        pe.matmul(PS[:, 3 + u % 2, 2 * P:4 * P], kt_[r, cols[b]], at_rt[r, :, cols[b]],
                                  start=True, stop=True)
                        pe.matmul(PS[:, 5 + u % 2, 0:P], at_rt[r, 0, cols[b]], bt_[r, cols[b]],
                                  start=True, stop=True).then_inc(sm["ab_done"], 1)
                pe.wait_ge(sm["tm_ready"], 3 * q + 3)
                pe.wait_ge(sm["sa_ready"], 6 * q + 8)
                for h in range(2):
                    for b in range(WAVE):
                        u = 3 * h + b
                        last = pe.matmul(PS[:, 6, u * HD:(u + 1) * HD], sa[:, h, b, 2, :], tm[:, b, 3, halves[h]],
                                         start=True, stop=True)
                last.then_inc(sm["akv_done"], 1)
                for l in range(LEVELS - 1):
                    for h in range(2):
                        if l or not h:
                            pe.wait_ge(sm["bt_ready"], 9 * q + (1 if l == 0 else 2 * l + h))
                        if l == 0:
                            pe.wait_ge(sm["x_init1"] if h else sm["x_init"], q + 1)
                            if h:
                                pe.wait_ge(sm["bt1_ready"], q + 1)
                        else:
                            pe.wait_ge(sm["xadd"], 10 * q + (2 * (l - 1) + h + 1))
                        for b in range(WAVE):
                            last = pe.matmul(PS[:, h, b * P:(b + 1) * P], bt_level[:, h, b, :], xx[:, h, 0, b, :],
                                             start=True, stop=True)
                        last.then_inc(sm["y_done"], 1)
                    for h in range(2):
                        pe.wait_ge(sm["ysb_ready"], 10 * q + (2 * l + h + 1))
                        for b in range(WAVE):
                            if l < LEVELS - 2:
                                pe.matmul(PS[:, 2 + 2 * h, b * P:(b + 1) * P], xx[:, h, 1, b, :], y_sb[:, h, b, :],
                                          start=True, stop=True)
                            last = pe.matmul(PS[:, 3 + 2 * h, b * P:(b + 1) * P], y_sb[:, h, b, :],
                                             xx[:, h, 1, b, :], start=True, stop=True)
                        last.then_inc(sm["xprod_done"], 1)
                pe.wait_ge(sm["akv_ready"], q + 1)
                for h in range(2):
                    pe.wait_ge(sm["xadd"], 10 * q + (8 + h + 1))
                    for b in range(WAVE):
                        pe.matmul(PS[:, h, b * P:b * P + HD], xx[:, h, 1, b, :], tm[:, b, 0, halves[h]],
                                  start=True, stop=True)
                        last = pe.matmul(PS[:, h, b * P + HD:(b + 1) * P], xx[:, h, 1, b, :], akv[:, h, b, :],
                                         start=True, stop=True)
                    last.then_inc(sm["wz_done"], 1)
                pe.wait_ge(sm["wz_ready"], 2 * q + 2)
                for h, r in enumerate(halves):
                    for b in range(WAVE):
                        last = pe.matmul(PS[r, 4, b * P:(b + 1) * P], wz[:, h, b, 0, :], sa[:, h, b, 1, :],
                                         start=True, stop=True)
                last.then_inc(sm["reff_done"], 1)
                for p, rows in enumerate(halves):
                    for h, r in enumerate(halves):
                        for b in range(WAVE):
                            pe.matmul(PS[r, 2 + p, b * P:b * P + HD], wz[rows, h, b, 0, :], tm[rows, b, 1, r],
                                      start=True, stop=True)
                            out = PS[r, 2 + p, b * P + HD:(b + 1) * P]
                            pe.matmul(out, tm[rows, b, 1, r], wz[rows, h, b, 1, :], start=True, stop=False)
                            last = pe.matmul(out, tm[rows, b, 2, r], tm[rows, b, 3, r], start=False, stop=True)
                last.then_inc(sm["mh_done"], 1)
                pe.wait_ge(sm["y_stored"], q + 1)
                for b in range(WAVE):
                    for h, r in enumerate(halves):
                        out = PS[r, 7, b * P:(b + 1) * P]
                        pe.matmul(out, tm[:, b, 3, r], sa[:, h, b, 3, :], start=b == 0, stop=False,
                                  skip_group_check=True)
                        pe.matmul(out, wz[:, h, b, 1, :], sa[:, h, b, 1, :], start=False, stop=False,
                                  skip_group_check=True)
                steps = 2 * WAVE if w < 2 else 2 * WAVE - 1
                pe.wait_ge(sm["mbd_ready"], q + 1)
                pe.wait_ge(sm["s_init"], q + 1)
                for c in range(steps):
                    if c:
                        pe.wait_ge(sm["s_new"], 17 * m + (6 * w + c))
                    pe.matmul(PS[:, 5, 0:P], m_bd[:, c, :], s_bd[:, c, :], start=True, stop=True)\
                      .then_inc(sm["s_done"], 1)
                    if w < 2:
                        if c == 0:
                            pe.wait_ge(sm["hat_ready"], q + 2)
                        token_major(w + 1, c // 2, c % 2)
                pe.wait_ge(sm["s_new"], 17 * m + (6 * w + 5))
                pe.wait_ge(sm["r_ready"], q + 1)
                for b in range(WAVE):
                    for p in range(2):
                        last = pe.matmul(PS[:, 7, b * P + p * HD:b * P + (p + 1) * HD], s_bd[:, 2 * b + p, :],
                                         r_eff[:, b, halves[p]], start=False, stop=True, skip_group_check=True)
                last.then_inc(sm["yb_done"], 1)
            over_pairs(lambda start, end, body: repeat(pe, start, end, body), between, waves)

        def rwkv_dve(dve, chain):
            for t in (at_rt[:, :, W1:WP], kt_[:, W1:WP], bt_[:, W1:WP], bonus[:, W1:WP], v_cur[:, W1:WP],
                      decay_end[:, :], h_bd[:, :, :]):
                dve.memset(t, 0.0)
            dve.wait_ge(sm["rw_loaded"], 64)
            chain(dve.tensor_scalar(rw_par[:, :, 7:8], rw_par[:, :, 3:4], -1.0, 1.0, ALU.mult, ALU.add))
            dve.memset(s_bd[:, :, :], 0.0).then_inc(sm["gated"], 1)
            dve.memset(wz[:, :, :, :, :], 0.0).then_inc(sm["sa_ready"], 2)
            dve.memset(r_eff[:, :, :], 0.0).then_inc(sm["y_stored"], 1)

            def between(p, f):
                T0, T2, T1 = at_rt[:, 0, 0:W1], at_rt[:, 1, 0:W1], kt_[:, 0:W1]
                T3, T4, T5, T6 = pinv[:, 0:W1], bonus[:, 0:W1], kk_[:, 0:W1], bt_[:, 0:W1]

                def tile(i):
                    return pb[:, ds(i, 1), 1:PBW].rearrange("p a c -> p (a c)")

                def tile_thirds(i):
                    return pb[:, ds(i, 1), 1:PBW].rearrange("p a (g c) -> p (a g) c", g=3)

                if f is not None:
                    dve.wait_ge(sm["mean_done"], f + 1)
                    chain(dve.scalar_tensor_tensor(thirds(y_mid), PS[:, 0:3, 0:G3], -1.0 / HD, thirds(T2),
                                                   ALU.mult, ALU.add))
                    dve.tensor_tensor(y_var[:, :], y_mid[:, :], y_mid[:, :], ALU.mult).then_inc(sm["yc_ready"], 1)
                if p is not None:
                    dve.wait_ge(sm["sg_ready"], 2 * p + 2)
                    for c in range(SEQ // CHUNK + 1):
                        c0 = c * CHUNK if c < SEQ // CHUNK else W1 - DEC
                        n = chain.step(dve.tensor_tensor_scan(kt_[:, c0:c0 + CHUNK], ones[:, 0:CHUNK],
                                                              at_rt[:, 0, c0:c0 + CHUNK], 0.0, ALU.mult, ALU.add))
                    n = chain.step(dve.memset(kt_[:, SEQ:W1 - DEC], 0.0))
                    chain.wait(n)
                    dve.tensor_tensor(T0, T1, T0, ALU.subtract).then_inc(sm["cum_ready"], 1)
                    kk_step = chain.step(dve.tensor_scalar(T5, tile(p), rc[:, 2:3], None, ALU.mult))
                if f is not None:
                    dve.wait_ge(sm["var_done"], f + 1)
                    dve.tensor_scalar(thirds(y_var), PS[:, 3:6, 0:G3], 1.0 / HD, LNX_EPS, ALU.mult, ALU.add)\
                       .then_inc(sm["var_read"], 1)
                if p is not None:
                    chain.wait(kk_step)
                    dve.wait_ge(sm["exp_ready"], 3 * p + 3)
                    dve.tensor_tensor(T1, T5, T5, ALU.mult).then_inc(sm["ksq_ready"], 1)
                if p is not None:
                    dve.wait_ge(sm["ss_done"], p + 1)
                    dve.tensor_scalar(thirds(T1), PS[:, 0:3, 0:G3], 1e-24, None, ALU.max).then_inc(sm["ss_read"], 1)
                if f is not None:
                    dve.wait_ge(sm["vroot_ready"], f + 1)
                    end = chain.step(dve.tensor_tensor(y_mid[:, :], y_mid[:, :], y_var[:, :], ALU.mult))
                if p is not None:
                    dve.wait_ge(sm["root_ready"], p + 1)
                    kk_step = chain.step(dve.tensor_tensor(T5, T5, T1, ALU.mult))
                if f is not None:
                    dve.wait_ge(sm["end_staged"], 2 * f + 2)
                    chain.wait(end)
                    end = chain.step(dve.tensor_scalar(y_mid[:, :], y_mid[:, :], rc_end[:, 5:6], rc_end[:, 6:7],
                                                       ALU.mult, ALU.add))
                if p is not None:
                    chain.wait(kk_step)
                    chain.step(dve.scalar_tensor_tensor(T0, T5, -1.0, T0, ALU.mult, ALU.mult))
                    b_step = chain.step(dve.tensor_tensor(T6, T5, T4, ALU.mult))
                if f is not None:
                    chain.wait(end)
                    end = chain.step(dve.tensor_tensor(y_mid[:, :], y_mid[:, :], tile(f + 4), ALU.add))
                if p is not None:
                    k_step = chain.step(dve.tensor_scalar(T1, T4, rc[:, 3:4], rc[:, 7:8], ALU.mult, ALU.add))
                    chain.wait(b_step)
                    chain.step(dve.tensor_tensor(T6, T6, T3, ALU.mult))
                    chain.wait(k_step)
                    k_step = chain.step(dve.tensor_tensor(T1, T1, tile(p), ALU.mult))
                if f is not None:
                    dve.wait_ge(sm["zg_done"], f + 1)
                    chain.wait(end)
                    dve.tensor_tensor(tile_thirds(f + 8), PS[:, 3:6, 0:G3], thirds(y_mid), ALU.mult)\
                       .then_inc(sm["gated"], 1)
                if p is not None:
                    chain.wait(k_step)
                    chain(dve.scalar_tensor_tensor(T5, tile(p + 8), rc[:, 4:5], T1, ALU.mult, ALU.mult))
                    dve.tensor_tensor(T1, T1, T3, ALU.mult).then_inc(sm["rk_ready"], 1)
                    nq = SEQ // CHUNK
                    dve.tensor_copy(decay_end[:, 0:nq].unsqueeze(2),
                                    at_rt[:, 1, 0:SEQ].rearrange("p (n c) -> p n c", c=CHUNK)[:, :, CHUNK - 1:CHUNK])
                    chain(dve.tensor_copy(decay_end[:, nq:nq + 1], at_rt[:, 1, W1 - 1:W1]))
                    chain(dve.tensor_tensor(T2, T2, tile(p + 8), ALU.mult))
                    dve.wait_ge(sm["bonus_done"], p + 1)
                    chain(dve.tensor_tensor(tile_thirds(p + 4), PS[:, 0:3, 0:G3], thirds(v_cur[:, 0:W1]), ALU.mult))
                    dve.wait_ge(sm["gated"], p + 1)

            def hats(w):
                for blk, n, c0 in wave_runs(w):
                    ends = decay_end[:, 2 * (WAVE * w + blk):2 * (WAVE * w + blk + n)]
                    for i, src in enumerate((bt_, kt_)):
                        ins = dve.tensor_tensor(
                            bk_hat[:, i, blk * P:(blk + n) * P].rearrange("p (a c) -> p a c", c=CHUNK),
                            src[:, c0:c0 + n * P].rearrange("p (a c) -> p a c", c=CHUNK),
                            ends.unsqueeze(2).broadcast_to([P, 2 * n, CHUNK]), ALU.mult)
                ins.then_inc(sm["hat_ready"], 1)

            def wave(m, w):
                q = 3 * m + w
                if w == 0:
                    hats(0)
                if w == 0:
                    ins = dve.memset(s_bd[:, 0, :], 0.0)
                else:
                    dve.wait_ge(sm["y_stored"], 3 * m + (w + 1))
                    dve.wait_ge(sm["s_new"], 17 * m + 6 * w)
                    ins = dve.tensor_copy(s_bd[:, 0, :], s_bd[:, 2 * WAVE, :])
                if w == 2:
                    for r in halves:
                        ins = dve.tensor_copy(s_bd[r, 4, r], state_in[r, ds(m, 1), :].rearrange("p a c -> p (a c)"))
                ins.then_inc(sm["s_init"], 1)
                for h in range(2):
                    for b in range(WAVE):
                        u = 3 * h + b
                        dve.wait_ge(sm["ab_done"], 6 * q + (u + 1))
                        dve.tensor_tensor(sa[:, h, b, :, :], PS[:, 3 + u % 2, :].rearrange("p (a c) -> p a c", a=4),
                                          sa_mask[:, :, :], ALU.mult)
                        dve.tensor_tensor(xx[:, h, 0, b, :], PS[:, 5 + u % 2, 0:P], x0_mask[:, 0, :],
                                          ALU.mult).then_inc(sm["sa_ready"], 1)
                dve.wait_ge(sm["sa_ready"], 6 * q + 8)
                chain(dve.tensor_tensor(xx[:, 1, 1, :, :], sa[:, 1, :, 0, :],
                                        x0_mask[:, 1:2, :].broadcast_to([P, WAVE, P]), ALU.mult))
                dve.tensor_tensor(xx[:, 1, :, :, :].rearrange("p a b c -> p (a b) c"),
                                  xx[:, 1, :, :, :].rearrange("p a b c -> p (a b) c"),
                                  ident[:, :].unsqueeze(1).broadcast_to([P, 2 * WAVE, P]), ALU.add)\
                   .then_inc(sm["x_init1"], 1)
                dve.tensor_tensor(bt_level[:, 1, :, :], sa[:, 1, :, 0, :],
                                  level_mask[:, 0:1, :].broadcast_to([P, WAVE, P]), ALU.mult)\
                   .then_inc(sm["bt1_ready"], 1)
                for l in range(LEVELS - 1):
                    for h in range(2):
                        dve.wait_ge(sm["xprod_done"], 10 * q + (2 * l + h + 1))
                        k0 = 0 if l < LEVELS - 2 else 1
                        dst = xx[:, h, k0:2, :, :].rearrange("p a b c -> p a (b c)")
                        dve.tensor_tensor(dst, PS[:, 2 + 2 * h + k0:4 + 2 * h, 0:WAVE * P], dst, ALU.add)\
                           .then_inc(sm["xadd"], 1)
                for h in range(2):
                    dve.wait_ge(sm["wz_done"], 2 * q + (h + 1))
                    dve.tensor_copy(wz[:, h, :, :, :].rearrange("p b a c -> p (b a c)"), PS[:, h, 0:WAVE * P])\
                       .then_inc(sm["wz_ready"], 1)
                dve.wait_ge(sm["reff_done"], q + 1)
                for blk, n, c0 in wave_runs(w):
                    ins = dve.tensor_tensor(r_eff[:, blk:blk + n, :].rearrange("p b c -> p (b c)"),
                                            PS[:, 4, blk * P:(blk + n) * P], at_rt[:, 1, c0:c0 + n * P], ALU.add)
                ins.then_inc(sm["r_ready"], 1)
                if w < 2:
                    hats(w + 1)
                dve.wait_ge(sm["mh_done"], q + 1)
                dve.wait_ge(sm["mdiag_ready"], q + 1)
                dve.wait_ge(sm["hbd_ready"], 4 * q + 4)
                for r in halves:
                    for p in range(2):
                        ins = dve.tensor_tensor(
                            m_bd[r, p:2 * WAVE:2, r],
                            PS[r, 2 + p, 0:WAVE * P].rearrange("p (b c) -> p b c", b=WAVE)[:, :, 0:HD],
                            m_bd[r, p:2 * WAVE:2, r], ALU.add)
                ins.then_inc(sm["mbd_ready"], 1)
                for c in range(2 * WAVE if w < 2 else 2 * WAVE - 1):
                    dve.wait_ge(sm["s_done"], 17 * m + (6 * w + c + 1))
                    to = 2 * WAVE if w == 2 and c == 3 else c + 1
                    dve.tensor_tensor(s_bd[:, to, :], PS[:, 5, 0:P], h_bd[:, c, :], ALU.add).then_inc(sm["s_new"], 1)
                if w == 2:
                    dve.wait_ge(sm["s_new"], 17 * m + 17)
                    for i, slot in enumerate((2 * WAVE, 2 * WAVE - 1)):
                        for r in halves:
                            dve.tensor_copy(state_out[r, i, ds(m, 1), :].rearrange("p a c -> p (a c)"),
                                            s_bd[r, slot, r]).then_inc(sm["state_ready"], 1)

            def waves(m):
                for w in range(3):
                    wave(m, w)
            over_pairs(lambda start, end, body: chain.loop(start, end, 36, body), between, waves)

        UNITS = 2 * BLOCKS
        TURN_CREDIT = 6

        def in_turn(*parts):
            for step in range(UNITS + max(lag for _, lag in parts)):
                for part, lag in parts:
                    if 0 <= step - lag < UNITS:
                        part(step - lag)

        def unit_shape(cfg, b):
            if b < BLOCKS - 1:
                n = min(b + 1, cfg["nb"])
                return P, n, 0, n * P
            return DEC, 0, cfg["cache"], cfg["cache"] * P + DEC

        def att_pe(pe, cfg):
            mem, nb = cfg["mem"], cfg["nb"]
            pe.wait_ge(sm["hk_loaded"], cfg["hk"] + 16 * 10)
            for hd in range(8):
                if hd >= 2:
                    pe.wait_ge(sm["bias_ready"], cfg["bias0"] + hd - 1)
                for c0 in range(0, nb * P, 512):
                    cn = min(512, nb * P - c0)
                    last = pe.matmul(PS[:, 2 * (hd % 2) + c0 // 512, 0:cn], flip[:, :],
                                     mem["hankel"][:, hd, c0:c0 + cn], start=True, stop=True)
                last.then_inc(sm["hk_done"], 1)
            pe.wait_ge(sm["bias_ready"], cfg["bias0"] + 10)

            def token_major_v(m):
                pe.wait_ge(sm["v_staged"], 2 * m + (cfg["v0"] + 2))
                for b in range(BLOCKS):
                    if b % 4 == 0 and b >= 8:
                        pe.wait_ge(sm["vt_ready"], 3 * m + (3 * cfg["v0"] // 2 + b // 4 - 1))
                    last = pe.transpose(PS[:, 4 + (b // 4) % 2, (b % 4) * P:(b % 4 + 1) * P],
                                        mem["vf"][:, b * P:(b + 1) * P], ident[:, :])
                    if b % 4 == 3 or b == BLOCKS - 1:
                        last.then_inc(sm["vtr_done"], 1)
                pe.wait_ge(sm["vt_ready"], 3 * m + (3 * cfg["v0"] // 2 + 3))

            def pair(m):
                U0 = cfg["unit0"]
                if not cfg["shared_v"]:
                    token_major_v(m)
                pe.wait_ge(sm["q_staged"], 2 * m + (cfg["q0"] + 2))

                def scores(u):
                    b, h = divmod(u, 2)
                    rows, own, cached, width = unit_shape(cfg, b)
                    base = 2 * (u % 2)
                    pe.wait_ge(sm["st_done"], UNITS * m + (U0 + u + 1))
                    q = mem["qz"][:, h, b * P:(b + 1) * P]
                    if own:
                        parts = [(cfg["keys"](m, (b + 1 - own) * P, width), 0, width)]
                    else:
                        parts = [(mem["k_cache"][:, cfg["kslot"](m), :].rearrange("p a c -> p (a c)"), 0, cached * P),
                                 (cfg["keys"](m, SEQ, DEC), cached * P, DEC)]
                    for src, to, width in parts:
                        for c0 in range(0, width, 512):
                            cn = min(512, width - c0)
                            col = to + c0
                            last = pe.matmul(PS[:, base + col // 512, col % 512:col % 512 + cn], q,
                                             src[:, c0:c0 + cn], start=True, stop=True)
                    last.then_inc(sm["sc_done"], 1)

                def turn(u):
                    b, h = divmod(u, 2)
                    rows, own, cached, width = unit_shape(cfg, b)
                    pe.wait_ge(sm["p_ready"], UNITS * m + (U0 + u + 1))
                    pe.wait_ge(sm["pt_ev"], UNITS * m + (U0 + u + 3 - cfg["turns"]))
                    bank = 4 + (u % 2 if cfg["turns"] == 2 else 0)
                    for i in range((width + P - 1) // P):
                        n = min(P, width - i * P)
                        last = pe.transpose(PS[0:n, bank + i // 4, (i % 4) * P:(i % 4 + 1) * P],
                                            mem["s"][:, u % cfg["slots"], i * P:i * P + n], ident[:, :])
                    last.then_inc(sm["pt_done"], 1)

                def values(u):
                    b, h = divmod(u, 2)
                    rows, own, cached, width = unit_shape(cfg, b)
                    r = halves[h]
                    pe.wait_ge(sm["pt_ev"], UNITS * m + (U0 + u + 3))
                    pe.wait_ge(sm["o_ev"], UNITS * m + (U0 + u + 1))
                    count = (width + P - 1) // P
                    for i in range(count):
                        n = min(P, width - i * P)
                        if own:
                            v = mem["vt"][:, b + 1 - own + i, r]
                        elif i < cached:
                            v = mem["vcc"][:, i, r]
                        else:
                            v = mem["vt"][0:DEC, BLOCKS - 1, r]
                        last = pe.matmul(PS[r, 6 + u % 2, 0:rows], v, mem["pt"][0:n, u % 2, i, 0:rows],
                                         start=i == 0, stop=i == count - 1)
                    last.then_inc(sm["pv_done"], 1)

                scores(0)
                in_turn((scores, -1), (turn, cfg["lag"]), (values, cfg["lag"] + 1))
            if cfg["shared_v"]:
                token_major_v(0)
            repeat(pe, 0, PAIRS, pair)

        def att_act(act, cfg):
            mem = cfg["mem"]

            def token_major_v(m):
                for i in range(3):
                    n = min(4, BLOCKS - 4 * i)
                    act.wait_ge(sm["vtr_done"], 3 * m + (3 * cfg["v0"] // 2 + i + 1))
                    rows = P if n > 1 else DEC
                    act.activation(mem["vt"][0:rows, 4 * i:4 * i + n, :],
                                   PS[0:rows, 4 + i % 2, 0:n * P].rearrange("p (a c) -> p a c", c=P), ACT.Copy)\
                       .then_inc(sm["vt_ready"], 1)

            def pair(m):
                U0 = cfg["unit0"]
                if not cfg["shared_v"]:
                    token_major_v(m)

                def exps(u):
                    i = u % cfg["slots"]
                    rows, _, _, width = unit_shape(cfg, u // 2)
                    st = mem["stat"]
                    if cfg["sink"]:
                        act.wait_ge(sm["max_ready"], UNITS * m + (U0 + u + 1))
                    else:
                        act.wait_ge(sm["st_done"], UNITS * m + (U0 + u + 3))
                    ins = act.activation(mem["s"][0:rows, i, 0:width], mem["s"][0:rows, i, 0:width], ACT.Exp,
                                         bias=st[0:rows, i, 0:1], accum_out=st[0:rows, i, 1:2])
                    if cfg["sink"]:
                        ins = act.activation(st[0:rows, i, 3:4], sink[0:rows, ds(2 * m + u % 2, 1)], ACT.Exp,
                                             bias=st[0:rows, i, 0:1])
                    ins.then_inc(sm["exp_done"], 1)

                def evac(u):
                    rows, _, _, width = unit_shape(cfg, u // 2)
                    act.wait_ge(sm["pt_done"], UNITS * m + (U0 + u + 1 + TURN_CREDIT))
                    act.wait_ge(sm["pv_done"], UNITS * m + (U0 + u + 1))
                    whole = width // P
                    bank = 4 + (u % 2 if cfg["turns"] == 2 else 0)
                    pieces = [(i, min(4, whole - i)) for i in range(0, whole, 4)]
                    for i, n in pieces:
                        ins = act.activation(mem["pt"][:, u % 2, i:i + n, 0:rows],
                                             PS[:, bank + i // 4, 0:n * P].rearrange("p (a c) -> p a c", c=P)[:, :, 0:rows],
                                             ACT.Copy)
                    if width % P:
                        i = whole
                        ins = act.activation(mem["pt"][0:DEC, u % 2, i, 0:rows],
                                             PS[0:DEC, bank + i // 4, (i % 4) * P:(i % 4) * P + rows], ACT.Copy)
                    ins.then_inc(sm["pt_ev"], 1)

                in_turn((exps, 0), (evac, cfg["lag"]))
            if cfg["shared_v"]:
                token_major_v(0)
            repeat(act, 0, PAIRS, pair)

        def att_pool(pool, cfg, chain):
            mem = cfg["mem"]
            for t in (mem["qz"][:, :, NT:BLOCKS * P], mem["vf"][:, NT:BLOCKS * P]):
                chain(pool.memset(t, 0.0))

            def stage_v(m):
                pool.tensor_copy(mem["vf"][:, 0:NT], cfg["v"](m)).then_inc(sm["v_staged"], 1)
                if isinstance(m, int) and m == 0:
                    pool.wait_ge(sm["hk_loaded"], cfg["hk"] + 16 * 10)
                pool.tensor_copy(mem["vcc"][:, :, :], cfg["vc"](m)).then_inc(sm["v_staged"], 1)

            def pair(m):
                pool.wait_ge(sm["st_done"], UNITS * m + (cfg["unit0"] + 2))
                for h in range(2):
                    pool.tensor_tensor(mem["qz"][:, h, 0:NT], cfg["q"](m),
                                       head_ones[:, h * HD:h * HD + 1].broadcast_to([P, NT]), ALU.mult)\
                        .then_inc(sm["q_staged"], 1)
                if not cfg["shared_v"]:
                    pool.wait_ge(sm["pv_done"], UNITS * m + (cfg["unit0"] + 2))
                    stage_v(m)
                if not cfg["sink"]:
                    pool.wait_ge(sm["z_ready"], m + 1)
                    pool.tensor_copy(cc[:, :], conv_par[:, ds(m, 1), :].rearrange("p a c -> p (a c)"))\
                        .then_inc(sm["conv_staged"], 1)
                    pool.wait_ge(sm["conv_staged"], m + 1)
                    pool.wait_ge(sm["bias_ready"], cfg["bias0"] + 8)
                    for t in range(TAPS - POOL_TAPS, TAPS):
                        first = t == TAPS - POOL_TAPS
                        to = zc_pool if first else tap_pool
                        chain(pool.tensor_scalar(to[:, :], u_buf[:, m, t:t + ZW], cc[:, t:t + 1], None, ALU.mult))
                        if first:
                            continue
                        ins = pool.tensor_tensor(zc_pool[:, :], zc_pool[:, :], tap_pool[:, :], ALU.add)
                        if t < TAPS - 1:
                            chain(ins)
                    ins.then_inc(sm["zc_pool_ready"], 1)
            if cfg["shared_v"]:
                stage_v(0)
                repeat(pool, 0, PAIRS, pair)
                return
            for m in range(PAIRS):
                pair(m)

        def att_dve(dve, cfg, chain, taps=None):
            mem, nb = cfg["mem"], cfg["nb"]
            if cfg["sink"]:
                chain(dve.tensor_scalar(neg_sink[:, :], sink[:, :], -1.0, None, ALU.mult))
            for hd in range(8):
                dve.wait_ge(sm["hk_done"], cfg["bias0"] * 8 // 10 + hd + 1)
                for c0 in range(0, nb * P, 512):
                    cn = min(512, nb * P - c0)
                    ins = dve.tensor_copy(mem["bias"][:, hd, c0:c0 + cn], PS[:, 2 * (hd % 2) + c0 // 512, 0:cn])
                ins.then_inc(sm["bias_ready"], 1)
            dve.wait_ge(sm["bias_ready"], cfg["bias0"] + 8)
            dve.memset(mem["bias"][0:HD, :, nb * P - CHUNK:nb * P], NEG).then_inc(sm["bias_ready"], 1)
            dve.memset(mem["bias"][HD:P, :, 0:CHUNK], NEG).then_inc(sm["bias_ready"], 1)
            dve.wait_ge(sm["bias_ready"], cfg["bias0"] + 10)
            if cfg["unit0"] == 0:
                for i, (credit, count) in enumerate(((sm["st_done"], 2), (sm["pt_done"], TURN_CREDIT),
                                                     (sm["pt_ev"], 2), (sm["pv_done"], 2), (sm["o_ev"], 2))):
                    dve.memset(mem["stat"][:, i // 4, i % 4:i % 4 + 1], 0.0).then_inc(credit, count)
                dve.wait_ge(sm["o_ev"], 2)

            def pair(m):
                U0 = cfg["unit0"]
                st = mem["stat"]
                if taps:
                    dve.wait_ge(sm["conv_staged"], m + 1)

                def scores(u):
                    b, h = divmod(u, 2)
                    i = u % cfg["slots"]
                    rows, own, cached, width = unit_shape(cfg, b)
                    dve.wait_ge(sm["sc_done"], UNITS * m + (U0 + u + 1))
                    dve.wait_ge(sm["pt_done"], UNITS * m + (U0 + u + 1 + TURN_CREDIT - cfg["slots"]))
                    blocks = own if own else cached + 1
                    bias0 = (nb - blocks) * P
                    for c0 in range(0, width, 512):
                        cn = min(512, width - c0)
                        steps["scores"] = chain.step(dve.scalar_tensor_tensor(
                            mem["s"][0:rows, i, c0:c0 + cn], PS[0:rows, 2 * (u % 2) + c0 // 512, 0:cn],
                            HD ** -0.5, mem["bias"][0:rows, ds(2 * m + h, 1), bias0 + c0:bias0 + c0 + cn]
                            .rearrange("p a c -> p (a c)"), ALU.mult, ALU.add))

                def maximum(u):
                    i = u % cfg["slots"]
                    rows, _, _, width = unit_shape(cfg, u // 2)
                    chain.wait(steps["scores"])
                    ins = dve.tensor_reduce(st[0:rows, i, 0:1], mem["s"][0:rows, i, 0:width], AX, ALU.max,
                                            negate=True)
                    ins.then_inc(sm["st_done"], 1)

                def sink_maximum(u):
                    i = u % cfg["slots"]
                    rows = unit_shape(cfg, u // 2)[0]
                    dve.wait_ge(sm["st_done"], UNITS * m + (U0 + u + 3))
                    dve.tensor_tensor(st[0:rows, i, 0:1], st[0:rows, i, 0:1],
                                      neg_sink[0:rows, ds(2 * m + u % 2, 1)], ALU.min).then_inc(sm["max_ready"], 1)

                def total(u):
                    i = u % cfg["slots"]
                    rows = unit_shape(cfg, u // 2)[0]
                    dve.wait_ge(sm["exp_done"], UNITS * m + (U0 + u + 1))
                    steps["total"] = chain.step(dve.tensor_tensor(st[0:rows, i, 1:2], st[0:rows, i, 1:2],
                                                                  st[0:rows, i, 3:4], ALU.add))

                def inverse(u):
                    i = u % cfg["slots"]
                    rows = unit_shape(cfg, u // 2)[0]
                    if cfg["sink"]:
                        chain.wait(steps["total"])
                    else:
                        dve.wait_ge(sm["exp_done"], UNITS * m + (U0 + u + 1))
                    steps["inverse"] = chain.step(dve.reciprocal(st[0:rows, i, 2:3], st[0:rows, i, 1:2]))

                def scale(u):
                    i = u % cfg["slots"]
                    rows, _, _, width = unit_shape(cfg, u // 2)
                    chain.wait(steps["inverse"])
                    dve.tensor_scalar(mem["s"][0:rows, i, 0:width], mem["s"][0:rows, i, 0:width],
                                      st[0:rows, i, 2:3], None, ALU.mult).then_inc(sm["p_ready"], 1)

                def out(u):
                    b, h = divmod(u, 2)
                    rows = unit_shape(cfg, b)[0]
                    dve.wait_ge(sm["pv_done"], UNITS * m + (U0 + u + 1 + 2))
                    dve.tensor_copy(cfg["q"](m)[halves[h], b * P:b * P + rows], PS[halves[h], 6 + u % 2, 0:rows])\
                       .then_inc(sm["o_ev"], 1)

                steps, lag = {}, cfg["lag"]
                if cfg["sink"]:
                    in_turn((scores, 0), (total, lag), (maximum, 0), (inverse, lag), (sink_maximum, 0), (scale, lag),
                            (out, lag + 2))
                else:
                    in_turn((scores, 0), (inverse, lag), (lambda u: taps(m, 2 * u), 0), (maximum, 0), (scale, lag),
                            (out, lag + 2), (lambda u: taps(m, 2 * u + 1), 0))
                    taps(m, None)
            chain.loop(0, PAIRS, cfg["chain"], pair)

        def conv_taps(chain, dve):
            zc = mem_c["zc"]

            last = {}
            DVE_TAPS = TAPS - POOL_TAPS

            def taps(m, part):
                if part is None:
                    chain.wait(last["tap"])
                    dve.wait_ge(sm["zc_pool_ready"], m + 1)
                    dve.tensor_tensor(z_buf[:, ds(m, 1), 0:SEQ].rearrange("p a c -> p (a c)"), zc[:, 0:SEQ],
                                      zc_pool[:, 0:SEQ], ALU.add)
                    dve.tensor_tensor(z_buf[:, ds(m, 1), SEQ:NT].rearrange("p a c -> p (a c)"), zc[:, ZW - DEC:ZW],
                                      zc_pool[:, ZW - DEC:ZW], ALU.add).then_inc(sm["z_ready"], 1)
                    return
                for t in range(DVE_TAPS * part // (2 * UNITS), DVE_TAPS * (part + 1) // (2 * UNITS)):
                    src = u_buf[:, ds(m, 1), t:t + ZW].rearrange("p a c -> p (a c)")
                    if t == 0:
                        ins = dve.tensor_scalar(zc[:, :], src, cc[:, 0:1], cc[:, TAPS:TAPS + 1], ALU.mult, ALU.add)
                    else:
                        chain.wait(last["tap"])
                        ins = dve.scalar_tensor_tensor(zc[:, :], src, cc[:, t:t + 1], zc[:, :], ALU.mult, ALU.add)
                    last["tap"] = chain.step(ins)
            return taps

        QN = NT // 4

        def quarters(t):
            return t.rearrange("p (g c) -> p g c", g=4)

        def ln_pe(pe):
            for src, bank, done in ((z_buf, 0, sm["lnm_done"]), (ln_t, 4, sm["lnv_done"])):
                for i in range(4):
                    if bank:
                        pe.wait_ge(sm["lnq_ready"], i + 1)
                    for g in range(4):
                        last = pe.matmul(PS[:, bank + g, 0:QN], ones[:, :], src[:, i, g * QN:(g + 1) * QN],
                                         start=i == 0, stop=i == 3)
                last.then_inc(done, 1)

        def ln_dve(dve, chain):
            dve.wait_ge(sm["lnm_done"], 1)
            for i in range(4):
                dve.scalar_tensor_tensor(quarters(z_buf[:, i, :]), PS[:, 0:4, 0:QN], -1.0 / 512,
                                         quarters(z_buf[:, i, :]), ALU.mult, ALU.add).then_inc(sm["lnc_ready"], 1)
            dve.wait_ge(sm["lnv_done"], 1)
            dve.tensor_scalar(quarters(ln_r[:, :]), PS[:, 4:8, 0:QN], 1.0 / 512, LN_EPS, ALU.mult, ALU.add)\
               .then_inc(sm["lnr_ready"], 1)
            dve.wait_ge(sm["lnz_ready"], 2)
            for i in range(4):
                dve.tensor_tensor(z_buf[:, i, :], z_buf[:, i, :], ln_r[:, :], ALU.mult).then_inc(sm["lnc_ready"], 1)

        def ln_pool(pool):
            for i in range(4):
                pool.wait_ge(sm["lnc_ready"], i + 1)
                pool.tensor_tensor(ln_t[:, i, :], z_buf[:, i, :], z_buf[:, i, :], ALU.mult).then_inc(sm["lnq_ready"], 1)

        def ln_act(act):
            act.wait_ge(sm["lnr_ready"], 1)
            act.activation(ln_r[:, :], ln_r[:, :], ACT.Ln).then_inc(sm["lnz_ready"], 1)
            act.wait_ge(sm["lnz_ready"], 1)
            act.activation(ln_r[:, :], ln_r[:, :], ACT.Exp, scale=-0.5).then_inc(sm["lnz_ready"], 1)
            for i in range(4):
                act.wait_ge(sm["lnc_ready"], 4 + i + 1)
                act.activation(z_buf[:, i, :], z_buf[:, i, :], ACT.Silu, scale=conv_par[:, i, TAPS + 1:TAPS + 2],
                               bias=conv_par[:, i, TAPS + 2:TAPS + 3]).then_inc(sm["silu_ready"], 1)

        flat = "p a c -> p (a c)"
        cfg_a = dict(nb=2, cache=1, mem=mem_a, sink=True, unit0=0, hk=0, bias0=0, q0=0, v0=0, chain=54,
                     slots=6, lag=2, turns=2, shared_v=True,
                     keys=lambda m, c0, cn: akvq[:, 0, c0:c0 + cn], kslot=lambda m: slice(0, 1),
                     q=lambda m: akvq[:, ds(m + 2, 1), :].rearrange(flat), v=lambda m: akvq[:, 1, :],
                     vc=lambda m: mem_a["v_cache"][:, :, :])
        cfg_c = dict(nb=5, cache=2, mem=mem_c, sink=False, unit0=PAIRS * UNITS, hk=160, bias0=10, q0=8, v0=2,
                     chain=26 + 18 + TAPS - POOL_TAPS, slots=3, lag=1, turns=1, shared_v=False,
                     keys=lambda m, c0, cn: cproj[:, ds(m, 1), c0:c0 + cn].rearrange(flat),
                     kslot=lambda m: ds(m, 1),
                     q=lambda m: cproj[:, ds(m + 8, 1), :].rearrange(flat),
                     v=lambda m: cproj[:, ds(m + 4, 1), :].rearrange(flat),
                     vc=lambda m: mem_c["v_cache"][:, :, ds(m * P, P)])

        block = ctx.enter_context(nc.Block())

        @block.sync
        def _(sp):
            sp.dma_start(whole(gains), d["gains"]).then_inc(sm["gains_loaded"], 16)
            for g, (c0, cn) in enumerate(GROUPS):
                sp.dma_start(x[:, :, c0:c0 + cn], d["x"][:, :, c0:c0 + cn]).then_inc(x_loaded[g], 16)
                if g < 2:
                    sp_tile(sp, 0, g, g)
            n_const = 0
            for name, t in (("ones", ones), ("pick_a", pick_a), ("pick_c", pick_c), ("table_a", table_a),
                            ("table_c", table_c), ("mu", mu), ("shift_in", shift_in), ("rw_par", rw_par),
                            ("ident", ident), ("flip", flip), ("head_ones", head_ones), ("sa_mask", sa_mask),
                            ("level_mask", level_mask), ("conv_par", conv_par), ("sink", sink)):
                sp.dma_start(whole(t), d[name]).then_inc(sm["consts_loaded"], 16)
                n_const += 16
            assert n_const == N_CONST
            sp.wait_ge(sm["vec_copied"], 3)
            sp.dma_start(vec_home.ap().rearrange("a h c -> h a c"), vec_sb[0:8, :, :]).then_inc(sm["vec_stored"], 16)
            sp_rest(sp, 0)
            sp_first(sp, 1)
            sp.wait_ge(sm["vec_stored"], 16)
            sp.wait_ge(sm["barrier"], 4)
            for t, name in ((wa2, "wa2"), (g2, "g2"), (x0_mask, "x0_mask"), (state_in, "state_in")):
                sp.dma_start(whole(t), d[name]).then_inc(sm["rw_loaded"], 16)
            sp.dma_start(d["out_akv"], akvq[:, 0:2, NT - 192:NT]).then_inc(sm["stored"], 16)
            sp.wait_ge(sm["barrier"], 8)
            sp.dma_start(d["out_state"], state_out[:, :, :, :]).then_inc(sm["stored"], 16)
            sp.dma_start(d["out_shift"], shift_out[:, :, :]).then_inc(sm["stored"], 16)
            sp.wait_ge(sm["stored"], 48)

            def attention_loads(mem, which, nb, length, kc, vc):
                for hd in range(8):
                    src = bass.AP(tensor=vec_home, offset=(which * 8 + hd) * VEC_C, ap=[[1, P], [1, nb * P]])
                    sp.dma_start(mem["hankel"][:, hd, :], src).then_inc(sm["hk_loaded"], 16)
                sp.dma_start(mem["k_cache"][:, :, :], d[kc]).then_inc(sm["hk_loaded"], 16)
                sp.dma_start(mem["v_cache"][:, :, :], d[vc]).then_inc(sm["hk_loaded"], 16)

            attention_loads(mem_a, 0, 2, VEC_A, "a_kc", "a_vc")
            sp.wait_ge(sm["barrier"], 12)
            for g, (c0, cn) in enumerate(GROUPS):
                sp.dma_start(x[:, :, c0:c0 + cn], d["x"][:, :, c0:c0 + cn]).then_inc(x_loaded[g], 16)
            sp_rest(sp, 1)
            for s in range(2, S_IN[1]):
                sp_first(sp, s)
                sp_rest(sp, s)
            sp_first(sp, S_IN[1])
            sp.wait_ge(sm["evac_done"], (x_from[2] + KT) * NG)
            sp.dma_start(x_home, x[:, :, :]).then_inc(sm["x_saved"], 16)
            sp_rest(sp, S_IN[1])
            sp_first(sp, S_IN[1] + 1)
            sp.wait_ge(sm["barrier"], 16)
            sp.dma_start(u_buf[:, :, TAPS - 1 + SEQ:2 * (TAPS - 1) + SEQ], d["conv_in"])\
              .then_inc(sm["cstate_loaded"], 16)
            attention_loads(mem_c, 1, 5, VEC_C, "c_kc", "c_vc")
            sp.dma_start(d["out_ckv"], cproj[:, 0:8, 512:NT]).then_inc(sm["stored"], 16)
            sp.dma_start(d["out_conv"][:, :, 0, :], u_buf[:, :, SEQ:SEQ + TAPS - 1]).then_inc(sm["stored"], 16)
            sp.dma_start(d["out_conv"][:, :, 1, :], u_buf[:, :, UW - TAPS + 1:UW]).then_inc(sm["stored"], 16)
            sp.wait_ge(sm["barrier"], 20)
            sp.wait_ge(sm["stored"], 96)
            for g, (c0, cn) in enumerate(GROUPS):
                sp.dma_start(x[:, :, c0:c0 + cn], x_home[:, :, c0:c0 + cn]).then_inc(x_loaded[g], 16)
            sp_rest(sp, S_IN[1] + 1)
            for s in range(S_IN[1] + 2, len(stages)):
                sp_first(sp, s)
                sp_rest(sp, s)
            for g, (c0, cn) in enumerate(GROUPS):
                sp.wait_ge(sm["y_ready"], KT * (g + 1))
                sp.dma_start(d["out_y"][:, :, c0:c0 + cn], x[:, :, c0:c0 + cn]).then_inc(sm["stored"], 16)
            sp.wait_ge(sm["stored"], 96 + 48)

        @block.tensor
        def _(pe):
            def bias_values():
                pe.wait_ge(sm["consts_loaded"], N_CONST)
                pe.matmul(PS[0:8, 7, 0:VEC_A], table_a[:, :], pick_a[:, :], start=True, stop=True)\
                  .then_inc(sm["vec_done"], 1)
                for n, c0 in enumerate(range(0, VEC_C, 512)):
                    pe.wait_ge(sm["vec_copied"], n + 1)
                    cn = min(512, VEC_C - c0)
                    for k in range(3):
                        last = pe.matmul(PS[0:8, 7, 0:cn], table_c[:, k, :], pick_c[:, k, c0:c0 + cn],
                                         start=k == 0, stop=k == 2)
                    last.then_inc(sm["vec_done"], 1)
                pe.wait_ge(sm["vec_copied"], 3)
            pe_stage(pe, 0, h_hi, h_lo, h_groups_first(pe, 0), norm=0, between=bias_values)
            pe.wait_ge(sm["evac_done"], bases[1] * NG)
            sync_all("pe", pe)
            rwkv_pe(pe)
            sync_all("pe", pe)
            att_pe(pe, cfg_a)
            sync_all("pe", pe)
            pe_stage(pe, 1, h_hi, h_lo, h_groups_first(pe, 1))
            for n, (sg, sd, k0, kn) in enumerate(groups0):
                pe_stage(pe, sg, h_hi, h_lo, None if n else h_groups_first(pe, 2), norm=None if n else 1)
                pe_stage(pe, sd, hid_hi, hid_lo, hidden_ready(pe, 0, k0, kn))
            pe_stage(pe, S_IN[1], h_hi, h_lo, h_tiles_first(pe, 3), norm=2)
            pe.wait_ge(sm["evac_done"], bases[S_IN[1] + 1] * NG)
            sync_all("pe", pe)
            att_pe(pe, cfg_c)
            sync_all("pe", pe)
            ln_pe(pe)
            sync_all("pe", pe)
            pe_stage(pe, S_IN[1] + 1, h_hi, h_lo, h_groups_first(pe, 4))
            for n, (sg, sd, k0, kn) in enumerate(groups1):
                pe_stage(pe, sg, h_hi, h_lo, None if n else h_groups_first(pe, 5), norm=None if n else 3)
                pe_stage(pe, sd, hid_hi, hid_lo, hidden_ready(pe, 1, k0, kn))
            pe_stats(pe, 4)

        @block.scalar
        def _(act):
            act.wait_ge(sm["gains_loaded"], 16)
            act_h(act, 0, 0, by_group)
            act_hi(act, 0, 0, 0, KT)
            act_hi(act, 0, 1, 0, KT)
            act.wait_ge(sm["consts_loaded"], N_CONST)
            act_rstd(act, 0)
            act_stage(act, 0)
            sync_all("act", act)
            rwkv_act(act)
            sync_all("act", act)
            att_act(act, cfg_a)
            sync_all("act", act)
            act_concat(act, 0)
            act_stage(act, 1)

            def ffn(layer, groups, norm, h):
                act.wait_ge(sm["product_done"], bases[groups[0][0]] * NG)
                act_h(act, norm, h, by_group)
                act_rstd(act, norm)
                for n, (sg, sd, k0, kn) in enumerate(groups):
                    act_hidden(act, sg, layer, k0, kn)
                    last = n == len(groups) - 1 and layer == 0
                    act_stage(act, sd, (lambda j, slot: act_h(act, 2, 3, [(2 * j + slot, g) for g in range(NG)]))
                              if last else None)

            ffn(0, groups0, 1, 2)
            act_rstd(act, 2)

            def conv_gate(j, slot):
                if slot:
                    return
                for g, (c0, cn) in enumerate(GROUPS):
                    act.wait_ge(sm["evac_done"], j * (2 * NG) + ((bases[S_IN[1]] + 12) * NG + g + 1))
                    act.activation(gate_t[:, g, 0:cn], gate_t[:, g, 0:cn], ACT.Sigmoid).then_inc(sm["gate_ready"], 1)
            base = bases[S_IN[1]]

            def splits(j):
                for slot in range(2):
                    act_hi(act, j, slot, base + 2, KT)

            def conv_pair(j):
                for slot in range(2):
                    conv_gate(j, slot)
                    act_hi(act, j, slot, base + 14, KT)
            repeat(act, 0, 6, splits)
            repeat(act, 0, 3, conv_pair)
            conv_pair_last = 3
            for slot in range(2):
                conv_gate(conv_pair_last, slot)
                act_hi(act, 0, slot, bases[S_IN[1] + 1], KT)
            sync_all("act", act)
            att_act(act, cfg_c)
            sync_all("act", act)
            ln_act(act)
            sync_all("act", act)
            act_concat(act, 1)
            act_stage(act, S_IN[1] + 1)
            ffn(1, groups1, 3, 5)
            act_rstd(act, 4)

        @block.gpsimd
        def _(pool):
            chain = Chain(pool, sm["pool_chain"])

            def squares(norm):
                return lambda j, slot: pool_sq(pool, norm, 2 * j + slot)

            pool_sq_start(pool, 0)
            pool_lo(pool, 0, 0, KT)
            pool_lo(pool, 1, 1, KT)
            for i in range(POOL_SQ):
                pool_sq(pool, 0, i, 1 if i < POOL_SQ - 1 else 1 + KT - POOL_SQ)
            pool.wait_ge(sm["consts_loaded"], N_CONST)
            pool_stage(pool, 0)
            sync_all("pool", pool)
            rwkv_pool(pool, chain)
            sync_all("pool", pool)
            att_pool(pool, cfg_a, chain)
            sync_all("pool", pool)
            pool_sq_start(pool, 1)
            pool_stage(pool, 1, squares(1))
            for n, (sg, sd, k0, kn) in enumerate(groups0):
                pool_hidden(pool, sg, 0, k0, kn)
                last = n == len(groups0) - 1
                if last:
                    pool_sq_start(pool, 2)
                pool_stage(pool, sd, squares(2) if last else None)
            pool_stage(pool, S_IN[1])
            sync_all("pool", pool)
            att_pool(pool, cfg_c, chain)
            sync_all("pool", pool)
            ln_pool(pool)
            sync_all("pool", pool)
            pool_sq_start(pool, 3)
            pool_stage(pool, S_IN[1] + 1, squares(3))
            for n, (sg, sd, k0, kn) in enumerate(groups1):
                pool_hidden(pool, sg, 1, k0, kn)
                last = n == len(groups1) - 1
                if last:
                    pool_sq_start(pool, 4)
                pool_stage(pool, sd, squares(4) if last else None)

        @block.vector
        def _(dve):
            chain = Chain(dve, sm["dve_chain"])
            dve.wait_ge(sm["gains_loaded"], 16)
            dve_h(dve, 0, 0, by_group, 0)
            dve_first_squares(dve, chain)
            dve.wait_ge(sm["consts_loaded"], N_CONST)
            for n, (which, c0, cn) in enumerate(((0, 0, VEC_A), (1, 0, 512), (1, 512, VEC_C - 512))):
                dve.wait_ge(sm["vec_done"], n + 1)
                if n == 0:
                    chain(dve.memset(vec_sb[0:8, 0, :], 0.0))
                dve.tensor_copy(vec_sb[0:8, which, c0:c0 + cn], PS[0:8, 7, 0:cn]).then_inc(sm["vec_copied"], 1)
            dve_in_even(dve, chain)
            dve.wait_ge(sm["evac_done"], bases[1] * NG)
            sync_all("dve", dve)
            rwkv_dve(dve, chain)
            sync_all("dve", dve)
            att_dve(dve, cfg_a, chain)
            sync_all("dve", dve)
            dve_concat(dve, 0, KT * NG)
            for g in range(NG):
                dve.wait_ge(x_loaded[g], 32)
            dve_residual(dve, 1)

            def ffn(layer, groups, norm, h):
                dve_h(dve, norm, h, by_group, h * KT * NG)
                dve_rstd(dve, norm)
                dve_first_rstd(dve, norm)
                for n, (sg, sd, k0, kn) in enumerate(groups):
                    dve_hidden(dve, sg, layer, k0, kn)
                    last = n == len(groups) - 1 and layer == 0
                    dve_residual(dve, sd, (lambda i: dve_h(dve, 2, 3, [(i, g) for g in range(NG)],
                                                           i * NG + 3 * KT * NG)) if last else None)

            ffn(0, groups0, 1, 2)
            dve_in_odd(dve)
            dve.wait_ge(sm["evac_done"], bases[S_IN[1] + 1] * NG)
            sync_all("dve", dve)
            dve.memset(u_buf[:, :, 0:TAPS - 1], 0.0).then_inc(sm["z_ready"], 1)
            dve.wait_ge(sm["z_ready"], 1)
            dve.wait_ge(sm["cstate_loaded"], 16)
            att_dve(dve, cfg_c, chain, conv_taps(chain, dve))
            sync_all("dve", dve)
            ln_dve(dve, chain)
            sync_all("dve", dve)
            dve_concat(dve, 1, 4 * KT * NG)
            for g in range(NG):
                dve.wait_ge(x_loaded[g], 48)
            dve_residual(dve, S_IN[1] + 1)
            ffn(1, groups1, 3, 5)
            dve_rstd(dve, 4)
            for g, (c0, cn) in enumerate(GROUPS):
                dve.wait_ge(sm["rstd_ready"], 4 * NG + g + 1)
                for i in range(KT):
                    dve.scalar_tensor_tensor(x[:, i, c0:c0 + cn], x[:, i, c0:c0 + cn], gains[:, 4, i:i + 1],
                                             rstd[:, c0:c0 + cn], ALU.mult, ALU.mult).then_inc(sm["y_ready"], 1)


def weight_tiles(w):
    k, m = w.shape
    return w.reshape(k // P, P, m // P, P).transpose(2, 1, 0, 3)


def feature_major(t):
    return t.T.reshape(t.shape[1] // P, P, t.shape[0]).transpose(1, 0, 2)


def shape_constants():
    i = np.arange(P)
    s, t = i[:, None], i[None, :]
    same = s // CHUNK == t // CHUNK
    before, upto = same & (s < t), same & (s <= t)
    c = {"ident": np.eye(P), "flip": np.eye(P)[::-1], "ones": np.ones((P, P)), "head_ones": s // HD == t // HD,
         "sa_mask": np.stack([before, upto, before, upto], 1)}

    def off_diagonal(b):
        return (s // (2 * b) == t // (2 * b)) & (s // b % 2 == 0) & (t // b % 2 == 1)
    c["level_mask"] = np.stack([off_diagonal(2 ** l) for l in range(1, LEVELS)], 1)
    c["x0_mask"] = np.stack([off_diagonal(1).T, off_diagonal(1)], 1)
    rel = np.arange(VEC_A) - 255
    nb = 16
    exact = nb // 2
    n = np.abs(rel)
    nf = np.maximum(n, exact).astype(np.float32)
    large = exact + (np.log(nf / exact) / np.log(128 / exact) * (nb - exact)).astype(np.int32)
    bucket = np.where(rel > 0, nb, 0) + np.where(n < exact, n, np.minimum(large, nb - 1))
    c["pick_a"] = i[:, None] == bucket[None, :]
    dist = np.clip(639 - np.arange(VEC_C), -128, 128) + 128
    c["pick_c"] = (np.arange(3 * P)[:, None] == dist[None, :]).reshape(3, P, VEC_C).transpose(1, 0, 2)
    return {k: np.ascontiguousarray(v, dtype=np.float32) for k, v in c.items()}


def rwkv_columns():
    r, wd, k, v, ad, gd = np.split(np.arange(1792), np.cumsum([512, 64, 512, 512, 64]))
    return np.concatenate([k, v, r, wd, ad, gd])


HEAD_ORDER = [0, 4, 1, 5, 2, 6, 3, 7]


def lay_out(a):
    f = {}
    cols = rwkv_columns()
    heads = np.concatenate([np.arange(h * HD, (h + 1) * HD) for h in HEAD_ORDER])
    f["x"] = feature_major(np.concatenate([a["x_prompt"][0], a["x_sample"][0]], 0))
    f["w_e"] = weight_tiles(a["w_in_e"][0][:, np.concatenate([768 + cols, np.arange(512, 768), heads])])
    f["w_oe"] = weight_tiles(a["w_out_e"][0][np.concatenate([heads, np.arange(512, 1024)])])
    i = np.arange(P)
    pairs = np.concatenate([np.concatenate([2048 + j * P + i, 1536 + j * P + i]) for j in range(4)])
    f["w_o"] = weight_tiles(a["w_in_o"][0][:, np.concatenate([np.arange(512, 1536), np.arange(512), pairs])])
    f["w_oo"] = weight_tiles(a["w_out_o"][0])
    for n in range(2):
        gu = np.stack([weight_tiles(a["ffn_w_gate"][n]), weight_tiles(a["ffn_w_up"][n])], 1)
        f[f"w_gu{n}"] = gu.reshape((2 * FT,) + gu.shape[2:])
        f[f"w_d{n}"] = weight_tiles(a["ffn_w_down"][n])
    g = [a["norm_mix_g"][0], a["norm_ffn_g"][0], a["norm_mix_g"][1], a["norm_ffn_g"][1], a["norm_final_g"]]
    f["gains"] = np.stack([v.reshape(KT, P).T for v in g], 1)
    f["mu"] = a["b_mu"][0][cols].reshape(NPB, P).T
    f["shift_in"] = a["state_b_shift"][0, 0][cols].reshape(NPB, P).T
    par = [a["b_w0"][0], a["b_a0"][0], a["b_kk"][0], a["b_ka"][0], a["b_rk"][0].reshape(-1), a["b_lnx_w"][0],
           a["b_lnx_b"][0]]
    par += [np.zeros_like(par[0])] * 2
    f["rw_par"] = np.stack([v.reshape(PAIRS, P).T for v in par], 2)
    par = list(a["d_dw_w"][0]) + [a["d_dw_b"][0], a["d_ln_g"][0], a["d_ln_b"][0]]
    f["conv_par"] = np.stack([v.reshape(4, P).T for v in par], 2)
    f["sink"] = np.broadcast_to(a["a_sink"][0][HEAD_ORDER], (P, 8))
    table = np.zeros((P, 8), np.float32)
    table[:32] = a["t5_table"][:, HEAD_ORDER]
    f["table_a"] = table
    table = np.zeros((3 * P, 8), np.float32)
    table[:257] = a["c_rel_table"][0].T
    f["table_c"] = table.reshape(3, P, 8).transpose(1, 0, 2)
    f["wa2"] = np.concatenate([a["b_w2"][0], a["b_a2"][0]], 0)
    f["g2"] = a["b_g2"][0]
    f["state_in"] = a["state_b_wkv"][0, 0].reshape(PAIRS, 2, HD, HD).transpose(1, 3, 0, 2).reshape(P, PAIRS, HD)
    f["a_kc"] = feature_major(a["cache_a_k"][0, 0].reshape(P, P))
    f["a_vc"] = a["cache_a_v"][0, 0].reshape(P, 1, P)
    f["c_kc"] = feature_major(a["cache_c_k"][0, 0].reshape(C_CACHE, 512))
    f["c_vc"] = a["cache_c_v"][0, 0].reshape(2, P, 512).transpose(1, 0, 2)
    f["conv_in"] = feature_major(a["state_d_conv"][0, 0])
    f.update(shape_constants())
    return f


OUTPUTS = {"out_y": (P, KT, NT), "out_akv": (P, 2, 192), "out_state": (P, 2, PAIRS, HD), "out_shift": (P, 2, NPB),
           "out_ckv": (P, 8, 576), "out_conv": (P, 4, 2, TAPS - 1)}


def kernel(**inputs):
    import concourse.bacc as bacc
    from concourse.bass_utils import run_bass_kernel_spmd

    nc = bacc.Bacc("TRN2", target_bir_lowering=False, num_devices=1)
    arrays, d = {}, {}
    for name, v in lay_out({k: np.asarray(v) for k, v in inputs.items()}).items():
        arrays[f"in_{name}"] = np.ascontiguousarray(v)
        d[name] = nc.dram_tensor(f"in_{name}", v.shape, F32, kind="ExternalInput").ap()
    for name, shape in OUTPUTS.items():
        d[name] = nc.dram_tensor(name, shape, F32, kind="ExternalOutput").ap()
    trunk(nc, d)
    r = run_bass_kernel_spmd(nc, [arrays], core_ids=[0]).results[0]

    def token_major(t):
        return t.transpose(2, 1, 0).reshape(t.shape[2], -1)

    y = token_major(r["out_y"])
    akv = [r["out_akv"][:, i].T.reshape(192, 2, HD) for i in range(2)]
    ckv = [token_major(r["out_ckv"][:, 4 * i:4 * i + 4]).reshape(576, 8, HD) for i in range(2)]
    wkv = r["out_state"].reshape(2, HD, 2, PAIRS, HD).transpose(2, 3, 0, 4, 1).reshape(2, 8, HD, HD)
    back = np.argsort(rwkv_columns())
    shift = [r["out_shift"][:, i].T.reshape(-1)[back] for i in range(2)]
    conv = [token_major(r["out_conv"][:, :, i]) for i in range(2)]
    return (y[None, :SEQ], y[None, SEQ:],
            akv[0][None, None, :P], akv[1][None, None, :P], wkv[0][None, None], shift[0][None, None],
            ckv[0][None, None, :512], ckv[1][None, None, :512], conv[0][None, None],
            akv[0][None, None, P:], akv[1][None, None, P:], wkv[1][None, None], shift[1][None, None],
            ckv[0][None, None, 512:], ckv[1][None, None, 512:], conv[1][None, None])
```
